# Optimizing a Trainium2 kernel written in Bass

```python
import math
import jax
import jax.numpy as jnp
from jax import lax
import numpy as np

D_MODEL = 1024
BATCH = 1
SEQ = 256
DEPTH = 2

PLE_DIM = 256
EPS = 1e-6

N_ATTN_HEADS = 8
N_BUCKETS = 32
MAX_DISTANCE = 128

SC_WIDTH = D_MODEL // 2
CONV_WIDTH = 3
SWA_HEADS = N_ATTN_HEADS
SWA_KV_HEADS = 2
SWA_HEAD_DIM = (D_MODEL // 2) // SWA_HEADS
SWA_WINDOW = 128
SWA_BLOCK = 128
SWA_Q_WIDTH = SWA_HEADS * SWA_HEAD_DIM
SWA_KV_WIDTH = SWA_KV_HEADS * SWA_HEAD_DIM
D_IN_EVEN = 3 * SC_WIDTH + SWA_Q_WIDTH + 2 * SWA_KV_WIDTH

MOBA_HEADS = N_ATTN_HEADS
MOBA_HEAD_DIM = D_MODEL // MOBA_HEADS
MOBA_BLOCK = 256
MOBA_TOPK = 3
MOBA_Q_CHUNK = 32

D_FF = ((8 * D_MODEL // 3 + 127) // 128) * 128
N_EXPERTS = 8
TOP_K = 2
D_FF_EXPERT = 7 * D_MODEL // 2

N_EVEN = (DEPTH + 1) // 2
N_ODD = DEPTH // 2

kernel_name = "hybrid_conv_swa_moba_moe_trunk"

def rms_norm(x, g):
    xf = x.astype(jnp.float32)
    y = xf * lax.rsqrt(jnp.mean(xf * xf, axis=-1, keepdims=True) + EPS)
    return (y * g.astype(jnp.float32)).astype(x.dtype)

def t5_bucket(dist):
    d = jnp.maximum(dist, 0).astype(jnp.int32)
    max_exact = N_BUCKETS // 2
    scaled = jnp.log(jnp.maximum(d, max_exact).astype(jnp.float32) / max_exact) / math.log(MAX_DISTANCE / max_exact)
    large = jnp.minimum(max_exact + (scaled * (N_BUCKETS - max_exact)).astype(jnp.int32), N_BUCKETS - 1)
    return jnp.where(d < max_exact, d, large)

def short_conv_mixer(b_gate, c_gate, u, conv_w):
    cu = c_gate * u
    y = lax.conv_general_dilated(
        cu, conv_w[:, None, :].astype(cu.dtype), window_strides=(1,),
        padding=[(CONV_WIDTH - 1, 0)], dimension_numbers=("NWC", "WIO", "NWC"),
        feature_group_count=cu.shape[-1])
    return b_gate * y

def sliding_window_attention(q, k, v, sinks, rel_bias):
    bsz, seq, n_h, hd = q.shape
    n_kv = k.shape[2]
    grp = n_h // n_kv
    nb = seq // SWA_BLOCK
    blk = SWA_BLOCK
    qb = q.reshape(bsz, nb, blk, n_kv, grp, hd)

    def band(t):
        tb = t.reshape(bsz, nb, blk, n_kv, hd)
        prev = jnp.concatenate([jnp.zeros_like(tb[:, :1]), tb[:, :-1]], axis=1)
        return jnp.concatenate([prev, tb], axis=2)

    kw, vw = band(k), band(v)
    logits = jnp.einsum("bnqkgd,bnjkd->bnkgqj", qb, kw,
                        preferred_element_type=jnp.float32) * (hd ** -0.5)
    qi = jnp.arange(blk)[:, None]
    kj = jnp.arange(2 * blk)[None, :]
    diff = qi - kj + blk
    kpos = jnp.arange(nb)[:, None, None] * blk - blk + kj[None]
    valid = (diff >= 0)[None] & (diff < SWA_WINDOW)[None] & (kpos >= 0)
    bias = rel_bias[t5_bucket(diff)].astype(jnp.float32)
    bias = bias.transpose(2, 0, 1).reshape(n_kv, grp, blk, 2 * blk)
    logits = jnp.where(valid[None, :, None, None], logits + bias, -jnp.inf)
    sink = jnp.broadcast_to(sinks.astype(jnp.float32).reshape(1, 1, n_kv, grp, 1, 1),
                            logits.shape[:-1] + (1,))
    probs = jax.nn.softmax(jnp.concatenate([logits, sink], axis=-1), axis=-1)[..., :-1]
    out = jnp.einsum("bnkgqj,bnjkd->bnqkgd", probs.astype(v.dtype), vw)
    return out.reshape(bsz, seq, n_h * hd)

def moba_attention(q, k, v, rel_bias):
    bsz, seq, n_h, hd = q.shape
    bs = MOBA_BLOCK
    s_pad = ((seq + bs - 1) // bs) * bs
    pad = [(0, 0), (0, s_pad - seq), (0, 0), (0, 0)]
    q, k, v = jnp.pad(q, pad), jnp.pad(k, pad), jnp.pad(v, pad)
    nblk = s_pad // bs
    topk = min(MOBA_TOPK, nblk)
    scale = hd ** -0.5

    kb = k.reshape(bsz, nblk, bs, n_h, hd)
    kmean = jnp.mean(kb.astype(jnp.float32), axis=2)
    gate = jnp.einsum("bshd,bnhd->bhsn", q.astype(jnp.float32), kmean)
    qblk = jnp.arange(s_pad) // bs
    past = jnp.arange(nblk)[None, :] < qblk[:, None]
    gate = jnp.where(past[None, None], gate, -jnp.inf)
    _, sel = lax.top_k(gate, topk)
    sel_valid = sel < qblk[None, None, :, None]

    kbh = kb.transpose(0, 3, 1, 2, 4)
    vbh = v.reshape(bsz, nblk, bs, n_h, hd).transpose(0, 3, 1, 2, 4)
    bi = jnp.arange(bsz)[:, None, None, None]
    hi = jnp.arange(n_h)[None, :, None, None]
    hi5 = jnp.arange(n_h)[None, :, None, None, None]
    qc_len = MOBA_Q_CHUNK
    n_chunks = s_pad // qc_len

    def chunk(c):
        start = c * qc_len
        qc = lax.dynamic_slice_in_dim(q, start, qc_len, axis=1)
        selc = lax.dynamic_slice_in_dim(sel, start, qc_len, axis=2)
        validc = lax.dynamic_slice_in_dim(sel_valid, start, qc_len, axis=2)
        kg = kbh[bi, hi, selc]
        vg = vbh[bi, hi, selc]
        qpos = start + jnp.arange(qc_len)
        kpos_sel = selc[..., None] * bs + jnp.arange(bs)
        d_sel = qpos[None, None, :, None, None] - kpos_sel
        l_sel = jnp.einsum("bqhd,bhqtjd->bhqtj", qc, kg,
                           preferred_element_type=jnp.float32) * scale
        l_sel = l_sel + rel_bias[t5_bucket(d_sel), hi5].astype(jnp.float32)
        l_sel = jnp.where(validc[..., None], l_sel, -jnp.inf)
        l_sel = l_sel.reshape(bsz, n_h, qc_len, topk * bs)
        own = start // bs
        ko = lax.dynamic_slice_in_dim(k, own * bs, bs, axis=1)
        vo = lax.dynamic_slice_in_dim(v, own * bs, bs, axis=1)
        d_own = qpos[:, None] - (own * bs + jnp.arange(bs))[None, :]
        l_own = jnp.einsum("bqhd,bjhd->bhqj", qc, ko,
                           preferred_element_type=jnp.float32) * scale
        l_own = l_own + rel_bias[t5_bucket(d_own)].astype(jnp.float32).transpose(2, 0, 1)[None]
        l_own = jnp.where((d_own >= 0)[None, None], l_own, -jnp.inf)
        probs = jax.nn.softmax(jnp.concatenate([l_sel, l_own], axis=-1), axis=-1).astype(v.dtype)
        p_sel, p_own = probs[..., : topk * bs], probs[..., topk * bs:]
        out = jnp.einsum("bhqj,bhqjd->bqhd", p_sel, vg.reshape(bsz, n_h, qc_len, topk * bs, hd))
        return out + jnp.einsum("bhqj,bjhd->bqhd", p_own, vo)

    outs = lax.map(chunk, jnp.arange(n_chunks))
    out = outs.transpose(1, 0, 2, 3, 4).reshape(bsz, s_pad, n_h * hd)
    return out[:, :seq]

def swiglu(x, w_gate, w_up, w_down):
    return (jax.nn.silu(x @ w_gate) * (x @ w_up)) @ w_down

def moe_swiglu(x, w_router, w_gate, w_up, w_down):
    logits = (x @ w_router).astype(jnp.float32)
    top_vals, top_idx = lax.top_k(logits, TOP_K)
    top_w = jax.nn.softmax(top_vals, axis=-1)
    gates = jnp.sum(jax.nn.one_hot(top_idx, N_EXPERTS, dtype=jnp.float32) * top_w[..., None], axis=-2)
    out = jnp.zeros_like(x)
    for e in range(N_EXPERTS):
        out = out + gates[..., e:e + 1].astype(x.dtype) * swiglu(x, w_gate[e], w_up[e], w_down[e])
    return out

def per_layer_embedding(h, p_i, g, w_gate, w_proj):
    return h + jax.nn.sigmoid(rms_norm(h, g) @ w_gate) * (p_i @ w_proj)

def setup_inputs(seed: int = 0) -> dict:
    key = jax.random.key(seed)
    ks = iter(jax.random.split(key, 40))
    f32 = jnp.float32

    def dense(shape, fan_in):
        return jax.random.normal(next(ks), shape, f32) * (fan_in ** -0.5)

    def gain(shape):
        return 1.0 + 0.05 * jax.random.normal(next(ks), shape, f32)

    return {
        "x": jax.random.normal(next(ks), (BATCH, SEQ, D_MODEL), f32),
        "p": jax.random.normal(next(ks), (DEPTH, BATCH, SEQ, PLE_DIM), f32),
        "rel_bias": 0.5 * jax.random.normal(next(ks), (N_BUCKETS, N_ATTN_HEADS), f32),
        "final_norm": gain((D_MODEL,)),
        "e_norm_mix": gain((N_EVEN, D_MODEL)),
        "e_w_in": dense((N_EVEN, D_MODEL, D_IN_EVEN), D_MODEL),
        "e_conv_w": dense((N_EVEN, CONV_WIDTH, SC_WIDTH), CONV_WIDTH),
        "e_sinks": 0.5 * jax.random.normal(next(ks), (N_EVEN, SWA_HEADS), f32),
        "e_w_out": dense((N_EVEN, SC_WIDTH + SWA_Q_WIDTH, D_MODEL), SC_WIDTH + SWA_Q_WIDTH),
        "e_norm_ffn": gain((N_EVEN, D_MODEL)),
        "e_ffn_gate": dense((N_EVEN, D_MODEL, D_FF), D_MODEL),
        "e_ffn_up": dense((N_EVEN, D_MODEL, D_FF), D_MODEL),
        "e_ffn_down": dense((N_EVEN, D_FF, D_MODEL), D_FF),
        "e_norm_ple": gain((N_EVEN, D_MODEL)),
        "e_ple_gate": dense((N_EVEN, D_MODEL, D_MODEL), D_MODEL),
        "e_ple_proj": dense((N_EVEN, PLE_DIM, D_MODEL), PLE_DIM),
        "o_norm_mix": gain((N_ODD, D_MODEL)),
        "o_w_qkv": dense((N_ODD, D_MODEL, 3 * D_MODEL), D_MODEL),
        "o_w_o": dense((N_ODD, D_MODEL, D_MODEL), D_MODEL),
        "o_norm_ffn": gain((N_ODD, D_MODEL)),
        "o_router": dense((N_ODD, D_MODEL, N_EXPERTS), D_MODEL),
        "o_exp_gate": dense((N_ODD, N_EXPERTS, D_MODEL, D_FF_EXPERT), D_MODEL),
        "o_exp_up": dense((N_ODD, N_EXPERTS, D_MODEL, D_FF_EXPERT), D_MODEL),
        "o_exp_down": dense((N_ODD, N_EXPERTS, D_FF_EXPERT, D_MODEL), D_FF_EXPERT),
        "o_norm_ple": gain((N_ODD, D_MODEL)),
        "o_ple_gate": dense((N_ODD, D_MODEL, D_MODEL), D_MODEL),
        "o_ple_proj": dense((N_ODD, PLE_DIM, D_MODEL), PLE_DIM),
    }

def reference(x, p, rel_bias, final_norm,
              e_norm_mix, e_w_in, e_conv_w, e_sinks, e_w_out,
              e_norm_ffn, e_ffn_gate, e_ffn_up, e_ffn_down,
              e_norm_ple, e_ple_gate, e_ple_proj,
              o_norm_mix, o_w_qkv, o_w_o, o_norm_ffn, o_router,
              o_exp_gate, o_exp_up, o_exp_down,
              o_norm_ple, o_ple_gate, o_ple_proj):
    bsz, seq, _ = x.shape
    splits_even = [SC_WIDTH, 2 * SC_WIDTH, 3 * SC_WIDTH, 3 * SC_WIDTH + SWA_Q_WIDTH,
                   3 * SC_WIDTH + SWA_Q_WIDTH + SWA_KV_WIDTH]
    h = x
    for i in range(DEPTH):
        j = i // 2
        if i % 2 == 0:
            z = rms_norm(h, e_norm_mix[j]) @ e_w_in[j]
            b_gate, c_gate, u, q, k, v = jnp.split(z, splits_even, axis=-1)
            a_out = short_conv_mixer(b_gate, c_gate, u, e_conv_w[j])
            b_out = sliding_window_attention(
                q.reshape(bsz, seq, SWA_HEADS, SWA_HEAD_DIM),
                k.reshape(bsz, seq, SWA_KV_HEADS, SWA_HEAD_DIM),
                v.reshape(bsz, seq, SWA_KV_HEADS, SWA_HEAD_DIM),
                e_sinks[j], rel_bias)
            h = h + jnp.concatenate([a_out, b_out], axis=-1) @ e_w_out[j]
            h = h + swiglu(rms_norm(h, e_norm_ffn[j]), e_ffn_gate[j], e_ffn_up[j], e_ffn_down[j])
            h = per_layer_embedding(h, p[i], e_norm_ple[j], e_ple_gate[j], e_ple_proj[j])
        else:
            qkv = rms_norm(h, o_norm_mix[j]) @ o_w_qkv[j]
            q, k, v = jnp.split(qkv, 3, axis=-1)
            shp = (bsz, seq, MOBA_HEADS, MOBA_HEAD_DIM)
            c_out = moba_attention(q.reshape(shp), k.reshape(shp), v.reshape(shp), rel_bias)
            h = h + c_out @ o_w_o[j]
            h = h + moe_swiglu(rms_norm(h, o_norm_ffn[j]), o_router[j],
                               o_exp_gate[j], o_exp_up[j], o_exp_down[j])
            h = per_layer_embedding(h, p[i], o_norm_ple[j], o_ple_gate[j], o_ple_proj[j])
    return rms_norm(h, final_norm)


_drawn_inputs = setup_inputs


def setup_inputs(seed=0):
    import zlib

    import numpy as np

    out = dict(_drawn_inputs(seed))
    spreads = {}
    factors = {'e_sinks': 4.742, 'o_norm_ple': 66.872, 'e_norm_ple': 3.262, 'o_norm_mix': 2.96}
    for name, (base, spread) in spreads.items():
        noise = np.random.default_rng([zlib.crc32(name.encode()), seed]).standard_normal(out[name].shape)
        drawn = base * np.exp(spread * noise) if base else spread * noise
        out[name] = jnp.asarray(drawn.astype(out[name].dtype))
    for name, factor in factors.items():
        out[name] = (out[name] * factor).astype(out[name].dtype)
    return out
```

```python
from contextlib import ExitStack

import numpy as np

import concourse.bass as bass
from concourse import mybir

F32 = mybir.dt.float32
F32R = mybir.dt.float32r
I32 = mybir.dt.int32
ALU = mybir.AluOpType
ACT = mybir.ActivationFunctionType
AX = mybir.AxisListType.X

P = 128
SEQ, D, HEADS, BUCKETS, PLE = 256, 1024, 8, 32, 256
TT = SEQ // P
KC = D // P
EPS = 1e-6
HALF = 512
MASKED = -1e30
DIAGS = 3 * P

SC = D // 2
SWA_D, SWA_KV, SWA_WINDOW = 64, 2, 128
MOBA_D = D // HEADS
D_FF = 2816
PAIRS = D_FF // (2 * P)
EXPERTS, TOP_K, D_FFE = 8, 2, 3584
BLOCKS = D_FFE // HALF
EXTRA = 3
JOBS = EXPERTS + EXTRA

TILE = 2048
RAW, SPLIT = 6, 3
Q0_T, KV_T, CONV_T = 0, 2, 3
OUT0_T = 9
FFN_T = 13
PLE0_T = FFN_T + 3 * PAIRS
QK_T = PLE0_T + 5
V_T = QK_T + 8
OUT1_T = V_T + 4
MOE_T = OUT1_T + 4
JOB_TILES = 6 * BLOCKS
PLE1_T = MOE_T
END_T = PLE1_T + 5
assert JOB_TILES % RAW == 0 and RAW % SPLIT == 0

C_IDENT, C_TRI, C_IOTA, C_ONES = 0, P, 2 * P, 3 * P
C_BEFORE = 4 * P
C_EIDX = C_BEFORE + EXPERTS * EXPERTS
C_END = C_EIDX + EXPERTS


def shape_constants():
    c = np.zeros((P, C_END), np.float32)
    c[:, C_IDENT:C_IDENT + P] = np.eye(P)
    c[:, C_TRI:C_TRI + P] = np.arange(P)[:, None] < np.arange(P)[None]
    c[:, C_IOTA:C_IOTA + P] = np.arange(P)
    c[:, C_ONES:C_ONES + P] = 1.0
    e = np.arange(EXPERTS)
    c[:, C_BEFORE:C_EIDX] = (e[None] < e[:, None]).reshape(-1)
    c[:, C_EIDX:C_END] = e
    dist = 2 * P - 1 - np.arange(DIAGS)
    exact = BUCKETS // 2
    far = exact + (np.log(np.maximum(dist, exact) / exact) / np.log(P / exact) * (BUCKETS - exact)).astype(int)
    bucket = np.where(dist < exact, dist, np.minimum(far, BUCKETS - 1))
    oh = np.zeros((BUCKETS + 1, 2, DIAGS), np.float32)
    for layer, reach in ((0, SWA_WINDOW), (1, SEQ)):
        valid = (dist >= 0) & (dist < reach)
        m = np.flatnonzero(valid)
        oh[bucket[m], layer, m] = 1.0
        oh[BUCKETS, layer] = np.where(valid, 0.0, MASKED)
    return c, oh.reshape(BUCKETS + 1, 2 * DIAGS)


def trunk(nc, x, p, rel_bias, final_norm, e_norm_mix, e_w_in, e_conv_w, e_sinks, e_w_out,
          e_norm_ffn, e_ffn_gate, e_ffn_up, e_ffn_down, e_norm_ple, e_ple_gate, e_ple_proj,
          o_norm_mix, o_w_qkv, o_w_o, o_norm_ffn, o_router, o_exp_gate, o_exp_up, o_exp_down,
          o_norm_ple, o_ple_gate, o_ple_proj, consts, onehots, out):
    gains = [e_norm_mix[0:1], e_norm_ffn[0:1], e_norm_ple[0:1], o_norm_mix[0:1], o_norm_ffn[0:1],
             o_norm_ple[0:1], final_norm.rearrange("(a d) -> a d", a=1)]
    diag_dram = nc.dram_tensor("diag_scratch", (2, HEADS, P, DIAGS), F32, kind="Internal").ap()

    with ExitStack() as ctx:
        def sb(name, shape, dt=F32):
            return ctx.enter_context(nc.sbuf_tensor(name, shape, dt))

        def sem(name):
            return ctx.enter_context(nc.semaphore(name))

        raw = sb("raw", [P, RAW, TILE])
        w_hi = sb("w_hi", [P, SPLIT, TILE], F32R)
        w_lo = sb("w_lo", [P, SPLIT, TILE], F32R)
        h = sb("h", [P, TT, D])
        xn = sb("xn", [P, TT, D])
        x_hi = sb("x_hi", [P, KC, SEQ], F32R)
        x_lo = sb("x_lo", [P, KC, SEQ], F32R)
        m_hi = sb("m_hi", [P, KC, SEQ], F32R)
        m_lo = sb("m_lo", [P, KC, SEQ], F32R)
        p_hi = sb("p_hi", [P, 2, 2, SEQ], F32R)
        p_lo = sb("p_lo", [P, 2, 2, SEQ], F32R)
        r_raw = sb("r_raw", [P, KC, EXPERTS])
        r_hi = sb("r_hi", [P, KC, EXPERTS], F32R)
        r_lo = sb("r_lo", [P, KC, EXPERTS], F32R)
        zeros_r = sb("zeros_r", [P, P], F32R)
        gain = sb("gain", [P, 2, D])
        cst = sb("cst", [P, C_END])
        rel = sb("rel", [BUCKETS + 1, HEADS])
        bias = sb("bias", [P, HEADS, DIAGS])
        sink = sb("sink", [P, HEADS])
        conv_w = sb("conv_w", [P, 3 * SC // P])
        ssq = sb("ssq", [P, 4, TT])
        rstd = sb("rstd", [P, TT])
        score = sb("score", [P, 2, DIAGS])
        probT = sb("probT", [P, DIAGS])
        stat = sb("stat", [P, 2, 5, TT])
        diag = score[0:HEADS].rearrange("p b n -> p (b n)")
        work = sb("work", [P, 6 * D])
        oh = work[0:BUCKETS + 1, 4224:4992]
        taps = work[0:3 * SC // P, 4992:5120]
        p_raw = work[:, 5 * D:6 * D].rearrange("p (l t n) -> p l t n", l=2, t=TT)
        q0T = work[:, 0:D].rearrange("p (j t) -> p j t", j=4)
        k0T = work[:, D:D + SEQ]
        v0 = work[:, D + SEQ:D + 2 * SEQ].rearrange("p (t n) -> p t n", t=TT)
        c_sb = work[:, 1536:2048].rearrange("p (j t) -> p j t", j=2)
        cu = work[:, 2048:2048 + 4 * (SEQ + 2)].rearrange("p (j t) -> p j t", j=4)
        conv_y = work[:, 3200:3712].rearrange("p (j t) -> p j t", j=2)
        conv_a = work[:, 3712:4224].rearrange("p (j t) -> p j t", j=2)
        q1T = work[:, 0:2 * D].rearrange("p (j t) -> p j t", j=HEADS)
        k1T = work[:, 2 * D:4 * D].rearrange("p (j t) -> p j t", j=HEADS)
        v1 = work[:, 4 * D:6 * D].rearrange("p (t n) -> p t n", t=TT)
        silu = work[:, 0:HALF]
        hid = work[:, HALF:2 * HALF]
        sig = work[:, 2 * D:4 * D].rearrange("p (b n) -> p b n", b=4)
        gated = work[:, 4 * D:4 * D + HALF]
        y_sb = work[:, 2 * D:3 * D]
        pick = work[:, 3 * D:3 * D + 2 * P].rearrange("p (t s) -> p t s", t=TT)
        pick_g = work[:, 3 * D + 2 * P:3 * D + 4 * P].rearrange("p (t s) -> p t s", t=TT)
        place = work[:, 3 * D + 4 * P:3 * D + 6 * P]
        route = work[:, 4 * D:5 * D]
        hid_hi, hid_lo = m_hi[:, 0:2], m_lo[:, 0:2]
        hidT_hi = m_hi[:, 0:2].rearrange("p a (b s) -> p (a b) s", b=2)
        hidT_lo = m_lo[:, 0:2].rearrange("p a (b s) -> p (a b) s", b=2)
        jobs = sb("jobs", [P, JOBS + 1, 2, TT])
        job = sb("job", [P, 1, 2, TT])
        job_int = sb("job_int", [1, 4], I32)
        ident = cst[:, C_IDENT:C_IDENT + P]
        iota = cst[:, C_IOTA:C_IOTA + P]
        bank = [ctx.enter_context(nc.psum_tensor(f"bank{i}", [P, HALF], F32)) for i in range(8)]

        tile_loaded = [sem(f"tile_loaded{i}") for i in range(RAW)]
        hi_made, lo_made, tile_used = sem("hi_made"), sem("lo_made"), sem("tile_used")
        x_loaded, cst_loaded, aux_loaded = sem("x_loaded"), sem("cst_loaded"), sem("aux_loaded")
        gain_loaded = [sem("gain_loaded0"), sem("gain_loaded1")]
        diag_ready, diag_copied, diag_stored = sem("diag_ready"), sem("diag_copied"), sem("diag_stored")
        bias_loaded = [sem("bias_loaded0"), sem("bias_loaded1")]
        pT_ready, p_hi_made, p_lo_made = sem("pT_ready"), sem("p_hi_made"), sem("p_lo_made")
        r_hi_made, r_lo_made = sem("r_hi_made"), sem("r_lo_made")
        memsets_done = sem("memsets_done")
        h_ready, squares_made, xn_ready = sem("h_ready"), sem("squares_made"), sem("xn_ready")
        xT_ready, x_hi_made, x_lo_made = sem("xT_ready"), sem("x_hi_made"), sem("x_lo_made")
        vec_step = sem("vec_step")
        q0_made, kv0_made, c_made, b_made = sem("q0_made"), sem("kv0_made"), sem("c_made"), sem("b_made")
        conv_hi_made, conv_lo_made, conv_made = sem("conv_hi_made"), sem("conv_lo_made"), sem("conv_made")
        qkv1_made = sem("qkv1_made")
        scores_ready, negmax_ready, exp_made = sem("scores_ready"), sem("negmax_ready"), sem("exp_made")
        probs_ready, probT_ready, probT_made = sem("probs_ready"), sem("probT_ready"), sem("probT_made")
        oT_ready, oT_hi_made, oT_lo_made = sem("oT_ready"), sem("oT_hi_made"), sem("oT_lo_made")
        silu_made, hid_made = sem("silu_made"), sem("hid_made")
        hid_hi_made, hid_lo_made = sem("hid_hi_made"), sem("hid_lo_made")
        sig_made = sem("sig_made")
        logits_ready, route_exp_ready, route_exp_made = sem("logits_ready"), sem("route_exp_ready"), sem("route_exp_made")
        chosen_ready, ranks_ready, jobs_ready = sem("chosen_ready"), sem("ranks_ready"), sem("jobs_ready")
        pick_made, gather_ready, xg_hi_made, xg_lo_made = sem("pick_made"), sem("gather_ready"), sem("xg_hi_made"), sem("xg_lo_made")
        job_read = sem("job_read")
        pickT_ready, place_made = sem("pickT_ready"), sem("place_made")
        e_silu_made, e_hid_made = sem("e_silu_made"), sem("e_hid_made")
        hidT_ready, hidT_hi_made, hidT_lo_made = sem("hidT_ready"), sem("hidT_hi_made"), sem("hidT_lo_made")
        y_made, scatter_ready, scatter_added = sem("y_made"), sem("scatter_ready"), sem("scatter_added")
        out_stored = sem("out_stored")

        block = ctx.enter_context(nc.Block())

        def job_count(eng):
            eng.wait_ge(jobs_ready, 1)
            return eng.value_load(job_int[0:1, 3:4], min_val=EXPERTS, max_val=JOBS)

        def each_job(eng, body):
            with eng.Fori(0, EXPERTS) as j:
                body(j)
            n = job_count(eng)
            with eng.If(n > EXPERTS):
                with eng.Fori(EXPERTS, n) as j:
                    body(j)
            return n

        def by_group(tile, regrouped):
            if regrouped:
                v = tile.rearrange("p (k j g d) -> p g k j d", k=4, j=4, g=SWA_KV)
            else:
                v = tile.rearrange("p (k g j d) -> p g k j d", k=4, g=SWA_KV, j=4)
            return [v[:, g] for g in range(SWA_KV)]

        def head_out(layer, hd, dst):
            if layer == 0:
                lanes = slice(SWA_D * (hd % 2), SWA_D * (hd % 2) + SWA_D)
                return dst[lanes, 4 + hd // 2, :], bank[7][lanes, 0:SEQ]
            return dst[:, hd, :], bank[7][:, 0:SEQ]

        @block.sync
        def _(sp):
            def load(n, src, slot=None):
                if slot is not None or n >= RAW:
                    sp.wait_ge(lo_made, n - RAW + 1)
                slot = n % RAW if slot is None else slot
                sp.dma_start(raw[:, slot].rearrange("p (c n) -> p c n", c=src.shape[1]), src)\
                  .then_inc(tile_loaded[slot], 16)

            def cols_of(w, c0, n, k0=0, k=KC):
                return w[k0 * P:(k0 + k) * P, c0:c0 + n].rearrange("(c p) n -> p c n", p=P)

            def rows_of(w, pair):
                return w[pair * 2 * P:(pair + 1) * 2 * P, :].rearrange("(c p) n -> p c n", p=P)

            w_in = e_w_in[0]
            for i in range(2):
                load(Q0_T + i, cols_of(w_in, 3 * SC, HALF, 4 * i, 4))
            load(KV_T, cols_of(w_in, 4 * SC, 2 * P))
            for i in range(2):
                for part, first in enumerate((SC, 2 * SC, 0)):
                    load(CONV_T + 3 * i + part, cols_of(w_in, first + i * 2 * P, 2 * P))
            for i in range(4):
                load(OUT0_T + i, rows_of(e_w_out[0], i))
            load(FFN_T, cols_of(e_ffn_gate[0], 0, 2 * P))
            load(FFN_T + 1, cols_of(e_ffn_up[0], 0, 2 * P))
            gate_v = e_ffn_gate[0].rearrange("(c p) (i n) -> i p c n", p=P, n=2 * P)
            up_v = e_ffn_up[0].rearrange("(c p) (i n) -> i p c n", p=P, n=2 * P)
            down_v = e_ffn_down[0].rearrange("(i c p) n -> i p c n", p=P, c=2)
            with sp.Fori(0, (PAIRS - 1) // 2) as r:
                for u in range(2):
                    i = 1 + u + 2 * r
                    for part, src in enumerate((gate_v[i], up_v[i], down_v[i - 1])):
                        n = FFN_T + 2 + 3 * u + part
                        load(n + 6 * r, src, slot=n % RAW)
            load(PLE0_T - 1, down_v[PAIRS - 1])
            load(PLE0_T, rows_of(e_ple_proj[0], 0))
            for i in range(4):
                load(PLE0_T + 1 + i, rows_of(e_ple_gate[0], i))
            for i in range(12):
                load(QK_T + i, cols_of(o_w_qkv[0], i * 2 * P, 2 * P))
            for i in range(4):
                load(OUT1_T + i, rows_of(o_w_o[0], i))
            eg = o_exp_gate[0].rearrange("e (c p) (b n) -> e b p c n", p=P, n=HALF)
            eu = o_exp_up[0].rearrange("e (c p) (b n) -> e b p c n", p=P, n=HALF)
            ed = o_exp_down[0].rearrange("e (i c p) n -> e i p c n", p=P, c=2)

            def expert(j, e):
                base = MOE_T + JOB_TILES * j

                halves = tuple(enumerate(((eg, 0), (eg, 4), (eu, 0), (eu, 4))))
                for i, (w, k) in halves:
                    load(base + i, w[e, 0, :, k:k + 4], slot=(MOE_T + i) % RAW)
                with sp.Fori(1, BLOCKS) as b:
                    for i, (w, k) in halves:
                        load(base + 6 * b + (i - 2), w[e, b, :, k:k + 4], slot=(MOE_T + 4 + i) % RAW)
                    for i in range(2):
                        load(base + 6 * b + (i + 2), ed[e, 2 * b + (i - 2)], slot=(MOE_T + 8 + i) % RAW)
                for i in range(2):
                    load(base + (JOB_TILES - 2 + i), ed[e, 2 * BLOCKS - 2 + i], slot=(MOE_T + 4 + i) % RAW)

            with sp.Fori(0, EXPERTS) as j:
                expert(j, j)
            nj = job_count(sp)
            with sp.If(nj > EXPERTS):
                with sp.Fori(EXPERTS, nj) as j:
                    expert(j, sp.value_load(job_int[0:1, bass.ds(j - EXPERTS, 1)], min_val=0, max_val=EXPERTS - 1))
            base = JOB_TILES * nj
            for i in range(5):
                load(base + (PLE1_T + i), rows_of(o_ple_proj[0], 0) if i == 0 else rows_of(o_ple_gate[0], i - 1),
                     slot=(PLE1_T + i) % RAW)
            for t in range(TT):
                sp.wait_ge(xn_ready, TT * 6 + t + 1)
                sp.dma_start(out[0, t * P:(t + 1) * P, :], xn[:, t]).then_inc(out_stored, 16)
            sp.wait_ge(out_stored, 16 * TT)

        @block.gpsimd
        def _(pool):
            def load_gain(i):
                pool.dma_start(gain[:, i % 2], bass.AP(tensor=gains[i].tensor, offset=gains[i].offset, ap=[[0, P], [1, D]]))\
                    .then_inc(gain_loaded[i % 2], 16)

            load_gain(0)
            pool.dma_start(oh, onehots).then_inc(aux_loaded, 16)
            pool.dma_start(rel[0:BUCKETS, :], rel_bias).then_inc(aux_loaded, 16)
            pool.dma_start(rel[BUCKETS:BUCKETS + 1, :], consts[0:1, C_ONES:C_ONES + HEADS]).then_inc(aux_loaded, 16)
            pool.dma_start(sink[:, :], bass.AP(tensor=e_sinks.tensor, offset=0, ap=[[0, P], [1, HEADS]])).then_inc(aux_loaded, 16)
            pool.dma_start(p_raw[:, 0], p[0, 0].rearrange("(t q) n -> q t n", q=P)).then_inc(aux_loaded, 16)
            pool.dma_start(p_raw[:, 1], p[1, 0].rearrange("(t q) n -> q t n", q=P)).then_inc(aux_loaded, 16)
            pool.dma_start(taps, e_conv_w[0].rearrange("k (c q) -> (k c) q", q=P)).then_inc(aux_loaded, 16)
            pool.dma_start(r_raw[:, :, :], o_router[0].rearrange("(c q) e -> q c e", q=P)).then_inc(aux_loaded, 16)
            load_gain(1)
            pool.wait_ge(diag_copied, 2)
            for layer in range(2):
                pool.dma_start(diag_dram[layer], diag[:, layer * DIAGS:(layer + 1) * DIAGS].unsqueeze(1)
                               .broadcast_to((HEADS, P, DIAGS))).then_inc(diag_stored, 16)
            pool.wait_ge(diag_stored, 32)

            def load_bias(layer):
                for first, col, n in ((P, 0, P), (0, P, 2 * P)):
                    pool.dma_start(bias[:, :, col:col + n],
                                   bass.AP(tensor=diag_dram.tensor, offset=layer * HEADS * P * DIAGS + P - 1 + first,
                                           ap=[[DIAGS - 1, P], [P * DIAGS, HEADS], [1, n]])).then_inc(bias_loaded[layer], 16)

            load_bias(0)
            pool.wait_ge(negmax_ready, HEADS)
            load_bias(1)
            for i in range(2, 7):
                pool.wait_ge(xn_ready, TT * (i - 1))
                load_gain(i)

        @block.scalar
        def _(act):
            act.dma_start(h[:, 0], x[0, 0:P, :]).then_inc(x_loaded, 16)
            act.dma_start(h[:, 1], x[0, P:2 * P, :]).then_inc(x_loaded, 16)
            act.dma_start(cst[:, :], consts).then_inc(cst_loaded, 16)

            def split(n, slot=None, rounds=None):
                slot = n % RAW if slot is None else slot
                rounds = n // RAW if rounds is None else rounds
                act.wait_ge(tile_loaded[slot], 16 * rounds + 16)
                act.activation(w_hi[:, slot % SPLIT], raw[:, slot], ACT.Copy).then_inc(hi_made, 1)

            def step(n, slot=None, rounds=None):
                act.wait_ge(tile_used, n + 1)
                split(n + SPLIT if slot is None else None, None if slot is None else (slot + SPLIT) % RAW, rounds)

            def norm(i):
                for t in range(TT):
                    act.wait_ge(*((h_ready, TT * (i - 1) + t + 1) if i else (x_loaded, 32)))
                    act.activation(xn[:, t], h[:, t], ACT.Square, accum_out=ssq[:, 0, t:t + 1]).then_inc(squares_made, 1)
                if i == 6:
                    return
                for g in range(4):
                    t, half = g // 2, g % 2
                    act.wait_ge(xT_ready, 4 * i + g + 1)
                    act.activation(x_hi[:, 4 * half:4 * half + 4, t * P:(t + 1) * P],
                                   bank[g][:, :].rearrange("p (c t) -> p c t", c=4), ACT.Copy).then_inc(x_hi_made, 1)

            def attention(layer, extra):
                for hd in range(HEADS):
                    a = layer * HEADS + hd
                    s, st = score[:, a % 2], stat[:, a % 2]
                    act.wait_ge(negmax_ready, a + 1)
                    act.activation(s[:, 0:P], s[:, 0:P], ACT.Exp, bias=st[:, 1, 0:1], accum_out=st[:, 2, 0:1])
                    if layer == 0:
                        act.activation(st[:, 3, :], st[:, 1, :], ACT.Exp, bias=sink[:, hd:hd + 1])
                    act.activation(s[:, P:DIAGS], s[:, P:DIAGS], ACT.Exp, bias=st[:, 1, 1:2],
                                   accum_out=st[:, 2, 1:2]).then_inc(exp_made, 1)
                    extra(hd)
                    act.wait_ge(probT_ready, a + 1)
                    act.activation(probT[:, :], bank[6][:, 0:DIAGS], ACT.Copy).then_inc(probT_made, 1)
                    act.wait_ge(oT_ready, a + 1)
                    dst, src = head_out(layer, hd, m_hi)
                    act.activation(dst, src, ACT.Copy).then_inc(oT_hi_made, 1)

            for n in range(SPLIT):
                if n == KV_T:
                    split(n)
                    continue
                act.wait_ge(tile_loaded[n], 16)
                for dst, src in zip(by_group(w_hi[:, n], True), by_group(raw[:, n], False)):
                    ins = act.activation(dst, src, ACT.Copy)
                ins.then_inc(hi_made, 1)
            norm(0)
            for l in range(2):
                act.wait_ge(diag_ready, 1 + 2 * l)
                act.activation(diag[:, l * DIAGS:(l + 1) * DIAGS], bank[4 + l][0:HEADS, 0:DIAGS], ACT.Copy).then_inc(diag_copied, 1)
            act.activation(conv_w[:, :], bank[5][:, DIAGS:DIAGS + 12], ACT.Copy).then_inc(diag_copied, 1)
            for l in range(2):
                act.wait_ge(pT_ready, l + 1)
                act.activation(p_hi[:, l], bank[6 + l][:, :].rearrange("p (c t) -> p c t", c=2), ACT.Copy).then_inc(p_hi_made, 1)
            act.activation(r_hi[:, :, :], r_raw[:, :, :], ACT.Copy).then_inc(r_hi_made, 1)
            step(Q0_T)
            step(Q0_T + 1)
            for j in range(4):
                act.activation(q0T[:, j], bank[j][:, 0:SEQ], ACT.Copy).then_inc(q0_made, 1)
            step(KV_T)
            act.activation(k0T, bank[4][:, 0:SEQ], ACT.Copy).then_inc(kv0_made, 1)
            act.activation(v0, bank[5][:, 0:SEQ].rearrange("p (t n) -> p t n", t=TT), ACT.Copy).then_inc(kv0_made, 1)

            def conv_part(hd):
                if hd >= 6:
                    return
                step(CONV_T + hd)
                i, part = hd // 3, hd % 3
                if part == 0:
                    if i:
                        act.wait_ge(conv_made, 1)
                    act.activation(c_sb, bank[(3 * i) % 4][:, :].rearrange("p (j t) -> p j t", j=2), ACT.Copy).then_inc(c_made, 1)
                if part == 2:
                    act.wait_ge(conv_made, i + 1)
                    act.activation(m_hi[:, 2 * i:2 * i + 2], conv_a, ACT.Copy).then_inc(conv_hi_made, 1)

            attention(0, conv_part)
            for i in range(4):
                step(OUT0_T + i)
            norm(1)

            def ffn_up(n, i, slot, rounds):
                step(n, slot, rounds[0])
                if not isinstance(i, int):
                    act.wait_ge(hid_made, i)
                act.activation(silu, bank[0][:, :], ACT.Silu).then_inc(silu_made, 1)
                step(n + 1, (slot + 1) % RAW, rounds[1])

            def ffn_hidden(i):
                act.wait_ge(hid_made, i + 1)
                act.activation(hid_hi, hid.rearrange("p (j t) -> p j t", j=2), ACT.Copy).then_inc(hid_hi_made, 1)

            def rounds(n):
                return (n + SPLIT) // RAW

            ffn_up(FFN_T, 0, FFN_T % RAW, (rounds(FFN_T), rounds(FFN_T + 1)))
            ffn_hidden(0)
            with act.Fori(0, (PAIRS - 1) // 2) as r:
                for u in range(2):
                    n = FFN_T + 2 + 3 * u
                    ffn_up(n + 6 * r, 1 + u + 2 * r, n % RAW, (rounds(n) + r, rounds(n + 1) + r))
                    step(n + 2 + 6 * r, (n + 2) % RAW, rounds(n + 2) + r)
                    ffn_hidden(1 + u + 2 * r)
            step(PLE0_T - 1)

            def ple(l, n, nj=None):
                def st(i):
                    if nj is None:
                        step(n + i)
                    elif i < 2:
                        step(n + i, (PLE1_T + i) % RAW, rounds(PLE1_T + i) + (JOB_TILES // RAW) * nj)
                st(0)
                norm(2 if l == 0 else 5)
                for i in range(1, 5):
                    st(i)
                if nj is not None:
                    act.wait_ge(tile_used, n + 5)
                for b in range(4):
                    act.activation(sig[:, b], bank[b][:, :], ACT.Sigmoid).then_inc(sig_made, 1)

            ple(0, PLE0_T)
            norm(3)
            for i in range(8):
                step(QK_T + i)
                dst = (q1T if i < 4 else k1T)[:, 2 * (i % 4):2 * (i % 4) + 2]
                act.activation(dst, bank[i % 4][:, :].rearrange("p (j t) -> p j t", j=2), ACT.Copy).then_inc(qkv1_made, 1)

            def v_part(hd):
                if hd >= 4:
                    return
                step(V_T + hd)
                act.activation(v1[:, :, hd * 2 * P:(hd + 1) * 2 * P],
                               bank[hd][:, :].rearrange("p (t n) -> p t n", t=TT), ACT.Copy).then_inc(qkv1_made, 1)

            attention(1, v_part)
            for i in range(4):
                step(OUT1_T + i)
            norm(4)
            act.wait_ge(route_exp_ready, 1)
            for t in range(TT):
                act.activation(route[:, 32 + 8 * t:40 + 8 * t], route[:, 8 * t:8 * t + 8], ACT.Exp,
                               bias=route[:, 24 + t:25 + t]).then_inc(route_exp_made, 1)

            def gathered(j):
                act.wait_ge(gather_ready, j + 1)
                for half in range(2):
                    act.activation(x_hi[:, 4 * half:4 * half + 4, 0:P],
                                   bank[4 + half][:, :].rearrange("p (c t) -> p c t", c=4), ACT.Copy).then_inc(xg_hi_made, 1)

            def expert(j):
                done = JOB_TILES * j

                def st(k, b=None):
                    n = MOE_T + k
                    r = (n + SPLIT) // RAW + (JOB_TILES // RAW) * j
                    if b is None:
                        step(n + done, n % RAW, r)
                    else:
                        step(n + done + 6 * b, n % RAW, r + b)

                def silu_of():
                    act.activation(silu, bank[0][:, :], ACT.Silu).then_inc(e_silu_made, 1)

                def hidT_of(b):
                    act.wait_ge(hidT_ready, BLOCKS * j + b + 1)
                    act.activation(hidT_hi, bank[2][:, :].rearrange("p (c t) -> p c t", c=4), ACT.Copy).then_inc(hidT_hi_made, 1)

                st(0)
                st(1)
                silu_of()
                st(2)
                st(3)
                hidT_of(0)
                act.wait_ge(pickT_ready, j + 1)
                act.activation(place, bank[3][:, 0:2 * P], ACT.Copy).then_inc(place_made, 1)
                with act.Fori(1, BLOCKS) as b:
                    st(-2, b)
                    st(-1, b)
                    silu_of()
                    for k in range(4):
                        st(k, b)
                    hidT_of(b)
                gathered(j + 1)
                st(JOB_TILES - 2)
                st(JOB_TILES - 1)
                for half in range(2):
                    act.activation(y_sb[:, half * HALF:(half + 1) * HALF], bank[6 + half][:, :], ACT.Copy).then_inc(y_made, 1)

            gathered(0)
            nj = each_job(act, expert)
            ple(1, PLE1_T + JOB_TILES * nj, nj)
            norm(6)

        PASSES = ((0, 1), (1, 0), (0, 0))

        @block.tensor
        def _(pe):
            def three(dst, stat_hl, mov_hl, start, stop, tick=None):
                for i, (a, b) in enumerate(PASSES):
                    mm = pe.matmul(dst, stat_hl[a], mov_hl[b], start=start and i == 0, stop=stop and i == 2)
                if tick is not None:
                    mm.then_inc(tick, 1)

            def w_tile(slot, n):
                return [w[:, slot % SPLIT].rearrange("p (c n) -> p c n", n=n) for w in (w_hi, w_lo)]

            def both(pair, *at):
                return [t[at] for t in pair]

            XHL, MHL = (x_hi, x_lo), (m_hi, m_lo)
            ALL = slice(None)

            def wait_tile(n):
                pe.wait_ge(lo_made, n + 1)

            def up_tile(n, b, slot=None):
                wait_tile(n)
                w = w_tile(n if slot is None else slot, 2 * P)
                for f in range(2):
                    for k in range(KC):
                        three(bank[b][:, f * SEQ:(f + 1) * SEQ], both(w, ALL, k, slice(f * P, (f + 1) * P)),
                              both(XHL, ALL, k), k == 0, k == KC - 1, tile_used if (f, k) == (1, KC - 1) else None)

            def token_tile(n, b, first, cols, tick):
                w = w_tile(n, 2 * P)
                for t in range(TT):
                    for k in range(KC):
                        three(bank[b][:, t * cols:(t + 1) * cols], both(XHL, ALL, k, slice(t * P, (t + 1) * P)),
                              both(w, ALL, k, slice(first, first + cols)), k == 0, k == KC - 1,
                              tick if (t, k) == (TT - 1, KC - 1) else None)

            def down_tile(n, a, c0, b0, start, stop, slot=None):
                wait_tile(n)
                w = w_tile(n if slot is None else slot, D)
                for kk in range(2):
                    for t in range(TT):
                        for half in range(2):
                            three(bank[b0 + 2 * t + half][:, :], both(a, ALL, c0 + kk, slice(t * P, (t + 1) * P)),
                                  both(w, ALL, kk, slice(half * HALF, (half + 1) * HALF)),
                                  start and kk == 0, stop and kk == 1,
                                  tile_used if (kk, t, half) == (1, TT - 1, 1) else None)

            def norm(i):
                for g in range(4):
                    t, half = g // 2, g % 2
                    pe.wait_ge(xn_ready, TT * i + t + 1)
                    for c in range(4):
                        at = (4 * half + c) * P
                        mm = pe.transpose(bank[g][:, c * P:(c + 1) * P], xn[:, t, at:at + P], ident)
                    mm.then_inc(xT_ready, 1)

            def attention(layer, qT_of, kT_of, v_of, extra):
                def scores(hd):
                    a = layer * HEADS + hd
                    b = bank[4 + a % 2]
                    if hd >= 2:
                        pe.wait_ge(negmax_ready, a - 1)
                    q, k = qT_of(hd), kT_of(hd)
                    pe.matmul(b[:, 0:P], q[:, 0:P], k[:, 0:P], start=True, stop=True)
                    pe.matmul(b[:, P:DIAGS], q[:, P:SEQ], k, start=True, stop=True).then_inc(scores_ready, 1)

                scores(0)
                scores(1)
                for hd in range(HEADS):
                    a = layer * HEADS + hd
                    extra(hd)
                    pe.wait_ge(probs_ready, a + 1)
                    if hd:
                        pe.wait_ge(probT_made, a)
                    for c in range(3):
                        mm = pe.transpose(bank[6][:, c * P:(c + 1) * P], score[:, a % 2, c * P:(c + 1) * P], ident)
                    mm.then_inc(probT_ready, 1)
                    if hd + 2 < HEADS:
                        scores(hd + 2)
                    pe.wait_ge(probT_made, a + 1)
                    if hd:
                        pe.wait_ge(oT_lo_made, a)
                    o = head_out(layer, hd, m_hi)[1]
                    v = v_of(hd)
                    pe.matmul(o[:, 0:P], v[0], probT[:, 0:P], start=True, stop=True)
                    pe.matmul(o[:, P:SEQ], v[0], probT[:, P:2 * P], start=True, stop=False)
                    pe.matmul(o[:, P:SEQ], v[1], probT[:, 2 * P:DIAGS], start=False, stop=True).then_inc(oT_ready, 1)

            pe.wait_ge(cst_loaded, 16)
            norm(0)
            pe.wait_ge(aux_loaded, 128)
            for l in range(2):
                pe.matmul(bank[4 + l][0:HEADS, 0:DIAGS], rel[:, :], oh[:, l * DIAGS:(l + 1) * DIAGS],
                          start=True, stop=True).then_inc(diag_ready, 1)
            pe.transpose(bank[5][:, DIAGS:DIAGS + 12], taps, cst[0:12, C_IDENT:C_IDENT + 12]).then_inc(diag_ready, 1)
            for l in range(2):
                for c in range(2):
                    for t in range(TT):
                        mm = pe.transpose(bank[6 + l][:, c * SEQ + t * P:c * SEQ + (t + 1) * P],
                                          p_raw[:, l, t, c * P:(c + 1) * P], ident)
                mm.then_inc(pT_ready, 1)
            pe.wait_ge(x_lo_made, 4)
            for i in range(2):
                wait_tile(Q0_T + i)
                w = w_tile(Q0_T + i, HALF)
                for j in range(4):
                    for k in range(4):
                        three(bank[j][:, 0:SEQ], both(w, ALL, k, slice(j * P, (j + 1) * P)), both(XHL, ALL, 4 * i + k), (i, k) == (0, 0), (i, k) == (1, 3),
                              tile_used if (j, k) == (3, 3) else None)
            wait_tile(KV_T)
            w = w_tile(KV_T, 2 * P)
            pe.wait_ge(diag_copied, 3)
            for k in range(KC):
                three(bank[4][:, 0:SEQ], both(w, ALL, k, slice(0, P)), both(XHL, ALL, k), k == 0, k == KC - 1)
            token_tile(KV_T, 5, P, P, tile_used)
            pe.wait_ge(kv0_made, 2)
            pe.wait_ge(q0_made, 4)

            def group(hd):
                return slice(SWA_D * (hd // 4), SWA_D * (hd // 4) + SWA_D)

            def conv_part(hd):
                if hd >= 6:
                    return
                if hd == 4:
                    pe.wait_ge(c_made, 1)
                if hd == 5:
                    pe.wait_ge(conv_made, 1)
                up_tile(CONV_T + hd, hd % 4)

            pe.wait_ge(p_lo_made, 2)
            attention(0, lambda hd: q0T[group(hd), hd % 4], lambda hd: k0T[group(hd)],
                      lambda hd: [v0[:, t, group(hd)] for t in range(TT)], conv_part)
            pe.wait_ge(conv_lo_made, 2)
            pe.wait_ge(oT_lo_made, HEADS)
            for i in range(4):
                down_tile(OUT0_T + i, MHL, 2 * i, 4, i == 0, i == 3)
            norm(1)
            HHL = (hid_hi, hid_lo)
            pe.wait_ge(x_lo_made, 8)
            up_tile(FFN_T, 0)
            up_tile(FFN_T + 1, 1)
            pe.wait_ge(h_ready, TT)
            pe.wait_ge(memsets_done, 2)
            for b in range(4, 8):
                for q in range(4):
                    pe.matmul(bank[b][:, q * P:(q + 1) * P], zeros_r[:, :], zeros_r[:, :], start=q == 0, stop=False,
                              skip_group_check=True)

            def acc_down(n, a, slot, stop):
                wait_tile(n)
                w = w_tile(slot, D)
                for kk in range(2):
                    for t in range(TT):
                        for half in range(2):
                            for i, (s, m) in enumerate(PASSES):
                                mm = pe.matmul(bank[4 + 2 * t + half][:, :], a[s][:, kk, t * P:(t + 1) * P],
                                               w[m][:, kk, half * HALF:(half + 1) * HALF], start=False,
                                               stop=stop and (kk, i) == (1, 2), skip_group_check=True)
                mm.then_inc(tile_used, 1)

            with pe.Fori(0, (PAIRS - 1) // 2) as r:
                for u in range(2):
                    n = FFN_T + 2 + 3 * u
                    pe.wait_ge(silu_made, 2 * r + (1 + u))
                    up_tile(n + 6 * r, 0, n)
                    pe.wait_ge(hid_made, 2 * r + (1 + u))
                    up_tile(n + 1 + 6 * r, 1, n + 1)
                    pe.wait_ge(hid_lo_made, 2 * r + (1 + u))
                    acc_down(n + 2 + 6 * r, HHL, n + 2, False)
            pe.wait_ge(hid_lo_made, PAIRS)
            acc_down(PLE0_T - 1, HHL, PLE0_T - 1, True)

            def ple(l, n):
                i = 2 if l == 0 else 5
                pe.wait_ge(h_ready, TT * i)
                down_tile(n, (p_hi[:, l], p_lo[:, l]), 0, 4, True, True, PLE0_T if l == 0 else PLE1_T)
                norm(i)
                pe.wait_ge(x_lo_made, 4 * i + 4)
                for g in range(4):
                    down_tile(n + 1 + g, XHL, 2 * g, 0, g == 0, g == 3, (PLE0_T if l == 0 else PLE1_T) + 1 + g)

            ple(0, PLE0_T)
            norm(3)
            pe.wait_ge(x_lo_made, 16)
            for i in range(8):
                if i >= 4:
                    pe.wait_ge(qkv1_made, i - 3)
                up_tile(QK_T + i, i % 4)
            pe.wait_ge(qkv1_made, 8)

            def v_part(hd):
                if hd < 4:
                    wait_tile(V_T + hd)
                    token_tile(V_T + hd, hd, 0, 2 * P, tile_used)
                    pe.wait_ge(qkv1_made, 9 + hd)

            attention(1, lambda hd: q1T[:, hd], lambda hd: k1T[:, hd],
                      lambda hd: [v1[:, t, hd * P:(hd + 1) * P] for t in range(TT)], v_part)
            pe.wait_ge(oT_lo_made, 2 * HEADS)
            for i in range(4):
                down_tile(OUT1_T + i, MHL, 2 * i, 4, i == 0, i == 3)
            norm(4)
            pe.wait_ge(x_lo_made, 20)
            pe.wait_ge(r_lo_made, 1)
            for t in range(TT):
                for k in range(KC):
                    three(bank[4][:, t * EXPERTS:(t + 1) * EXPERTS], both(XHL, ALL, k, slice(t * P, (t + 1) * P)),
                          (r_hi[:, k], r_lo[:, k]), k == 0, k == KC - 1, logits_ready if (t, k) == (1, KC - 1) else None)
            pe.wait_ge(chosen_ready, 1)
            tri, ones = cst[:, C_TRI:C_TRI + P], cst[:, C_ONES:C_ONES + P]
            chosen = [route[:, 64 + 8 * t:72 + 8 * t] for t in range(TT)]
            pe.matmul(bank[5][:, 0:8], tri, chosen[0], start=True, stop=True)
            pe.matmul(bank[5][:, 8:16], tri, chosen[1], start=True, stop=False)
            pe.matmul(bank[5][:, 8:16], ones, chosen[0], start=False, stop=True)
            pe.matmul(bank[5][:, 16:24], ones, chosen[0], start=True, stop=False)
            pe.matmul(bank[5][:, 16:24], ones, chosen[1], start=False, stop=True).then_inc(ranks_ready, 1)

            def gather(j):
                pe.wait_ge(pick_made, j + 1)
                for c in range(KC):
                    for t in range(TT):
                        mm = pe.matmul(bank[4 + c // 4][:, (c % 4) * P:(c % 4 + 1) * P], xn[:, t, c * P:(c + 1) * P],
                                       pick[:, t], start=t == 0, stop=t == TT - 1)
                mm.then_inc(gather_ready, 1)

            def scatter(j):
                pe.wait_ge(y_made, 2 * j + 2)
                pe.wait_ge(place_made, j + 1)
                for q in range(4):
                    pe.matmul(bank[2 + q][:, :], place[:, (q // 2) * P:(q // 2 + 1) * P],
                              y_sb[:, (q % 2) * HALF:(q % 2 + 1) * HALF], start=True, stop=True).then_inc(scatter_ready, 1)

            def expert(j):
                def up(k, b=None):
                    for i in range(4):
                        n = MOE_T + k + i
                        wait_tile(n + JOB_TILES * j if b is None else n + JOB_TILES * j + 6 * b)
                        w = w_tile(n, HALF)
                        for kk in range(4):
                            three(bank[i // 2][:, :], both(XHL, ALL, 4 * (i % 2) + kk, slice(0, P)), both(w, ALL, kk),
                                  (i % 2, kk) == (0, 0), (i % 2, kk) == (1, 3), tile_used if kk == 3 else None)

                def down(k, b, prev, stop):
                    pe.wait_ge(hidT_lo_made, BLOCKS * j + prev + 1)
                    for i in range(2):
                        n = MOE_T + k + i
                        wait_tile(n + JOB_TILES * j if b is None else n + JOB_TILES * j + 6 * b)
                        w = w_tile(n, D)
                        for kk in range(2):
                            for half in range(2):
                                for q, (s, m) in enumerate(PASSES):
                                    mm = pe.matmul(bank[6 + half][:, :], (hidT_hi, hidT_lo)[s][:, 2 * i + kk, :],
                                                   w[m][:, kk, half * HALF:(half + 1) * HALF], start=False,
                                                   stop=stop and (i, kk, q) == (1, 1, 2), skip_group_check=True)
                        mm.then_inc(tile_used, 1)

                def turn(b):
                    pe.wait_ge(e_hid_made, BLOCKS * j + b + 1)
                    for c in range(4):
                        mm = pe.transpose(bank[2][:, c * P:(c + 1) * P], hid[:, c * P:(c + 1) * P], ident)
                    mm.then_inc(hidT_ready, 1)

                pe.wait_ge(xg_lo_made, 2 * j + 2)
                up(0)
                scatter(j)
                for half in range(2):
                    for q in range(4):
                        pe.matmul(bank[6 + half][:, q * P:(q + 1) * P], zeros_r[:, :], zeros_r[:, :], start=q == 0,
                                  stop=False, skip_group_check=True)
                pe.wait_ge(scatter_added, 4 * j + 2)
                turn(0)
                for t in range(TT):
                    mm = pe.transpose(bank[3][:, t * P:(t + 1) * P], pick_g[:, t], ident)
                mm.then_inc(pickT_ready, 1)
                with pe.Fori(1, BLOCKS) as b:
                    up(-2, b)
                    down(2, b, b - 1, False)
                    turn(b)
                pe.wait_ge(scatter_added, 4 * j + 4)
                gather(j + 1)
                down(JOB_TILES - 2, None, BLOCKS - 1, True)

            gather(0)
            nj = each_job(pe, expert)
            pe.wait_ge(xg_lo_made, 2 * nj + 2)
            scatter(nj)
            ple(1, PLE1_T + JOB_TILES * nj)

        @block.vector
        def _(ve):
            steps = [0]

            def link(ins):
                ins.then_inc(vec_step, 1)
                steps[0] += 1
                ve.wait_ge(vec_step, steps[0])

            def split(n, slot=None):
                slot = n % RAW if slot is None else slot % RAW
                ve.wait_ge(hi_made, n + 1)
                ve.tensor_tensor(w_lo[:, slot % SPLIT], raw[:, slot], w_hi[:, slot % SPLIT], ALU.subtract).then_inc(lo_made, 1)

            def norm(i):
                v, a, b, y = ssq[:, 0], ssq[:, 1], ssq[:, 2], rstd[:, :]
                ve.wait_ge(squares_made, TT * i + 2)
                link(ve.tensor_scalar(v, v, 1.0 / D, EPS, ALU.mult, ALU.add))
                link(ve.tensor_scalar(y.bitcast(I32), v.bitcast(I32), 1, None, ALU.logical_shift_right))
                link(ve.tensor_scalar(y.bitcast(I32), y.bitcast(I32), -1.0, float(0x5F3759DF), ALU.mult, ALU.add))
                for _ in range(4):
                    link(ve.tensor_tensor(a, y, y, ALU.mult))
                    link(ve.scalar_tensor_tensor(out=b, in0=a, scalar=-0.5, in1=v, op0=ALU.mult, op1=ALU.mult))
                    link(ve.scalar_tensor_tensor(out=y, in0=b, scalar=1.5, in1=y, op0=ALU.add, op1=ALU.mult))
                ve.wait_ge(gain_loaded[i % 2], 16 * (i // 2 + 1))
                for t in range(TT):
                    ve.scalar_tensor_tensor(out=xn[:, t], in0=h[:, t], scalar=rstd[:, t:t + 1], in1=gain[:, i % 2],
                                            op0=ALU.mult, op1=ALU.mult).then_inc(xn_ready, 1)
                if i == 6:
                    return
                for g in range(4):
                    t, half = g // 2, g % 2
                    ve.wait_ge(x_hi_made, 4 * i + g + 1)
                    at = (slice(None), slice(4 * half, 4 * half + 4), slice(t * P, (t + 1) * P))
                    ve.tensor_tensor(x_lo[at], bank[g][:, :].rearrange("p (c t) -> p c t", c=4), x_hi[at],
                                     ALU.subtract).then_inc(x_lo_made, 1)

            def add_banks():
                for t in range(TT):
                    for half in range(2):
                        at = h[:, t, half * HALF:(half + 1) * HALF]
                        ins = ve.tensor_tensor(at, at, bank[4 + 2 * t + half][:, :], ALU.add)
                    ins.then_inc(h_ready, 1)

            def attention(layer, scale, extra):
                for hd in range(HEADS):
                    a = layer * HEADS + hd
                    s, st = score[:, a % 2], stat[:, a % 2]
                    ve.wait_ge(scores_ready, a + 1)
                    if hd == 0:
                        ve.wait_ge(bias_loaded[layer], 32)
                    link(ve.scalar_tensor_tensor(out=s, in0=bank[4 + a % 2][:, 0:DIAGS], scalar=scale, in1=bias[:, hd],
                                                 op0=ALU.mult, op1=ALU.add))
                    ve.tensor_reduce(st[:, 0, 0:1], s[:, 0:P], AX, ALU.max)
                    link(ve.tensor_reduce(st[:, 0, 1:2], s[:, P:DIAGS], AX, ALU.max))
                    if layer == 0:
                        ve.tensor_scalar(st[:, 1, :], st[:, 0, :], sink[:, hd:hd + 1], -1.0, ALU.max, ALU.mult)\
                            .then_inc(negmax_ready, 1)
                    else:
                        ve.tensor_scalar(st[:, 1, :], st[:, 0, :], -1.0, None, ALU.mult).then_inc(negmax_ready, 1)
                    ve.wait_ge(exp_made, a + 1)
                    if layer == 0:
                        link(ve.tensor_tensor(st[:, 2], st[:, 2], st[:, 3], ALU.add))
                    link(ve.reciprocal(st[:, 4], st[:, 2]))
                    ve.tensor_scalar(s[:, 0:P], s[:, 0:P], st[:, 4, 0:1], None, ALU.mult)
                    ve.tensor_scalar(s[:, P:DIAGS], s[:, P:DIAGS], st[:, 4, 1:2], None, ALU.mult).then_inc(probs_ready, 1)
                    extra(hd)
                    ve.wait_ge(oT_hi_made, a + 1)
                    dst, src = head_out(layer, hd, m_lo)
                    hi = head_out(layer, hd, m_hi)[0]
                    ve.tensor_tensor(dst, src, hi, ALU.subtract).then_inc(oT_lo_made, 1)

            ve.memset(zeros_r[:, :].bitcast(F32), 0.0).then_inc(memsets_done, 1)
            ve.memset(cu[:, :, 0:2], 0.0).then_inc(memsets_done, 1)
            for n in range(SPLIT):
                if n == KV_T:
                    split(n)
                    continue
                ve.wait_ge(hi_made, n + 1)
                for dst, src, hi in zip(by_group(w_lo[:, n], True), by_group(raw[:, n], False), by_group(w_hi[:, n], True)):
                    ins = ve.tensor_tensor(dst, src, hi, ALU.subtract)
                ins.then_inc(lo_made, 1)
            ve.wait_ge(x_loaded, 32)
            norm(0)
            for l in range(2):
                ve.wait_ge(p_hi_made, l + 1)
                ve.tensor_tensor(p_lo[:, l], bank[6 + l][:, :].rearrange("p (c t) -> p c t", c=2), p_hi[:, l],
                                 ALU.subtract).then_inc(p_lo_made, 1)
            ve.wait_ge(r_hi_made, 1)
            ve.tensor_tensor(r_lo[:, :, :], r_raw[:, :, :], r_hi[:, :, :], ALU.subtract).then_inc(r_lo_made, 1)
            ve.wait_ge(aux_loaded, 128)
            ve.wait_ge(diag_copied, 3)
            ve.wait_ge(memsets_done, 2)
            for i in range(3):
                split(SPLIT + i)

            def conv_part(hd):
                if hd >= 6:
                    return
                i, part = hd // 3, hd % 3
                ve.wait_ge(tile_used, CONV_T + hd + 1)
                ps = bank[hd % 4][:, :].rearrange("p (j t) -> p j t", j=2)
                if part == 1:
                    ve.wait_ge(c_made, i + 1)
                    link(ve.tensor_tensor(cu[:, 2 * i:2 * i + 2, 2:SEQ + 2], c_sb, ps, ALU.mult))
                    for tap in range(3):
                        for j in range(2):
                            src, w = cu[:, 2 * i + j, tap:tap + SEQ], conv_w[:, 4 * tap + 2 * i + j:4 * tap + 2 * i + j + 1]
                            if tap == 0:
                                ins = ve.tensor_scalar(conv_y[:, j], src, w, None, ALU.mult)
                            else:
                                ins = ve.scalar_tensor_tensor(out=conv_y[:, j], in0=src, scalar=w, in1=conv_y[:, j],
                                                              op0=ALU.mult, op1=ALU.add)
                        link(ins)
                if part == 2:
                    ve.tensor_tensor(conv_a, conv_y, ps, ALU.mult).then_inc(conv_made, 1)
                    ve.wait_ge(conv_hi_made, i + 1)
                    ve.tensor_tensor(m_lo[:, 2 * i:2 * i + 2], conv_a, m_hi[:, 2 * i:2 * i + 2], ALU.subtract)\
                        .then_inc(conv_lo_made, 1)
                split(CONV_T + hd + SPLIT)

            attention(0, SWA_D ** -0.5, conv_part)
            for i in range(4):
                split(OUT0_T + i + SPLIT)
            ve.wait_ge(tile_used, OUT0_T + 4)
            add_banks()
            norm(1)

            def hidden(n, i):
                ve.wait_ge(tile_used, n + 1)
                ve.wait_ge(silu_made, i + 1)
                if not isinstance(i, int):
                    ve.wait_ge(hid_lo_made, i)
                ve.tensor_tensor(hid, silu, bank[1][:, :], ALU.mult).then_inc(hid_made, 1)

            def hidden_lo(i):
                ve.wait_ge(hid_hi_made, i + 1)
                ve.tensor_tensor(hid_lo, hid.rearrange("p (j t) -> p j t", j=2), hid_hi, ALU.subtract).then_inc(hid_lo_made, 1)

            split(FFN_T + SPLIT)
            hidden(FFN_T + 1, 0)
            split(FFN_T + 1 + SPLIT)
            hidden_lo(0)
            with ve.Fori(0, (PAIRS - 1) // 2) as r:
                for u in range(2):
                    n = FFN_T + 2 + 3 * u
                    i = 1 + u + 2 * r
                    split(n + SPLIT + 6 * r, n + SPLIT)
                    hidden(n + 1 + 6 * r, i)
                    split(n + 1 + SPLIT + 6 * r, n + 1 + SPLIT)
                    split(n + 2 + SPLIT + 6 * r, n + 2 + SPLIT)
                    hidden_lo(i)
            split(PLE0_T - 1 + SPLIT)
            ve.wait_ge(tile_used, PLE0_T)
            add_banks()

            def ple(l, nj=None):
                if nj is None:
                    split(PLE0_T + SPLIT)
                    norm(2)
                    for i in range(1, 5):
                        split(PLE0_T + i + SPLIT)
                else:
                    split(PLE1_T + SPLIT + JOB_TILES * nj, PLE1_T + SPLIT)
                    norm(5)
                    split(PLE1_T + 1 + SPLIT + JOB_TILES * nj, PLE1_T + 1 + SPLIT)
                for b in range(4):
                    t, half = b // 2, b % 2
                    ve.wait_ge(sig_made, 4 * l + b + 1)
                    link(ve.tensor_tensor(gated, sig[:, b], bank[4 + b][:, :], ALU.mult))
                    at = h[:, t, half * HALF:(half + 1) * HALF]
                    ins = ve.tensor_tensor(at, at, gated, ALU.add)
                    if half == 0:
                        link(ins)
                    else:
                        ins.then_inc(h_ready, 1)
                        ve.wait_ge(h_ready, TT * (2 if l == 0 else 5) + t + 1)

            ple(0)
            norm(3)
            for i in range(8):
                split(QK_T + i + SPLIT)

            def v_part(hd):
                if hd < 4:
                    split(V_T + hd + SPLIT)

            attention(1, MOBA_D ** -0.5, v_part)
            for i in range(4):
                split(OUT1_T + i + SPLIT)
            ve.wait_ge(tile_used, OUT1_T + 4)
            add_banks()
            norm(4)
            E = EXPERTS
            R = lambda a, n: route[:, a:a + n]
            logit = R(0, 16).rearrange("p (t e) -> p t e", t=TT)
            top, negtop = R(16, 2), R(24, 2)
            ex = R(32, 16).rearrange("p (t e) -> p t e", t=TT)
            rank = R(48, 16).rearrange("p (t e) -> p t e", t=TT)
            chosen = R(64, 16).rearrange("p (t e) -> p t e", t=TT)
            gate = R(80, 16).rearrange("p (t e) -> p t e", t=TT)
            pos1 = R(96, 16).rearrange("p (t e) -> p t e", t=TT)
            den, rden = R(112, 2), R(114, 2)
            over, orank, is_o = R(116, 8), R(124, 8), R(132, 8)
            sums, eid = R(140, 4), R(144, 4)
            tmp = R(160, 64).rearrange("p (e f) -> p e f", e=E)
            tmp2 = R(224, 64).rearrange("p (e f) -> p e f", e=E)
            tmp3 = R(288, 16).rearrange("p (t e) -> p t e", t=TT)
            before = cst[:, C_BEFORE:C_EIDX].rearrange("p (e f) -> p e f", e=E)
            eidx = cst[:, C_EIDX:C_END]
            ve.wait_ge(logits_ready, 1)
            link(ve.tensor_copy(logit, bank[4][:, 0:2 * E].rearrange("p (t e) -> p t e", t=TT)))
            link(ve.tensor_reduce(top, logit, AX, ALU.max))
            ve.tensor_scalar(negtop, top, -1.0, None, ALU.mult).then_inc(route_exp_ready, 1)
            for t in range(TT):
                mine = logit[:, t].unsqueeze(2).broadcast_to((P, E, E))
                other = logit[:, t].unsqueeze(1).broadcast_to((P, E, E))
                ve.tensor_tensor(tmp, other, mine, ALU.is_gt)
                link(ve.tensor_tensor(tmp2, other, mine, ALU.is_equal))
                link(ve.tensor_tensor(tmp2, tmp2, before, ALU.mult))
                link(ve.tensor_tensor(tmp, tmp, tmp2, ALU.add))
                link(ve.tensor_reduce(rank[:, t], tmp, AX, ALU.add))
            ve.tensor_scalar(chosen, rank, TOP_K - 0.5, None, ALU.is_lt).then_inc(chosen_ready, 1)
            ve.wait_ge(chosen_ready, 1)
            ve.wait_ge(route_exp_made, 2)
            link(ve.tensor_tensor(ex, ex, chosen, ALU.mult))
            link(ve.tensor_reduce(den, ex, AX, ALU.add))
            link(ve.reciprocal(rden, den))
            for t in range(TT):
                link(ve.tensor_scalar(gate[:, t], ex[:, t], rden[:, t:t + 1], None, ALU.mult))
            ve.wait_ge(ranks_ready, 1)
            link(ve.scalar_tensor_tensor(out=pos1, in0=bank[5][:, 0:2 * E].rearrange("p (t e) -> p t e", t=TT),
                                         scalar=1.0, in1=chosen, op0=ALU.add, op1=ALU.mult))
            for t in range(TT):
                ve.tensor_scalar(jobs[:, 0:E, 0, t], pos1[:, t], -1.0, None, ALU.add)
                ve.tensor_copy(jobs[:, 0:E, 1, t], gate[:, t])
            link(ve.tensor_scalar(over, bank[5][:, 2 * E:3 * E], P + 0.5, None, ALU.is_gt))
            link(ve.tensor_tensor(tmp, before, over.unsqueeze(1).broadcast_to((P, E, E)), ALU.mult))
            ve.tensor_reduce(orank, tmp, AX, ALU.add)
            link(ve.tensor_reduce(eid[:, 3:4], over, AX, ALU.add))
            link(ve.tensor_scalar(eid[:, 3:4], eid[:, 3:4], float(EXPERTS), None, ALU.add))
            for o in range(EXTRA):
                link(ve.scalar_tensor_tensor(out=is_o, in0=orank, scalar=float(o), in1=over, op0=ALU.is_equal, op1=ALU.mult))
                link(ve.tensor_tensor(tmp3[:, 0], is_o, eidx, ALU.mult))
                link(ve.tensor_reduce(eid[:, o:o + 1], tmp3[:, 0], AX, ALU.add))
                for t in range(TT):
                    link(ve.tensor_tensor(tmp3[:, 0], is_o, pos1[:, t], ALU.mult))
                    link(ve.tensor_tensor(tmp3[:, 1], is_o, gate[:, t], ALU.mult))
                    link(ve.tensor_reduce(sums[:, 0:2], tmp3, AX, ALU.add))
                    ve.tensor_scalar(jobs[:, E + o, 0, t:t + 1], sums[:, 0:1], -1.0 - P, None, ALU.add)
                    link(ve.tensor_copy(jobs[:, E + o, 1, t:t + 1], sums[:, 1:2]))
            link(ve.memset(jobs[:, JOBS], -1.0))
            ve.tensor_copy(job_int[:, :], eid[0:1, :]).then_inc(jobs_ready, 1)

            def picks(j):
                ve.tensor_copy(job[:, :, :, :], jobs[:, bass.ds(j, 1), :, :]).then_inc(job_read, 1)
                ve.wait_ge(job_read, j + 1)
                for t in range(TT):
                    ve.tensor_scalar(pick_g[:, t], iota, job[:, 0, 0, t:t + 1], job[:, 0, 1, t:t + 1], ALU.is_equal, ALU.mult)
                for t in range(TT):
                    ins = ve.tensor_scalar(pick[:, t], iota, job[:, 0, 0, t:t + 1], None, ALU.is_equal)
                ins.then_inc(pick_made, 1)

            def gathered(j):
                for half in range(2):
                    ve.wait_ge(xg_hi_made, 2 * j + (half + 1))
                    at = x_lo[:, 4 * half:4 * half + 4, 0:P]
                    ve.tensor_tensor(at, bank[4 + half][:, :].rearrange("p (c t) -> p c t", c=4),
                                     x_hi[:, 4 * half:4 * half + 4, 0:P], ALU.subtract).then_inc(xg_lo_made, 1)

            def scattered(j, last=False):
                for q in range(4):
                    ve.wait_ge(scatter_ready, 4 * j + (q + 1))
                    at = h[:, q // 2, (q % 2) * HALF:(q % 2 + 1) * HALF]
                    ins = ve.tensor_tensor(at, at, bank[2 + q][:, :], ALU.add)
                    if not last:
                        ins.then_inc(scatter_added, 1)
                    elif q % 2:
                        ins.then_inc(h_ready, 1)

            def expert(j):
                def lo(k, b=None):
                    n = MOE_T + k + SPLIT
                    split(n + JOB_TILES * j if b is None else n + JOB_TILES * j + 6 * b, n)

                def hidden_of(k, b, looped):
                    n = MOE_T + k + 1 + JOB_TILES * j
                    ve.wait_ge(tile_used, n + 6 * b if looped else n)
                    ve.wait_ge(e_silu_made, BLOCKS * j + b + 1)
                    ve.tensor_tensor(hid, silu, bank[1][:, :], ALU.mult).then_inc(e_hid_made, 1)

                def hidT_of(b):
                    ve.wait_ge(hidT_hi_made, BLOCKS * j + b + 1)
                    ve.tensor_tensor(hidT_lo, bank[2][:, :].rearrange("p (c t) -> p c t", c=4), hidT_hi,
                                     ALU.subtract).then_inc(hidT_lo_made, 1)

                for k in range(3):
                    lo(k)
                hidden_of(3, 0, False)
                lo(3)
                scattered(j)
                hidT_of(0)
                ve.wait_ge(place_made, j + 2)
                picks(j + 1)
                with ve.Fori(1, BLOCKS) as b:
                    for k in range(-2, 1):
                        lo(k, b)
                    hidden_of(1, b, True)
                    for k in range(1, 4):
                        lo(k, b)
                    hidT_of(b)
                gathered(j + 1)
                lo(JOB_TILES - 2)
                lo(JOB_TILES - 1)

            ve.wait_ge(jobs_ready, 1)
            ve.memset(y_sb[:, 0:HALF], 0.0).then_inc(y_made, 1)
            ve.memset(y_sb[:, HALF:D], 0.0).then_inc(y_made, 1)
            ve.memset(place, 0.0).then_inc(place_made, 1)
            picks(0)
            gathered(0)
            nj = each_job(ve, expert)
            scattered(nj, last=True)
            ple(1, nj)
            norm(6)


_INS = ["x", "p", "rel_bias", "final_norm", "e_norm_mix", "e_w_in", "e_conv_w", "e_sinks", "e_w_out",
        "e_norm_ffn", "e_ffn_gate", "e_ffn_up", "e_ffn_down", "e_norm_ple", "e_ple_gate", "e_ple_proj",
        "o_norm_mix", "o_w_qkv", "o_w_o", "o_norm_ffn", "o_router", "o_exp_gate", "o_exp_up", "o_exp_down",
        "o_norm_ple", "o_ple_gate", "o_ple_proj"]


def kernel(**inputs):
    import concourse.bacc as _bacc
    from concourse.bass_utils import run_bass_kernel_spmd as _run

    nc = _bacc.Bacc("TRN2", target_bir_lowering=False, num_devices=1)
    arrays = {f"in_{name}": np.ascontiguousarray(inputs[name]) for name in _INS}
    consts, onehots = shape_constants()
    arrays["in_consts"], arrays["in_onehots"] = consts, onehots
    args = [nc.dram_tensor(n, a.shape, mybir.dt.from_np(a.dtype), kind="ExternalInput").ap() for n, a in arrays.items()]
    out = nc.dram_tensor("out_0", (1, SEQ, D), F32, kind="ExternalOutput").ap()
    trunk(nc, *args, out)
    r = _run(nc, [arrays], core_ids=[0])
    return r.results[0]["out_0"]
```

```python
from contextlib import ExitStack

import numpy as np

import concourse.bass as bass
from concourse import mybir

F32 = mybir.dt.float32
F32R = mybir.dt.float32r
I32 = mybir.dt.int32
ALU = mybir.AluOpType
ACT = mybir.ActivationFunctionType
AX = mybir.AxisListType.X

P = 128
SEQ, D, HEADS, BUCKETS, PLE = 256, 1024, 8, 32, 256
TT = SEQ // P
KC = D // P
EPS = 1e-6
HALF = 512
MASKED = -1e30
DIAGS = 3 * P

SC = D // 2
SWA_D, SWA_KV, SWA_WINDOW = 64, 2, 128
MOBA_D = D // HEADS
D_FF = 2816
PAIRS = D_FF // (2 * P)
EXPERTS, TOP_K, D_FFE = 8, 2, 3584
BLOCKS = D_FFE // HALF
EXTRA = 3
JOBS = EXPERTS + EXTRA

TILE = 2048
RAW, SPLIT = 6, 3
Q0_T, KV_T, CONV_T = 0, 2, 3
OUT0_T = 9
FFN_T = 13
PLE0_T = FFN_T + 3 * PAIRS
QK_T = PLE0_T + 5
V_T = QK_T + 8
OUT1_T = V_T + 4
PROJ1_T = OUT1_T + 4
MOE_T = PROJ1_T + 1
JOB_TILES = 6 * BLOCKS
GATE1_T = MOE_T
assert JOB_TILES % RAW == 0 and RAW % SPLIT == 0

C_IDENT, C_TRI, C_IOTA, C_ONES = 0, P, 2 * P, 3 * P
C_BEFORE = 4 * P
C_EIDX = C_BEFORE + EXPERTS * EXPERTS
C_END = C_EIDX + EXPERTS


def shape_constants():
    c = np.zeros((P, C_END), np.float32)
    c[:, C_IDENT:C_IDENT + P] = np.eye(P)
    c[:, C_TRI:C_TRI + P] = np.arange(P)[:, None] < np.arange(P)[None]
    c[:, C_IOTA:C_IOTA + P] = np.arange(P)
    c[:, C_ONES:C_ONES + P] = 1.0
    e = np.arange(EXPERTS)
    c[:, C_BEFORE:C_EIDX] = (e[None] < e[:, None]).reshape(-1)
    c[:, C_EIDX:C_END] = e
    dist = 2 * P - 1 - np.arange(DIAGS)
    exact = BUCKETS // 2
    far = exact + (np.log(np.maximum(dist, exact) / exact) / np.log(P / exact) * (BUCKETS - exact)).astype(int)
    bucket = np.where(dist < exact, dist, np.minimum(far, BUCKETS - 1))
    oh = np.zeros((BUCKETS + 1, 2, DIAGS), np.float32)
    for layer, reach in ((0, SWA_WINDOW), (1, SEQ)):
        valid = (dist >= 0) & (dist < reach)
        m = np.flatnonzero(valid)
        oh[bucket[m], layer, m] = 1.0
        oh[BUCKETS, layer] = np.where(valid, 0.0, MASKED)
    return c, oh.reshape(BUCKETS + 1, 2 * DIAGS)


def trunk(nc, x, p, rel_bias, final_norm, e_norm_mix, e_w_in, e_conv_w, e_sinks, e_w_out,
          e_norm_ffn, e_ffn_gate, e_ffn_up, e_ffn_down, e_norm_ple, e_ple_gate, e_ple_proj,
          o_norm_mix, o_w_qkv, o_w_o, o_norm_ffn, o_router, o_exp_gate, o_exp_up, o_exp_down,
          o_norm_ple, o_ple_gate, o_ple_proj, consts, onehots, out):
    gains = [e_norm_mix[0:1], e_norm_ffn[0:1], e_norm_ple[0:1], o_norm_mix[0:1], o_norm_ffn[0:1],
             o_norm_ple[0:1], final_norm.rearrange("(a d) -> a d", a=1)]
    diag_dram = nc.dram_tensor("diag_scratch", (2, HEADS, P, DIAGS), F32, kind="Internal").ap()

    with ExitStack() as ctx:
        def sb(name, shape, dt=F32):
            return ctx.enter_context(nc.sbuf_tensor(name, shape, dt))

        def sem(name):
            return ctx.enter_context(nc.semaphore(name))

        raw = sb("raw", [P, RAW, TILE])
        w_hi = sb("w_hi", [P, SPLIT, TILE], F32R)
        w_lo = sb("w_lo", [P, SPLIT, TILE], F32R)
        h = sb("h", [P, TT, D])
        xn = sb("xn", [P, TT, D])
        x_hi = sb("x_hi", [P, KC, SEQ], F32R)
        x_lo = sb("x_lo", [P, KC, SEQ], F32R)
        m_hi = sb("m_hi", [P, KC, SEQ], F32R)
        m_lo = sb("m_lo", [P, KC, SEQ], F32R)
        p_hi = sb("p_hi", [P, 2, 2, SEQ], F32R)
        p_lo = sb("p_lo", [P, 2, 2, SEQ], F32R)
        r_raw = sb("r_raw", [P, KC, EXPERTS])
        r_hi = sb("r_hi", [P, KC, EXPERTS], F32R)
        r_lo = sb("r_lo", [P, KC, EXPERTS], F32R)
        zeros_r = sb("zeros_r", [P, P], F32R)
        gain = sb("gain", [P, 2, D])
        cst = sb("cst", [P, C_END])
        rel = sb("rel", [BUCKETS + 1, HEADS])
        bias = sb("bias", [P, HEADS, DIAGS])
        sink = sb("sink", [P, HEADS])
        conv_w = sb("conv_w", [P, 3 * SC // P])
        ssq = sb("ssq", [P, 4, TT])
        rstd = sb("rstd", [P, TT])
        score = sb("score", [P, 2, DIAGS])
        probT = sb("probT", [P, 2, DIAGS])
        stat = sb("stat", [P, 2, 5, TT])
        diag = score[0:HEADS].rearrange("p b n -> p (b n)")
        work = sb("work", [P, 6 * D])
        proj1 = bias[:, 0:6].rearrange("p h m -> p (h m)")[:, 0:2 * D].rearrange("p (b n) -> p b n", b=4)
        oh = work[0:BUCKETS + 1, 4224:4992]
        taps = work[0:3 * SC // P, 4992:5120]
        p_raw = work[:, 5 * D:6 * D].rearrange("p (l t n) -> p l t n", l=2, t=TT)
        q0T = work[:, 0:D].rearrange("p (j t) -> p j t", j=4)
        k0T = work[:, D:D + SEQ]
        v0 = work[:, D + SEQ:D + 2 * SEQ].rearrange("p (t n) -> p t n", t=TT)
        c_sb = work[:, 1536:2048].rearrange("p (j t) -> p j t", j=2)
        cu = work[:, 2048:2048 + 4 * (SEQ + 2)].rearrange("p (j t) -> p j t", j=4)
        conv_y = work[:, 3200:3712].rearrange("p (j t) -> p j t", j=2)
        conv_a = work[:, 3712:4224].rearrange("p (j t) -> p j t", j=2)
        q1T = work[:, 0:2 * D].rearrange("p (j t) -> p j t", j=HEADS)
        k1T = work[:, 2 * D:4 * D].rearrange("p (j t) -> p j t", j=HEADS)
        v1 = work[:, 4 * D:6 * D].rearrange("p (t n) -> p t n", t=TT)
        silu = work[:, 0:HALF]
        hid = work[:, HALF:2 * HALF]
        sig = work[:, 2 * D:4 * D].rearrange("p (b n) -> p b n", b=4)
        y_sb = work[:, 2 * D:3 * D]
        pick = work[:, 3 * D:3 * D + 2 * P].rearrange("p (t s) -> p t s", t=TT)
        pick_g = work[:, 3 * D + 2 * P:3 * D + 4 * P].rearrange("p (t s) -> p t s", t=TT)
        place = work[:, 3 * D + 4 * P:3 * D + 6 * P]
        route = work[:, 4 * D:5 * D]
        hid_hi, hid_lo = m_hi[:, 0:2], m_lo[:, 0:2]
        hidT_hi = m_hi[:, 0:2].rearrange("p a (b s) -> p (a b) s", b=2)
        hidT_lo = m_lo[:, 0:2].rearrange("p a (b s) -> p (a b) s", b=2)
        jobs = sb("jobs", [P, JOBS + 1, 2, TT])
        job = sb("job", [P, 1, 2, TT])
        job_int = sb("job_int", [1, 4], I32)
        ident = cst[:, C_IDENT:C_IDENT + P]
        iota = cst[:, C_IOTA:C_IOTA + P]
        bank = [ctx.enter_context(nc.psum_tensor(f"bank{i}", [P, HALF], F32)) for i in range(8)]

        tile_loaded = [sem(f"tile_loaded{i}") for i in range(RAW)]
        hi_made, lo_made, tile_used = sem("hi_made"), sem("lo_made"), sem("tile_used")
        x_loaded, cst_loaded = sem("x_loaded"), sem("cst_loaded")
        diag_in_loaded, aux_loaded = sem("diag_in_loaded"), sem("aux_loaded")
        first_gain_loaded = sem("first_gain_loaded")
        gain_loaded = [sem("gain_loaded0"), sem("gain_loaded1")]
        diag_ready, diag_copied = sem("diag_ready"), sem("diag_copied")
        diag_stored = [sem("diag_stored0"), sem("diag_stored1")]
        bias_loaded = [sem("bias_loaded0"), sem("bias_loaded1")]
        taps_ready, taps_made = sem("taps_ready"), sem("taps_made")
        pT_ready, p_hi_made, p_lo_made = sem("pT_ready"), sem("p_hi_made"), sem("p_lo_made")
        r_hi_made, r_lo_made = sem("r_hi_made"), sem("r_lo_made")
        memsets_done = sem("memsets_done")
        h_ready, squares_made, xn_ready = sem("h_ready"), sem("squares_made"), sem("xn_ready")
        xT_ready, x_hi_made, x_lo_made = sem("xT_ready"), sem("x_hi_made"), sem("x_lo_made")
        vec_step = sem("vec_step")
        q0_made, kv0_made, c_made, b_made = sem("q0_made"), sem("kv0_made"), sem("c_made"), sem("b_made")
        conv_hi_made, conv_lo_made, conv_made = sem("conv_hi_made"), sem("conv_lo_made"), sem("conv_made")
        qkv1_made = sem("qkv1_made")
        scores_ready, negmax_ready, exp_made = sem("scores_ready"), sem("negmax_ready"), sem("exp_made")
        probs_ready, probT_ready, probT_made = sem("probs_ready"), sem("probT_ready"), sem("probT_made")
        oT_ready, oT_hi_made, oT_lo_made = sem("oT_ready"), sem("oT_hi_made"), sem("oT_lo_made")
        silu_made, hid_made = sem("silu_made"), sem("hid_made")
        hid_hi_made, hid_lo_made = sem("hid_hi_made"), sem("hid_lo_made")
        gated_made = sem("gated_made")
        sig_made, proj_made = sem("sig_made"), sem("proj_made")
        logits_ready, route_exp_ready, route_exp_made = sem("logits_ready"), sem("route_exp_ready"), sem("route_exp_made")
        chosen_ready, ranks_ready, jobs_ready = sem("chosen_ready"), sem("ranks_ready"), sem("jobs_ready")
        pick_made, gather_ready, xg_hi_made, xg_lo_made = sem("pick_made"), sem("gather_ready"), sem("xg_hi_made"), sem("xg_lo_made")
        job_read = sem("job_read")
        pickT_ready, place_made = sem("pickT_ready"), sem("place_made")
        e_silu_made, e_hid_made = sem("e_silu_made"), sem("e_hid_made")
        hidT_ready, hidT_hi_made, hidT_lo_made = sem("hidT_ready"), sem("hidT_hi_made"), sem("hidT_lo_made")
        y_made, scatter_ready, scatter_added = sem("y_made"), sem("scatter_ready"), sem("scatter_added")
        out_stored = sem("out_stored")

        block = ctx.enter_context(nc.Block())

        def job_count(eng):
            eng.wait_ge(jobs_ready, 1)
            return eng.value_load(job_int[0:1, 3:4], min_val=EXPERTS, max_val=JOBS)

        def each_job(eng, body):
            with eng.Fori(0, EXPERTS) as j:
                body(j)
            n = job_count(eng)
            with eng.If(n > EXPERTS):
                with eng.Fori(EXPERTS, n) as j:
                    body(j)
            return n

        def by_group(tile, regrouped):
            if regrouped:
                v = tile.rearrange("p (k j g d) -> p g k j d", k=4, j=4, g=SWA_KV)
            else:
                v = tile.rearrange("p (k g j d) -> p g k j d", k=4, g=SWA_KV, j=4)
            return [v[:, g] for g in range(SWA_KV)]

        def head_out(layer, hd, dst):
            if layer == 0:
                lanes = slice(SWA_D * (hd % 2), SWA_D * (hd % 2) + SWA_D)
                return dst[lanes, 4 + hd // 2, :], bank[7][lanes, 0:SEQ]
            return dst[:, hd, :], bank[7][:, 0:SEQ]

        def norm_groups(i):
            first = 0 if i in (0, 3) else 4
            return [(g, g // 2, g % 2, bank[first + g]) for g in range(4)]

        @block.sync
        def _(sp):
            def load(n, src, slot=None):
                if slot is not None or n >= RAW:
                    sp.wait_ge(lo_made, n - RAW + 1)
                slot = n % RAW if slot is None else slot
                sp.dma_start(raw[:, slot].rearrange("p (c n) -> p c n", c=src.shape[1]), src)\
                  .then_inc(tile_loaded[slot], 16)

            def cols_of(w, c0, n, k0=0, k=KC):
                return w[k0 * P:(k0 + k) * P, c0:c0 + n].rearrange("(c p) n -> p c n", p=P)

            def rows_of(w, pair):
                return w[pair * 2 * P:(pair + 1) * 2 * P, :].rearrange("(c p) n -> p c n", p=P)

            for t in range(TT):
                sp.dma_start(h[:, t], x[0, t * P:(t + 1) * P, :]).then_inc(x_loaded, 16)
            w_in = e_w_in[0]
            for i in range(2):
                load(Q0_T + i, cols_of(w_in, 3 * SC, HALF, 4 * i, 4))
            load(KV_T, cols_of(w_in, 4 * SC, 2 * P))
            for i in range(2):
                for part, first in enumerate((SC, 2 * SC, 0)):
                    load(CONV_T + 3 * i + part, cols_of(w_in, first + i * 2 * P, 2 * P))
            for i in range(4):
                load(OUT0_T + i, rows_of(e_w_out[0], i))
            load(FFN_T, cols_of(e_ffn_gate[0], 0, 2 * P))
            load(FFN_T + 1, cols_of(e_ffn_up[0], 0, 2 * P))
            gate_v = e_ffn_gate[0].rearrange("(c p) (i n) -> i p c n", p=P, n=2 * P)
            up_v = e_ffn_up[0].rearrange("(c p) (i n) -> i p c n", p=P, n=2 * P)
            down_v = e_ffn_down[0].rearrange("(i c p) n -> i p c n", p=P, c=2)
            with sp.Fori(0, (PAIRS - 1) // 2) as r:
                for u in range(2):
                    i = 1 + u + 2 * r
                    for part, src in enumerate((gate_v[i], up_v[i], down_v[i - 1])):
                        n = FFN_T + 2 + 3 * u + part
                        load(n + 6 * r, src, slot=n % RAW)
            load(PLE0_T - 1, down_v[PAIRS - 1])
            load(PLE0_T, rows_of(e_ple_proj[0], 0))
            for i in range(4):
                load(PLE0_T + 1 + i, rows_of(e_ple_gate[0], i))
            for i in range(12):
                load(QK_T + i, cols_of(o_w_qkv[0], i * 2 * P, 2 * P))
            for i in range(4):
                load(OUT1_T + i, rows_of(o_w_o[0], i))
            load(PROJ1_T, rows_of(o_ple_proj[0], 0))
            eg = o_exp_gate[0].rearrange("e (c p) (b n) -> e b p c n", p=P, n=HALF)
            eu = o_exp_up[0].rearrange("e (c p) (b n) -> e b p c n", p=P, n=HALF)
            ed = o_exp_down[0].rearrange("e (i c p) n -> e i p c n", p=P, c=2)

            def expert(j, e):
                base = MOE_T + JOB_TILES * j

                halves = tuple(enumerate(((eg, 0), (eg, 4), (eu, 0), (eu, 4))))
                for i, (w, k) in halves:
                    load(base + i, w[e, 0, :, k:k + 4], slot=(MOE_T + i) % RAW)
                with sp.Fori(1, BLOCKS) as b:
                    for i, (w, k) in halves:
                        load(base + 6 * b + (i - 2), w[e, b, :, k:k + 4], slot=(MOE_T + 4 + i) % RAW)
                    for i in range(2):
                        load(base + 6 * b + (i + 2), ed[e, 2 * b + (i - 2)], slot=(MOE_T + 8 + i) % RAW)
                for i in range(2):
                    load(base + (JOB_TILES - 2 + i), ed[e, 2 * BLOCKS - 2 + i], slot=(MOE_T + 4 + i) % RAW)

            with sp.Fori(0, EXPERTS) as j:
                expert(j, j)
            nj = job_count(sp)
            with sp.If(nj > EXPERTS):
                with sp.Fori(EXPERTS, nj) as j:
                    expert(j, sp.value_load(job_int[0:1, bass.ds(j - EXPERTS, 1)], min_val=0, max_val=EXPERTS - 1))
            for i in range(4):
                load(JOB_TILES * nj + (GATE1_T + i), rows_of(o_ple_gate[0], i), slot=(GATE1_T + i) % RAW)
            for t in range(TT):
                sp.wait_ge(xn_ready, TT * 6 + t + 1)
                sp.dma_start(out[0, t * P:(t + 1) * P, :], xn[:, t]).then_inc(out_stored, 16)
            sp.wait_ge(out_stored, 16 * TT)

        @block.gpsimd
        def _(pool):
            def load_gain(i):
                pool.dma_start(gain[:, i % 2], bass.AP(tensor=gains[i].tensor, offset=gains[i].offset, ap=[[0, P], [1, D]]))\
                    .then_inc(gain_loaded[i % 2], 16)

            pool.dma_start(oh, onehots).then_inc(diag_in_loaded, 16)
            pool.dma_start(rel[0:BUCKETS, :], rel_bias).then_inc(diag_in_loaded, 16)
            pool.dma_start(rel[BUCKETS:BUCKETS + 1, :], consts[0:1, C_ONES:C_ONES + HEADS]).then_inc(diag_in_loaded, 16)
            pool.dma_start(sink[:, :], bass.AP(tensor=e_sinks.tensor, offset=0, ap=[[0, P], [1, HEADS]])).then_inc(aux_loaded, 16)
            pool.dma_start(p_raw[:, 0], p[0, 0].rearrange("(t q) n -> q t n", q=P)).then_inc(aux_loaded, 16)
            pool.dma_start(p_raw[:, 1], p[1, 0].rearrange("(t q) n -> q t n", q=P)).then_inc(aux_loaded, 16)
            pool.dma_start(taps, e_conv_w[0].rearrange("k (c q) -> (k c) q", q=P)).then_inc(aux_loaded, 16)
            pool.dma_start(r_raw[:, :, :], o_router[0].rearrange("(c q) e -> q c e", q=P)).then_inc(aux_loaded, 16)
            load_gain(1)
            pool.wait_ge(diag_copied, 2)
            def store_diagonals(layer):
                pool.dma_start(diag_dram[layer], diag[:, layer * DIAGS:(layer + 1) * DIAGS].unsqueeze(1)
                               .broadcast_to((HEADS, P, DIAGS))).then_inc(diag_stored[layer], 16)

            def load_bias(layer):
                pool.wait_ge(diag_stored[layer], 16)
                for first, col, n in ((P, 0, P), (0, P, 2 * P)):
                    pool.dma_start(bias[:, :, col:col + n],
                                   bass.AP(tensor=diag_dram.tensor, offset=layer * HEADS * P * DIAGS + P - 1 + first,
                                           ap=[[DIAGS - 1, P], [P * DIAGS, HEADS], [1, n]])).then_inc(bias_loaded[layer], 16)

            store_diagonals(0)
            load_bias(0)
            store_diagonals(1)
            pool.wait_ge(negmax_ready, HEADS)
            load_bias(1)
            for i in range(2, 7):
                pool.wait_ge(xn_ready, TT * (i - 1))
                load_gain(i)

        @block.scalar
        def _(act):
            act.dma_start(gain[:, 0], bass.AP(tensor=gains[0].tensor, offset=gains[0].offset, ap=[[0, P], [1, D]]))\
               .then_inc(first_gain_loaded, 16)
            act.dma_start(cst[:, :], consts).then_inc(cst_loaded, 16)

            def split(n, slot=None, rounds=None):
                slot = n % RAW if slot is None else slot
                rounds = n // RAW if rounds is None else rounds
                act.wait_ge(tile_loaded[slot], 16 * rounds + 16)
                act.activation(w_hi[:, slot % SPLIT], raw[:, slot], ACT.Copy).then_inc(hi_made, 1)

            def step(n, slot=None, rounds=None):
                act.wait_ge(tile_used, n + 1)
                split(n + SPLIT if slot is None else None, None if slot is None else (slot + SPLIT) % RAW, rounds)

            def norm(i, between):
                for t in range(TT):
                    act.wait_ge(*((h_ready, TT * (i - 1) + t + 1) if i else (x_loaded, 32)))
                    act.activation(xn[:, t], h[:, t], ACT.Square, accum_out=ssq[:, 0, t:t + 1]).then_inc(squares_made, 1)
                if i == 6:
                    return
                between()
                for g, half, t, b in norm_groups(i):
                    act.wait_ge(xT_ready, 4 * i + g + 1)
                    act.activation(x_hi[:, 4 * half:4 * half + 4, t * P:(t + 1) * P],
                                   b[:, :].rearrange("p (c t) -> p c t", c=4), ACT.Copy).then_inc(x_hi_made, 1)

            def attention(layer, extra):
                first = layer * HEADS

                def exponentials(hd):
                    a = first + hd
                    s, st = score[:, a % 2], stat[:, a % 2]
                    act.wait_ge(negmax_ready, a + 1)
                    act.activation(s[:, 0:P], s[:, 0:P], ACT.Exp, bias=st[:, 1, 0:1], accum_out=st[:, 2, 0:1])
                    if layer == 0:
                        act.activation(st[:, 3, :], st[:, 1, :], ACT.Exp, bias=sink[:, hd:hd + 1])
                    act.activation(s[:, P:DIAGS], s[:, P:DIAGS], ACT.Exp, bias=st[:, 1, 1:2],
                                   accum_out=st[:, 2, 1:2]).then_inc(exp_made, 1)

                def output(hd):
                    act.wait_ge(oT_ready, first + hd + 1)
                    dst, src = head_out(layer, hd, m_hi)
                    act.activation(dst, src, ACT.Copy).then_inc(oT_hi_made, 1)

                exponentials(0)
                for hd in range(HEADS):
                    if hd + 1 < HEADS:
                        exponentials(hd + 1)
                    extra(hd)
                    if hd:
                        output(hd - 1)
                    act.wait_ge(probT_ready, first + hd + 1)
                    act.activation(probT[:, hd % 2], bank[6][:, 0:DIAGS], ACT.Copy).then_inc(probT_made, 1)
                output(HEADS - 1)

            def split_q():
                for n in range(2):
                    act.wait_ge(tile_loaded[n], 16)
                    for dst, src in zip(by_group(w_hi[:, n], True), by_group(raw[:, n], False)):
                        ins = act.activation(dst, src, ACT.Copy)
                    ins.then_inc(hi_made, 1)

            norm(0, split_q)
            split(KV_T)
            for l in range(2):
                act.wait_ge(diag_ready, l + 1)
                act.activation(diag[:, l * DIAGS:(l + 1) * DIAGS], bank[4 + l][0:HEADS, 0:DIAGS], ACT.Copy).then_inc(diag_copied, 1)
            step(Q0_T)
            step(Q0_T + 1)
            for j in range(4):
                act.activation(q0T[:, j], bank[j][:, 0:SEQ], ACT.Copy).then_inc(q0_made, 1)
            act.wait_ge(taps_ready, 1)
            act.activation(conv_w[:, :], bank[6][:, 0:12], ACT.Copy).then_inc(taps_made, 1)
            for l in range(2):
                act.wait_ge(pT_ready, l + 1)
                act.activation(p_hi[:, l], bank[6 + l][:, :].rearrange("p (c t) -> p c t", c=2), ACT.Copy).then_inc(p_hi_made, 1)
            act.activation(r_hi[:, :, :], r_raw[:, :, :], ACT.Copy).then_inc(r_hi_made, 1)
            step(KV_T)
            act.activation(k0T, bank[4][:, 0:SEQ], ACT.Copy).then_inc(kv0_made, 1)
            act.activation(v0, bank[5][:, 0:SEQ].rearrange("p (t n) -> p t n", t=TT), ACT.Copy).then_inc(kv0_made, 1)

            def beside(hd):
                if hd < 4:
                    conv_tile(hd + 2)
                elif hd % 2:
                    step(OUT0_T + hd // 2 - 2)

            def conv_tile(hd):
                step(CONV_T + hd)
                i, part = hd // 3, hd % 3
                if part == 0:
                    if i:
                        act.wait_ge(conv_made, 1)
                    act.activation(c_sb, bank[(3 * i) % 4][:, :].rearrange("p (j t) -> p j t", j=2), ACT.Copy).then_inc(c_made, 1)
                if part == 2:
                    act.wait_ge(conv_made, i + 1)
                    act.activation(m_hi[:, 2 * i:2 * i + 2], conv_a, ACT.Copy).then_inc(conv_hi_made, 1)

            conv_tile(0)
            conv_tile(1)
            attention(0, beside)
            step(OUT0_T + 2)
            norm(1, lambda: step(OUT0_T + 3))

            def ffn_up(n, i, slot, rounds):
                step(n, slot, rounds[0])
                if not isinstance(i, int):
                    act.wait_ge(hid_made, i)
                act.activation(silu, bank[0][:, :], ACT.Silu).then_inc(silu_made, 1)
                step(n + 1, (slot + 1) % RAW, rounds[1])

            def ffn_hidden(i):
                act.wait_ge(hid_made, i + 1)
                act.activation(hid_hi, hid.rearrange("p (j t) -> p j t", j=2), ACT.Copy).then_inc(hid_hi_made, 1)

            def rounds(n):
                return (n + SPLIT) // RAW

            ffn_up(FFN_T, 0, FFN_T % RAW, (rounds(FFN_T), rounds(FFN_T + 1)))
            ffn_hidden(0)
            with act.Fori(0, (PAIRS - 1) // 2) as r:
                for u in range(2):
                    n = FFN_T + 2 + 3 * u
                    ffn_up(n + 6 * r, 1 + u + 2 * r, n % RAW, (rounds(n) + r, rounds(n + 1) + r))
                    step(n + 2 + 6 * r, (n + 2) % RAW, rounds(n + 2) + r)
                    ffn_hidden(1 + u + 2 * r)
            def sigmoids():
                for b in range(4):
                    act.activation(sig[:, b], bank[4 + b][:, :], ACT.Sigmoid).then_inc(sig_made, 1)

            norm(2, lambda: step(PLE0_T - 1))
            for i in range(4):
                step(PLE0_T + i)
            act.wait_ge(tile_used, PLE0_T + 5)
            sigmoids()
            norm(3, lambda: split(PLE0_T + 4 + SPLIT))
            for i in range(8):
                step(QK_T + i)
                dst = (q1T if i < 4 else k1T)[:, 2 * (i % 4):2 * (i % 4) + 2]
                act.activation(dst, bank[i % 4][:, :].rearrange("p (j t) -> p j t", j=2), ACT.Copy).then_inc(qkv1_made, 1)

            def beside1(hd):
                i = hd
                if hd >= 4:
                    if hd != 6:
                        step(OUT1_T + (0, 1, None, 2)[hd - 4])
                    return
                step(V_T + i)
                act.activation(v1[:, :, i * 2 * P:(i + 1) * 2 * P],
                               bank[i][:, :].rearrange("p (t n) -> p t n", t=TT), ACT.Copy).then_inc(qkv1_made, 1)

            attention(1, beside1)
            norm(4, lambda: step(OUT1_T + 3))
            act.wait_ge(route_exp_ready, 1)
            for t in range(TT):
                act.activation(route[:, 32 + 8 * t:40 + 8 * t], route[:, 8 * t:8 * t + 8], ACT.Exp,
                               bias=route[:, 24 + t:25 + t]).then_inc(route_exp_made, 1)
            step(PROJ1_T)
            for b in range(4):
                act.activation(proj1[:, b], bank[b][:, :], ACT.Copy).then_inc(proj_made, 1)

            def gathered(j):
                act.wait_ge(gather_ready, j + 1)
                for half in range(2):
                    act.activation(x_hi[:, 4 * half:4 * half + 4, 0:P],
                                   bank[4 + half][:, :].rearrange("p (c t) -> p c t", c=4), ACT.Copy).then_inc(xg_hi_made, 1)

            def expert(j):
                done = JOB_TILES * j

                def st(k, b=None):
                    n = MOE_T + k
                    r = (n + SPLIT) // RAW + (JOB_TILES // RAW) * j
                    if b is None:
                        step(n + done, n % RAW, r)
                    else:
                        step(n + done + 6 * b, n % RAW, r + b)

                def silu_of():
                    act.activation(silu, bank[0][:, :], ACT.Silu).then_inc(e_silu_made, 1)

                def hidT_of(b):
                    act.wait_ge(hidT_ready, BLOCKS * j + b + 1)
                    act.activation(hidT_hi, bank[2][:, :].rearrange("p (c t) -> p c t", c=4), ACT.Copy).then_inc(hidT_hi_made, 1)

                st(0)
                st(1)
                silu_of()
                st(2)
                st(3)
                hidT_of(0)
                act.wait_ge(pickT_ready, j + 1)
                act.activation(place, bank[3][:, 0:2 * P], ACT.Copy).then_inc(place_made, 1)
                with act.Fori(1, BLOCKS) as b:
                    st(-2, b)
                    st(-1, b)
                    silu_of()
                    for k in range(4):
                        st(k, b)
                    hidT_of(b)
                gathered(j + 1)
                st(JOB_TILES - 2)
                st(JOB_TILES - 1)
                for half in range(2):
                    act.activation(y_sb[:, half * HALF:(half + 1) * HALF], bank[6 + half][:, :], ACT.Copy).then_inc(y_made, 1)

            gathered(0)
            nj = each_job(act, expert)
            norm(5, lambda: None)
            n = GATE1_T + JOB_TILES * nj
            step(n, GATE1_T % RAW, (GATE1_T + SPLIT) // RAW + (JOB_TILES // RAW) * nj)
            act.wait_ge(tile_used, n + 4)
            sigmoids()
            norm(6, None)

        PASSES = ((0, 1), (1, 0), (0, 0))

        @block.tensor
        def _(pe):
            def three(dst, stat_hl, mov_hl, start, stop, tick=None):
                for i, (a, b) in enumerate(PASSES):
                    mm = pe.matmul(dst, stat_hl[a], mov_hl[b], start=start and i == 0, stop=stop and i == 2)
                if tick is not None:
                    mm.then_inc(tick, 1)

            def w_tile(slot, n):
                return [w[:, slot % SPLIT].rearrange("p (c n) -> p c n", n=n) for w in (w_hi, w_lo)]

            def both(pair, *at):
                return [t[at] for t in pair]

            XHL, MHL = (x_hi, x_lo), (m_hi, m_lo)
            ALL = slice(None)

            def wait_tile(n):
                pe.wait_ge(lo_made, n + 1)

            def up_tile(n, b, slot=None):
                wait_tile(n)
                w = w_tile(n if slot is None else slot, 2 * P)
                for f in range(2):
                    for k in range(KC):
                        three(bank[b][:, f * SEQ:(f + 1) * SEQ], both(w, ALL, k, slice(f * P, (f + 1) * P)),
                              both(XHL, ALL, k), k == 0, k == KC - 1, tile_used if (f, k) == (1, KC - 1) else None)

            def token_tile(n, b, first, cols, tick):
                w = w_tile(n, 2 * P)
                for t in range(TT):
                    for k in range(KC):
                        three(bank[b][:, t * cols:(t + 1) * cols], both(XHL, ALL, k, slice(t * P, (t + 1) * P)),
                              both(w, ALL, k, slice(first, first + cols)), k == 0, k == KC - 1,
                              tick if (t, k) == (TT - 1, KC - 1) else None)

            def down_tile(n, a, c0, b0, start, stop, slot=None):
                wait_tile(n)
                w = w_tile(n if slot is None else slot, D)
                for kk in range(2):
                    for t in range(TT):
                        for half in range(2):
                            three(bank[b0 + 2 * t + half][:, :], both(a, ALL, c0 + kk, slice(t * P, (t + 1) * P)),
                                  both(w, ALL, kk, slice(half * HALF, (half + 1) * HALF)),
                                  start and kk == 0, stop and kk == 1,
                                  tile_used if (kk, t, half) == (1, TT - 1, 1) else None)

            def norm(i):
                for g, half, t, b in norm_groups(i):
                    pe.wait_ge(xn_ready, TT * i + t + 1)
                    for c in range(4):
                        at = (4 * half + c) * P
                        mm = pe.transpose(b[:, c * P:(c + 1) * P], xn[:, t, at:at + P], ident)
                    mm.then_inc(xT_ready, 1)

            def attention(layer, qT_of, kT_of, v_of, extra):
                def scores(hd):
                    a = layer * HEADS + hd
                    b = bank[4 + a % 2]
                    if hd >= 2:
                        pe.wait_ge(negmax_ready, a - 1)
                    q, k = qT_of(hd), kT_of(hd)
                    pe.matmul(b[:, 0:P], q[:, 0:P], k[:, 0:P], start=True, stop=True)
                    pe.matmul(b[:, P:DIAGS], q[:, P:SEQ], k, start=True, stop=True).then_inc(scores_ready, 1)

                def output(hd):
                    a = layer * HEADS + hd
                    if layer == 1:
                        pe.wait_ge(qkv1_made, 9 + hd // 2)
                    pe.wait_ge(probT_made, a + 1)
                    if hd:
                        pe.wait_ge(oT_lo_made, a)
                    o = head_out(layer, hd, m_hi)[1]
                    v, pT = v_of(hd), probT[:, hd % 2]
                    pe.matmul(o[:, 0:P], v[0], pT[:, 0:P], start=True, stop=True)
                    pe.matmul(o[:, P:SEQ], v[0], pT[:, P:2 * P], start=True, stop=False)
                    pe.matmul(o[:, P:SEQ], v[1], pT[:, 2 * P:DIAGS], start=False, stop=True).then_inc(oT_ready, 1)

                scores(0)
                scores(1)
                for hd in range(HEADS):
                    a = layer * HEADS + hd
                    extra(hd)
                    if hd:
                        output(hd - 1)
                    pe.wait_ge(probs_ready, a + 1)
                    for c in range(3):
                        mm = pe.transpose(bank[6][:, c * P:(c + 1) * P], score[:, a % 2, c * P:(c + 1) * P], ident)
                    mm.then_inc(probT_ready, 1)
                    if hd + 2 < HEADS:
                        scores(hd + 2)
                output(HEADS - 1)

            pe.wait_ge(cst_loaded, 16)
            norm(0)
            pe.wait_ge(diag_in_loaded, 48)
            for l in range(2):
                pe.matmul(bank[4 + l][0:HEADS, 0:DIAGS], rel[:, :], oh[:, l * DIAGS:(l + 1) * DIAGS],
                          start=True, stop=True).then_inc(diag_ready, 1)
            pe.wait_ge(x_lo_made, 4)
            for i in range(2):
                wait_tile(Q0_T + i)
                w = w_tile(Q0_T + i, HALF)
                for j in range(4):
                    for k in range(4):
                        three(bank[j][:, 0:SEQ], both(w, ALL, k, slice(j * P, (j + 1) * P)), both(XHL, ALL, 4 * i + k), (i, k) == (0, 0), (i, k) == (1, 3),
                              tile_used if (j, k) == (3, 3) else None)
            pe.wait_ge(aux_loaded, 80)
            pe.transpose(bank[6][:, 0:12], taps, cst[0:12, C_IDENT:C_IDENT + 12]).then_inc(taps_ready, 1)
            pe.wait_ge(taps_made, 1)
            for l in range(2):
                for c in range(2):
                    for t in range(TT):
                        mm = pe.transpose(bank[6 + l][:, c * SEQ + t * P:c * SEQ + (t + 1) * P],
                                          p_raw[:, l, t, c * P:(c + 1) * P], ident)
                mm.then_inc(pT_ready, 1)
            wait_tile(KV_T)
            w = w_tile(KV_T, 2 * P)
            pe.wait_ge(diag_copied, 2)
            for k in range(KC):
                three(bank[4][:, 0:SEQ], both(w, ALL, k, slice(0, P)), both(XHL, ALL, k), k == 0, k == KC - 1)
            token_tile(KV_T, 5, P, P, tile_used)
            pe.wait_ge(kv0_made, 2)
            pe.wait_ge(q0_made, 4)

            def group(hd):
                return slice(SWA_D * (hd // 4), SWA_D * (hd // 4) + SWA_D)

            def out_tile(i):
                if i == 0:
                    pe.wait_ge(conv_lo_made, 2)
                if i >= 2:
                    pe.wait_ge(oT_lo_made, 4 * i - 4)
                down_tile(OUT0_T + i, MHL, 2 * i, 0, i == 0, i == 3)

            def beside(hd):
                if hd < 4:
                    conv_tile(hd + 2)
                elif hd % 2:
                    out_tile(hd // 2 - 2)

            def conv_tile(hd):
                if hd == 4:
                    pe.wait_ge(c_made, 1)
                if hd == 5:
                    pe.wait_ge(conv_made, 1)
                up_tile(CONV_T + hd, hd % 4)

            pe.wait_ge(p_lo_made, 2)
            conv_tile(0)
            conv_tile(1)
            attention(0, lambda hd: q0T[group(hd), hd % 4], lambda hd: k0T[group(hd)],
                      lambda hd: [v0[:, t, group(hd)] for t in range(TT)], beside)
            out_tile(2)
            out_tile(3)
            norm(1)
            HHL = (hid_hi, hid_lo)
            pe.wait_ge(x_lo_made, 8)
            up_tile(FFN_T, 0)
            up_tile(FFN_T + 1, 1)
            pe.wait_ge(h_ready, TT)
            pe.wait_ge(memsets_done, 2)
            for b in range(4, 8):
                for q in range(4):
                    pe.matmul(bank[b][:, q * P:(q + 1) * P], zeros_r[:, :], zeros_r[:, :], start=q == 0, stop=False,
                              skip_group_check=True)

            def acc_down(n, a, slot, stop):
                wait_tile(n)
                w = w_tile(slot, D)
                for kk in range(2):
                    for t in range(TT):
                        for half in range(2):
                            for i, (s, m) in enumerate(PASSES):
                                mm = pe.matmul(bank[4 + 2 * t + half][:, :], a[s][:, kk, t * P:(t + 1) * P],
                                               w[m][:, kk, half * HALF:(half + 1) * HALF], start=False,
                                               stop=stop and (kk, i) == (1, 2), skip_group_check=True)
                mm.then_inc(tile_used, 1)

            with pe.Fori(0, (PAIRS - 1) // 2) as r:
                for u in range(2):
                    n = FFN_T + 2 + 3 * u
                    pe.wait_ge(silu_made, 2 * r + (1 + u))
                    up_tile(n + 6 * r, 0, n)
                    pe.wait_ge(hid_made, 2 * r + (1 + u))
                    up_tile(n + 1 + 6 * r, 1, n + 1)
                    pe.wait_ge(hid_lo_made, 2 * r + (1 + u))
                    acc_down(n + 2 + 6 * r, HHL, n + 2, False)
            pe.wait_ge(hid_lo_made, PAIRS)
            acc_down(PLE0_T - 1, HHL, PLE0_T - 1, True)

            def gate(i, n, at):
                norm(i)
                pe.wait_ge(x_lo_made, 4 * i + 4)
                for g in range(4):
                    down_tile(n + g, XHL, 2 * g, 4, g == 0, g == 3, at + g)

            down_tile(PLE0_T, (p_hi[:, 0], p_lo[:, 0]), 0, 0, True, True)
            gate(2, PLE0_T + 1, PLE0_T + 1)
            norm(3)
            pe.wait_ge(x_lo_made, 16)
            for i in range(8):
                if i >= 4:
                    pe.wait_ge(qkv1_made, i - 3)
                up_tile(QK_T + i, i % 4)
            pe.wait_ge(qkv1_made, 8)

            def out_tile(i):
                if i == 0:
                    pe.wait_ge(qkv1_made, 12)
                pe.wait_ge(oT_lo_made, HEADS + 2 * i + 2)
                down_tile(OUT1_T + i, MHL, 2 * i, 0, i == 0, i == 3)

            def beside1(hd):
                if hd < 4:
                    wait_tile(V_T + hd)
                    token_tile(V_T + hd, hd, 0, 2 * P, tile_used)
                elif hd != 6:
                    out_tile((0, 1, None, 2)[hd - 4])

            attention(1, lambda hd: q1T[:, hd], lambda hd: k1T[:, hd],
                      lambda hd: [v1[:, t, hd * P:(hd + 1) * P] for t in range(TT)], beside1)
            out_tile(3)
            norm(4)
            pe.wait_ge(x_lo_made, 20)
            pe.wait_ge(r_lo_made, 1)
            for t in range(TT):
                for k in range(KC):
                    three(bank[4][:, t * EXPERTS:(t + 1) * EXPERTS], both(XHL, ALL, k, slice(t * P, (t + 1) * P)),
                          (r_hi[:, k], r_lo[:, k]), k == 0, k == KC - 1, logits_ready if (t, k) == (1, KC - 1) else None)
            down_tile(PROJ1_T, (p_hi[:, 1], p_lo[:, 1]), 0, 0, True, True)
            pe.wait_ge(chosen_ready, 1)
            tri, ones = cst[:, C_TRI:C_TRI + P], cst[:, C_ONES:C_ONES + P]
            chosen = [route[:, 64 + 8 * t:72 + 8 * t] for t in range(TT)]
            pe.matmul(bank[5][:, 0:8], tri, chosen[0], start=True, stop=True)
            pe.matmul(bank[5][:, 8:16], tri, chosen[1], start=True, stop=False)
            pe.matmul(bank[5][:, 8:16], ones, chosen[0], start=False, stop=True)
            pe.matmul(bank[5][:, 16:24], ones, chosen[0], start=True, stop=False)
            pe.matmul(bank[5][:, 16:24], ones, chosen[1], start=False, stop=True).then_inc(ranks_ready, 1)

            def gather(j):
                pe.wait_ge(pick_made, j + 1)
                for c in range(KC):
                    for t in range(TT):
                        mm = pe.matmul(bank[4 + c // 4][:, (c % 4) * P:(c % 4 + 1) * P], xn[:, t, c * P:(c + 1) * P],
                                       pick[:, t], start=t == 0, stop=t == TT - 1)
                mm.then_inc(gather_ready, 1)

            def scatter(j):
                pe.wait_ge(y_made, 2 * j + 2)
                pe.wait_ge(place_made, j + 1)
                for q in range(4):
                    pe.matmul(bank[2 + q][:, :], place[:, (q // 2) * P:(q // 2 + 1) * P],
                              y_sb[:, (q % 2) * HALF:(q % 2 + 1) * HALF], start=True, stop=True).then_inc(scatter_ready, 1)

            def expert(j):
                def up(k, b=None):
                    for i in range(4):
                        n = MOE_T + k + i
                        wait_tile(n + JOB_TILES * j if b is None else n + JOB_TILES * j + 6 * b)
                        w = w_tile(n, HALF)
                        for kk in range(4):
                            three(bank[i // 2][:, :], both(XHL, ALL, 4 * (i % 2) + kk, slice(0, P)), both(w, ALL, kk),
                                  (i % 2, kk) == (0, 0), (i % 2, kk) == (1, 3), tile_used if kk == 3 else None)

                def down(k, b, prev, stop):
                    pe.wait_ge(hidT_lo_made, BLOCKS * j + prev + 1)
                    for i in range(2):
                        n = MOE_T + k + i
                        wait_tile(n + JOB_TILES * j if b is None else n + JOB_TILES * j + 6 * b)
                        w = w_tile(n, D)
                        for kk in range(2):
                            for half in range(2):
                                for q, (s, m) in enumerate(PASSES):
                                    mm = pe.matmul(bank[6 + half][:, :], (hidT_hi, hidT_lo)[s][:, 2 * i + kk, :],
                                                   w[m][:, kk, half * HALF:(half + 1) * HALF], start=False,
                                                   stop=stop and (i, kk, q) == (1, 1, 2), skip_group_check=True)
                        mm.then_inc(tile_used, 1)

                def turn(b):
                    pe.wait_ge(e_hid_made, BLOCKS * j + b + 1)
                    for c in range(4):
                        mm = pe.transpose(bank[2][:, c * P:(c + 1) * P], hid[:, c * P:(c + 1) * P], ident)
                    mm.then_inc(hidT_ready, 1)

                pe.wait_ge(xg_lo_made, 2 * j + 2)
                up(0)
                scatter(j)
                for half in range(2):
                    for q in range(4):
                        pe.matmul(bank[6 + half][:, q * P:(q + 1) * P], zeros_r[:, :], zeros_r[:, :], start=q == 0,
                                  stop=False, skip_group_check=True)
                pe.wait_ge(scatter_added, 4 * j + 2)
                turn(0)
                for t in range(TT):
                    mm = pe.transpose(bank[3][:, t * P:(t + 1) * P], pick_g[:, t], ident)
                mm.then_inc(pickT_ready, 1)
                with pe.Fori(1, BLOCKS) as b:
                    up(-2, b)
                    down(2, b, b - 1, False)
                    turn(b)
                pe.wait_ge(scatter_added, 4 * j + 4)
                gather(j + 1)
                down(JOB_TILES - 2, None, BLOCKS - 1, True)

            gather(0)
            pe.wait_ge(proj_made, 4)
            nj = each_job(pe, expert)
            pe.wait_ge(xg_lo_made, 2 * nj + 2)
            scatter(nj)
            gate(5, GATE1_T + JOB_TILES * nj, GATE1_T)

        @block.vector
        def _(ve):
            steps = [0]

            def link(ins):
                ins.then_inc(vec_step, 1)
                steps[0] += 1
                ve.wait_ge(vec_step, steps[0])

            def split(n, slot=None):
                slot = n % RAW if slot is None else slot % RAW
                ve.wait_ge(hi_made, n + 1)
                ve.tensor_tensor(w_lo[:, slot % SPLIT], raw[:, slot], w_hi[:, slot % SPLIT], ALU.subtract).then_inc(lo_made, 1)

            def norm(i, between=None):
                v, a, b, y = ssq[:, 0], ssq[:, 1], ssq[:, 2], rstd[:, :]
                ve.wait_ge(squares_made, TT * i + 2)
                link(ve.tensor_scalar(v, v, 1.0 / D, EPS, ALU.mult, ALU.add))
                link(ve.tensor_scalar(y.bitcast(I32), v.bitcast(I32), 1, None, ALU.logical_shift_right))
                link(ve.tensor_scalar(y.bitcast(I32), y.bitcast(I32), -1.0, float(0x5F3759DF), ALU.mult, ALU.add))
                for _ in range(3):
                    link(ve.tensor_tensor(a, y, y, ALU.mult))
                    link(ve.scalar_tensor_tensor(out=b, in0=a, scalar=-0.5, in1=v, op0=ALU.mult, op1=ALU.mult))
                    link(ve.scalar_tensor_tensor(out=y, in0=b, scalar=1.5, in1=y, op0=ALU.add, op1=ALU.mult))
                ve.wait_ge(*((gain_loaded[i % 2], 16 * ((i + 1) // 2)) if i else (first_gain_loaded, 16)))
                for t in range(TT):
                    ve.scalar_tensor_tensor(out=xn[:, t], in0=h[:, t], scalar=rstd[:, t:t + 1], in1=gain[:, i % 2],
                                            op0=ALU.mult, op1=ALU.mult).then_inc(xn_ready, 1)
                if i == 6:
                    return
                if between is not None:
                    between()
                for g, half, t, b in norm_groups(i):
                    ve.wait_ge(x_hi_made, 4 * i + g + 1)
                    at = (slice(None), slice(4 * half, 4 * half + 4), slice(t * P, (t + 1) * P))
                    ve.tensor_tensor(x_lo[at], b[:, :].rearrange("p (c t) -> p c t", c=4), x_hi[at],
                                     ALU.subtract).then_inc(x_lo_made, 1)

            def add_banks(first):
                for t in range(TT):
                    for half in range(2):
                        at = h[:, t, half * HALF:(half + 1) * HALF]
                        ins = ve.tensor_tensor(at, at, bank[first + 2 * t + half][:, :], ALU.add)
                    ins.then_inc(h_ready, 1)

            def attention(layer, scale, extra):
                first = layer * HEADS

                def maxima(hd):
                    a = first + hd
                    s, st = score[:, a % 2], stat[:, a % 2]
                    ve.wait_ge(scores_ready, a + 1)
                    if hd == 0:
                        ve.wait_ge(bias_loaded[layer], 32)
                        ve.wait_ge(diag_stored[1], 16)
                    link(ve.scalar_tensor_tensor(out=s, in0=bank[4 + a % 2][:, 0:DIAGS], scalar=scale, in1=bias[:, hd],
                                                 op0=ALU.mult, op1=ALU.add))
                    ve.tensor_reduce(st[:, 0, 0:1], s[:, 0:P], AX, ALU.max)
                    link(ve.tensor_reduce(st[:, 0, 1:2], s[:, P:DIAGS], AX, ALU.max))
                    if layer == 0:
                        ve.tensor_scalar(st[:, 1, :], st[:, 0, :], sink[:, hd:hd + 1], -1.0, ALU.max, ALU.mult)\
                            .then_inc(negmax_ready, 1)
                    else:
                        ve.tensor_scalar(st[:, 1, :], st[:, 0, :], -1.0, None, ALU.mult).then_inc(negmax_ready, 1)

                def output(hd):
                    ve.wait_ge(oT_hi_made, first + hd + 1)
                    dst, src = head_out(layer, hd, m_lo)
                    ve.tensor_tensor(dst, src, head_out(layer, hd, m_hi)[0], ALU.subtract).then_inc(oT_lo_made, 1)

                maxima(0)
                for hd in range(HEADS):
                    a = first + hd
                    s, st = score[:, a % 2], stat[:, a % 2]
                    if hd + 1 < HEADS:
                        maxima(hd + 1)
                    ve.wait_ge(exp_made, a + 1)
                    if layer == 0:
                        link(ve.tensor_tensor(st[:, 2], st[:, 2], st[:, 3], ALU.add))
                    link(ve.reciprocal(st[:, 4], st[:, 2]))
                    ve.tensor_scalar(s[:, 0:P], s[:, 0:P], st[:, 4, 0:1], None, ALU.mult)
                    ve.tensor_scalar(s[:, P:DIAGS], s[:, P:DIAGS], st[:, 4, 1:2], None, ALU.mult).then_inc(probs_ready, 1)
                    extra(hd)
                    if hd:
                        output(hd - 1)
                output(HEADS - 1)

            ve.memset(zeros_r[:, :].bitcast(F32), 0.0).then_inc(memsets_done, 1)
            ve.memset(cu[:, :, 0:2], 0.0).then_inc(memsets_done, 1)
            ve.wait_ge(x_loaded, 32)

            def split_q(n):
                ve.wait_ge(hi_made, n + 1)
                for dst, src, hi in zip(by_group(w_lo[:, n], True), by_group(raw[:, n], False), by_group(w_hi[:, n], True)):
                    ins = ve.tensor_tensor(dst, src, hi, ALU.subtract)
                ins.then_inc(lo_made, 1)

            norm(0, lambda: split_q(0))
            split_q(1)
            split(KV_T)
            for i in range(2):
                split(SPLIT + i)
            for l in range(2):
                ve.wait_ge(p_hi_made, l + 1)
                ve.tensor_tensor(p_lo[:, l], bank[6 + l][:, :].rearrange("p (c t) -> p c t", c=2), p_hi[:, l],
                                 ALU.subtract).then_inc(p_lo_made, 1)
            ve.wait_ge(r_hi_made, 1)
            ve.tensor_tensor(r_lo[:, :, :], r_raw[:, :, :], r_hi[:, :, :], ALU.subtract).then_inc(r_lo_made, 1)
            ve.wait_ge(aux_loaded, 80)
            ve.wait_ge(taps_made, 1)
            ve.wait_ge(memsets_done, 2)
            split(SPLIT + 2)

            def beside(hd):
                if hd < 4:
                    conv_tile(hd + 2)
                elif hd % 2:
                    split(OUT0_T + hd // 2 - 2 + SPLIT)

            def conv_tile(hd):
                i, part = hd // 3, hd % 3
                ve.wait_ge(tile_used, CONV_T + hd + 1)
                ps = bank[hd % 4][:, :].rearrange("p (j t) -> p j t", j=2)
                if part == 1:
                    ve.wait_ge(c_made, i + 1)
                    link(ve.tensor_tensor(cu[:, 2 * i:2 * i + 2, 2:SEQ + 2], c_sb, ps, ALU.mult))
                    for tap in range(3):
                        for j in range(2):
                            src, w = cu[:, 2 * i + j, tap:tap + SEQ], conv_w[:, 4 * tap + 2 * i + j:4 * tap + 2 * i + j + 1]
                            if tap == 0:
                                ins = ve.tensor_scalar(conv_y[:, j], src, w, None, ALU.mult)
                            else:
                                ins = ve.scalar_tensor_tensor(out=conv_y[:, j], in0=src, scalar=w, in1=conv_y[:, j],
                                                              op0=ALU.mult, op1=ALU.add)
                        link(ins)
                if part == 2:
                    ve.tensor_tensor(conv_a, conv_y, ps, ALU.mult).then_inc(conv_made, 1)
                    ve.wait_ge(conv_hi_made, i + 1)
                    ve.tensor_tensor(m_lo[:, 2 * i:2 * i + 2], conv_a, m_hi[:, 2 * i:2 * i + 2], ALU.subtract)\
                        .then_inc(conv_lo_made, 1)
                split(CONV_T + hd + SPLIT)

            conv_tile(0)
            conv_tile(1)
            attention(0, SWA_D ** -0.5, beside)
            split(OUT0_T + 2 + SPLIT)
            ve.wait_ge(tile_used, OUT0_T + 4)
            add_banks(0)
            norm(1)
            split(OUT0_T + 3 + SPLIT)

            def hidden(n, i):
                ve.wait_ge(tile_used, n + 1)
                ve.wait_ge(silu_made, i + 1)
                if not isinstance(i, int):
                    ve.wait_ge(hid_lo_made, i)
                ve.tensor_tensor(hid, silu, bank[1][:, :], ALU.mult).then_inc(hid_made, 1)

            def hidden_lo(i):
                ve.wait_ge(hid_hi_made, i + 1)
                ve.tensor_tensor(hid_lo, hid.rearrange("p (j t) -> p j t", j=2), hid_hi, ALU.subtract).then_inc(hid_lo_made, 1)

            split(FFN_T + SPLIT)
            hidden(FFN_T + 1, 0)
            split(FFN_T + 1 + SPLIT)
            hidden_lo(0)
            with ve.Fori(0, (PAIRS - 1) // 2) as r:
                for u in range(2):
                    n = FFN_T + 2 + 3 * u
                    i = 1 + u + 2 * r
                    split(n + SPLIT + 6 * r, n + SPLIT)
                    hidden(n + 1 + 6 * r, i)
                    split(n + 1 + SPLIT + 6 * r, n + 1 + SPLIT)
                    split(n + 2 + SPLIT + 6 * r, n + 2 + SPLIT)
                    hidden_lo(i)
            ve.wait_ge(tile_used, PLE0_T)
            add_banks(4)

            def embed(l, proj):
                for t in range(TT):
                    for half in range(2):
                        b = 2 * t + half
                        ve.wait_ge(sig_made, 4 * l + b + 1)
                        ve.tensor_tensor(sig[:, b], sig[:, b], proj(b), ALU.mult).then_inc(gated_made, 1)
                    for half in range(2):
                        b = 2 * t + half
                        ve.wait_ge(gated_made, 4 * l + b + 1)
                        at = h[:, t, half * HALF:(half + 1) * HALF]
                        ins = ve.tensor_tensor(at, at, sig[:, b], ALU.add)
                    ins.then_inc(h_ready, 1)

            norm(2)
            for i in range(-1, 4):
                split(PLE0_T + i + SPLIT)
            embed(0, lambda b: bank[b][:, :])
            norm(3)
            split(PLE0_T + 4 + SPLIT)
            for i in range(8):
                split(QK_T + i + SPLIT)

            def beside1(hd):
                if hd < 4:
                    split(V_T + hd + SPLIT)
                elif hd != 6:
                    split(OUT1_T + (0, 1, None, 2)[hd - 4] + SPLIT)

            attention(1, MOBA_D ** -0.5, beside1)
            ve.wait_ge(tile_used, OUT1_T + 4)
            add_banks(0)
            norm(4)
            split(OUT1_T + 3 + SPLIT)
            E = EXPERTS
            R = lambda a, n: route[:, a:a + n]
            logit = R(0, 16).rearrange("p (t e) -> p t e", t=TT)
            top, negtop = R(16, 2), R(24, 2)
            ex = R(32, 16).rearrange("p (t e) -> p t e", t=TT)
            rank = R(48, 16).rearrange("p (t e) -> p t e", t=TT)
            chosen = R(64, 16).rearrange("p (t e) -> p t e", t=TT)
            gate = R(80, 16).rearrange("p (t e) -> p t e", t=TT)
            pos1 = R(96, 16).rearrange("p (t e) -> p t e", t=TT)
            den, rden = R(112, 2), R(114, 2)
            over, orank, is_o = R(116, 8), R(124, 8), R(132, 8)
            sums, eid = R(140, 4), R(144, 4)
            tmp = R(160, 64).rearrange("p (e f) -> p e f", e=E)
            tmp2 = R(224, 64).rearrange("p (e f) -> p e f", e=E)
            tmp3 = R(288, 16).rearrange("p (t e) -> p t e", t=TT)
            before = cst[:, C_BEFORE:C_EIDX].rearrange("p (e f) -> p e f", e=E)
            eidx = cst[:, C_EIDX:C_END]
            ve.wait_ge(logits_ready, 1)
            link(ve.tensor_copy(logit, bank[4][:, 0:2 * E].rearrange("p (t e) -> p t e", t=TT)))
            link(ve.tensor_reduce(top, logit, AX, ALU.max))
            ve.tensor_scalar(negtop, top, -1.0, None, ALU.mult).then_inc(route_exp_ready, 1)
            for t in range(TT):
                mine = logit[:, t].unsqueeze(2).broadcast_to((P, E, E))
                other = logit[:, t].unsqueeze(1).broadcast_to((P, E, E))
                ve.tensor_tensor(tmp, other, mine, ALU.is_gt)
                link(ve.tensor_tensor(tmp2, other, mine, ALU.is_equal))
                link(ve.tensor_tensor(tmp2, tmp2, before, ALU.mult))
                link(ve.tensor_tensor(tmp, tmp, tmp2, ALU.add))
                link(ve.tensor_reduce(rank[:, t], tmp, AX, ALU.add))
            ve.tensor_scalar(chosen, rank, TOP_K - 0.5, None, ALU.is_lt).then_inc(chosen_ready, 1)
            ve.wait_ge(chosen_ready, 1)
            ve.wait_ge(route_exp_made, 2)
            link(ve.tensor_tensor(ex, ex, chosen, ALU.mult))
            link(ve.tensor_reduce(den, ex, AX, ALU.add))
            link(ve.reciprocal(rden, den))
            for t in range(TT):
                link(ve.tensor_scalar(gate[:, t], ex[:, t], rden[:, t:t + 1], None, ALU.mult))
            ve.wait_ge(ranks_ready, 1)
            link(ve.scalar_tensor_tensor(out=pos1, in0=bank[5][:, 0:2 * E].rearrange("p (t e) -> p t e", t=TT),
                                         scalar=1.0, in1=chosen, op0=ALU.add, op1=ALU.mult))
            for t in range(TT):
                ve.tensor_scalar(jobs[:, 0:E, 0, t], pos1[:, t], -1.0, None, ALU.add)
                ve.tensor_copy(jobs[:, 0:E, 1, t], gate[:, t])
            link(ve.tensor_scalar(over, bank[5][:, 2 * E:3 * E], P + 0.5, None, ALU.is_gt))
            link(ve.tensor_tensor(tmp, before, over.unsqueeze(1).broadcast_to((P, E, E)), ALU.mult))
            ve.tensor_reduce(orank, tmp, AX, ALU.add)
            link(ve.tensor_reduce(eid[:, 3:4], over, AX, ALU.add))
            link(ve.tensor_scalar(eid[:, 3:4], eid[:, 3:4], float(EXPERTS), None, ALU.add))
            for o in range(EXTRA):
                link(ve.scalar_tensor_tensor(out=is_o, in0=orank, scalar=float(o), in1=over, op0=ALU.is_equal, op1=ALU.mult))
                link(ve.tensor_tensor(tmp3[:, 0], is_o, eidx, ALU.mult))
                link(ve.tensor_reduce(eid[:, o:o + 1], tmp3[:, 0], AX, ALU.add))
                for t in range(TT):
                    link(ve.tensor_tensor(tmp3[:, 0], is_o, pos1[:, t], ALU.mult))
                    link(ve.tensor_tensor(tmp3[:, 1], is_o, gate[:, t], ALU.mult))
                    link(ve.tensor_reduce(sums[:, 0:2], tmp3, AX, ALU.add))
                    ve.tensor_scalar(jobs[:, E + o, 0, t:t + 1], sums[:, 0:1], -1.0 - P, None, ALU.add)
                    link(ve.tensor_copy(jobs[:, E + o, 1, t:t + 1], sums[:, 1:2]))
            link(ve.memset(jobs[:, JOBS], -1.0))
            ve.tensor_copy(job_int[:, :], eid[0:1, :]).then_inc(jobs_ready, 1)
            split(PROJ1_T + SPLIT)

            def picks(j):
                ve.tensor_copy(job[:, :, :, :], jobs[:, bass.ds(j, 1), :, :]).then_inc(job_read, 1)
                ve.wait_ge(job_read, j + 1)
                for t in range(TT):
                    ve.tensor_scalar(pick_g[:, t], iota, job[:, 0, 0, t:t + 1], job[:, 0, 1, t:t + 1], ALU.is_equal, ALU.mult)
                for t in range(TT):
                    ins = ve.tensor_scalar(pick[:, t], iota, job[:, 0, 0, t:t + 1], None, ALU.is_equal)
                ins.then_inc(pick_made, 1)

            def gathered(j):
                for half in range(2):
                    ve.wait_ge(xg_hi_made, 2 * j + (half + 1))
                    at = x_lo[:, 4 * half:4 * half + 4, 0:P]
                    ve.tensor_tensor(at, bank[4 + half][:, :].rearrange("p (c t) -> p c t", c=4),
                                     x_hi[:, 4 * half:4 * half + 4, 0:P], ALU.subtract).then_inc(xg_lo_made, 1)

            def scattered(j, last=False):
                for q in range(4):
                    ve.wait_ge(scatter_ready, 4 * j + (q + 1))
                    at = h[:, q // 2, (q % 2) * HALF:(q % 2 + 1) * HALF]
                    ins = ve.tensor_tensor(at, at, bank[2 + q][:, :], ALU.add)
                    if not last:
                        ins.then_inc(scatter_added, 1)
                    elif q % 2:
                        ins.then_inc(h_ready, 1)

            def expert(j):
                def lo(k, b=None):
                    n = MOE_T + k + SPLIT
                    split(n + JOB_TILES * j if b is None else n + JOB_TILES * j + 6 * b, n)

                def hidden_of(k, b, looped):
                    n = MOE_T + k + 1 + JOB_TILES * j
                    ve.wait_ge(tile_used, n + 6 * b if looped else n)
                    ve.wait_ge(e_silu_made, BLOCKS * j + b + 1)
                    ve.tensor_tensor(hid, silu, bank[1][:, :], ALU.mult).then_inc(e_hid_made, 1)

                def hidT_of(b):
                    ve.wait_ge(hidT_hi_made, BLOCKS * j + b + 1)
                    ve.tensor_tensor(hidT_lo, bank[2][:, :].rearrange("p (c t) -> p c t", c=4), hidT_hi,
                                     ALU.subtract).then_inc(hidT_lo_made, 1)

                for k in range(3):
                    lo(k)
                hidden_of(3, 0, False)
                lo(3)
                scattered(j)
                hidT_of(0)
                ve.wait_ge(place_made, j + 2)
                picks(j + 1)
                with ve.Fori(1, BLOCKS) as b:
                    for k in range(-2, 1):
                        lo(k, b)
                    hidden_of(1, b, True)
                    for k in range(1, 4):
                        lo(k, b)
                    hidT_of(b)
                gathered(j + 1)
                lo(JOB_TILES - 2)
                lo(JOB_TILES - 1)

            ve.wait_ge(jobs_ready, 1)
            ve.memset(y_sb[:, 0:HALF], 0.0).then_inc(y_made, 1)
            ve.memset(y_sb[:, HALF:D], 0.0).then_inc(y_made, 1)
            ve.memset(place, 0.0).then_inc(place_made, 1)
            picks(0)
            gathered(0)
            nj = each_job(ve, expert)
            scattered(nj, last=True)
            norm(5)
            split(GATE1_T + SPLIT + JOB_TILES * nj, GATE1_T + SPLIT)
            embed(1, lambda b: proj1[:, b])
            norm(6)


_INS = ["x", "p", "rel_bias", "final_norm", "e_norm_mix", "e_w_in", "e_conv_w", "e_sinks", "e_w_out",
        "e_norm_ffn", "e_ffn_gate", "e_ffn_up", "e_ffn_down", "e_norm_ple", "e_ple_gate", "e_ple_proj",
        "o_norm_mix", "o_w_qkv", "o_w_o", "o_norm_ffn", "o_router", "o_exp_gate", "o_exp_up", "o_exp_down",
        "o_norm_ple", "o_ple_gate", "o_ple_proj"]


def kernel(**inputs):
    import concourse.bacc as _bacc
    from concourse.bass_utils import run_bass_kernel_spmd as _run

    nc = _bacc.Bacc("TRN2", target_bir_lowering=False, num_devices=1)
    arrays = {f"in_{name}": np.ascontiguousarray(inputs[name]) for name in _INS}
    consts, onehots = shape_constants()
    arrays["in_consts"], arrays["in_onehots"] = consts, onehots
    args = [nc.dram_tensor(n, a.shape, mybir.dt.from_np(a.dtype), kind="ExternalInput").ap() for n, a in arrays.items()]
    out = nc.dram_tensor("out_0", (1, SEQ, D), F32, kind="ExternalOutput").ap()
    trunk(nc, *args, out)
    r = _run(nc, [arrays], core_ids=[0])
    return r.results[0]["out_0"]
```

```python
from contextlib import ExitStack

import numpy as np

import concourse.bass as bass
from concourse import mybir

F32 = mybir.dt.float32
F32R = mybir.dt.float32r
I32 = mybir.dt.int32
ALU = mybir.AluOpType
ACT = mybir.ActivationFunctionType
AX = mybir.AxisListType.X

P = 128
SEQ, D, HEADS, BUCKETS, PLE = 256, 1024, 8, 32, 256
TT = SEQ // P
KC = D // P
EPS = 1e-6
HALF = 512
MASKED = -1e30
DIAGS = 3 * P

SC = D // 2
SWA_D, SWA_KV, SWA_WINDOW = 64, 2, 128
MOBA_D = D // HEADS
D_FF = 2816
PAIRS = D_FF // (2 * P)
EXPERTS, TOP_K, D_FFE = 8, 2, 3584
BLOCKS = D_FFE // HALF
EXTRA = 3
JOBS = EXPERTS + EXTRA

TILE = 2048
RAW, SPLIT = 6, 3
Q0_T, KV_T, CONV_T = 0, 2, 3
OUT0_T = 9
FFN_T = 13
PLE0_T = FFN_T + 3 * PAIRS
QKV_T = PLE0_T + 5
OUT1_T = QKV_T + 3 * HEADS // 2
PROJ1_T = OUT1_T + 4
MOE_T = PROJ1_T + 1
JOB_TILES = 6 * BLOCKS
GATE1_T = MOE_T
assert JOB_TILES % RAW == 0 and RAW % SPLIT == 0

C_IDENT, C_TRI, C_IOTA, C_ONES = 0, P, 2 * P, 3 * P
C_BEFORE = 4 * P
C_EIDX = C_BEFORE + EXPERTS * EXPERTS
C_END = C_EIDX + EXPERTS


def shape_constants():
    c = np.zeros((P, C_END), np.float32)
    c[:, C_IDENT:C_IDENT + P] = np.eye(P)
    c[:, C_TRI:C_TRI + P] = np.arange(P)[:, None] < np.arange(P)[None]
    c[:, C_IOTA:C_IOTA + P] = np.arange(P)
    c[:, C_ONES:C_ONES + P] = 1.0
    e = np.arange(EXPERTS)
    c[:, C_BEFORE:C_EIDX] = (e[None] < e[:, None]).reshape(-1)
    c[:, C_EIDX:C_END] = e
    dist = 2 * P - 1 - np.arange(DIAGS)
    exact = BUCKETS // 2
    far = exact + (np.log(np.maximum(dist, exact) / exact) / np.log(P / exact) * (BUCKETS - exact)).astype(int)
    bucket = np.where(dist < exact, dist, np.minimum(far, BUCKETS - 1))
    oh = np.zeros((BUCKETS + 1, 2, DIAGS), np.float32)
    for layer, reach in ((0, SWA_WINDOW), (1, SEQ)):
        valid = (dist >= 0) & (dist < reach)
        m = np.flatnonzero(valid)
        oh[bucket[m], layer, m] = 1.0
        oh[BUCKETS, layer] = np.where(valid, 0.0, MASKED)
    return c, oh.reshape(BUCKETS + 1, 2 * DIAGS)


def trunk(nc, x, p, rel_bias, final_norm, e_norm_mix, e_w_in, e_conv_w, e_sinks, e_w_out,
          e_norm_ffn, e_ffn_gate, e_ffn_up, e_ffn_down, e_norm_ple, e_ple_gate, e_ple_proj,
          o_norm_mix, o_w_qkv, o_w_o, o_norm_ffn, o_router, o_exp_gate, o_exp_up, o_exp_down,
          o_norm_ple, o_ple_gate, o_ple_proj, consts, onehots, out):
    gains = [e_norm_mix[0:1], e_norm_ffn[0:1], e_norm_ple[0:1], o_norm_mix[0:1], o_norm_ffn[0:1],
             o_norm_ple[0:1], final_norm.rearrange("(a d) -> a d", a=1)]
    diag_dram = nc.dram_tensor("diag_scratch", (2, HEADS, P, DIAGS), F32, kind="Internal").ap()

    with ExitStack() as ctx:
        def sb(name, shape, dt=F32):
            return ctx.enter_context(nc.sbuf_tensor(name, shape, dt))

        def sem(name):
            return ctx.enter_context(nc.semaphore(name))

        raw = sb("raw", [P, RAW, TILE])
        w_hi = sb("w_hi", [P, SPLIT, TILE], F32R)
        w_lo = sb("w_lo", [P, SPLIT, TILE], F32R)
        h = sb("h", [P, TT, D])
        xn = sb("xn", [P, TT, D])
        x_hi = sb("x_hi", [P, KC, SEQ], F32R)
        x_lo = sb("x_lo", [P, KC, SEQ], F32R)
        m_hi = sb("m_hi", [P, KC, SEQ], F32R)
        m_lo = sb("m_lo", [P, KC, SEQ], F32R)
        p_hi = sb("p_hi", [P, 2, 2, SEQ], F32R)
        p_lo = sb("p_lo", [P, 2, 2, SEQ], F32R)
        r_raw = sb("r_raw", [P, KC, EXPERTS])
        r_hi = sb("r_hi", [P, KC, EXPERTS], F32R)
        r_lo = sb("r_lo", [P, KC, EXPERTS], F32R)
        zeros_r = sb("zeros_r", [P, P], F32R)
        gain = sb("gain", [P, 2, D])
        cst = sb("cst", [P, C_END])
        rel = sb("rel", [BUCKETS + 1, HEADS])
        bias = sb("bias", [P, HEADS, DIAGS])
        sink = sb("sink", [P, HEADS])
        conv_w = sb("conv_w", [P, 3 * SC // P])
        ssq = sb("ssq", [P, 4, TT])
        rstd = sb("rstd", [P, TT])
        score = sb("score", [P, 2, DIAGS])
        probT = sb("probT", [P, 2, DIAGS])
        stat = sb("stat", [P, 2, 5, TT])
        diag = probT[0:HEADS].rearrange("p b n -> p (b n)")
        work = sb("work", [P, 6 * D])
        proj1 = bias[:, 0:6].rearrange("p h m -> p (h m)")[:, 0:2 * D].rearrange("p (b n) -> p b n", b=4)
        oh = work[0:BUCKETS + 1, 4224:4992]
        taps = work[0:3 * SC // P, 4992:5120]
        p_raw = work[:, 5 * D:6 * D].rearrange("p (l t n) -> p l t n", l=2, t=TT)
        q0T = work[:, 0:D].rearrange("p (j t) -> p j t", j=4)
        k0T = work[:, D:D + SEQ]
        v0 = work[:, D + SEQ:D + 2 * SEQ].rearrange("p (t n) -> p t n", t=TT)
        c_sb = work[:, 1536:2048].rearrange("p (j t) -> p j t", j=2)
        cu = work[:, 2048:2048 + 4 * (SEQ + 2)].rearrange("p (j t) -> p j t", j=4)
        conv_y = work[:, 3200:3712].rearrange("p (j t) -> p j t", j=2)
        conv_a = work[:, 3712:4224].rearrange("p (j t) -> p j t", j=2)
        q1T = work[:, 0:2 * D].rearrange("p (j t) -> p j t", j=HEADS)
        k1T = work[:, 2 * D:4 * D].rearrange("p (j t) -> p j t", j=HEADS)
        v1 = work[:, 4 * D:6 * D].rearrange("p (t n) -> p t n", t=TT)
        silu = work[:, 0:HALF]
        hid = work[:, HALF:2 * HALF]
        sig = work[:, 2 * D:4 * D].rearrange("p (b n) -> p b n", b=4)
        y_sb = work[:, 2 * D:3 * D]
        pick = work[:, 3 * D:3 * D + 2 * P].rearrange("p (t s) -> p t s", t=TT)
        pick_g = work[:, 3 * D + 2 * P:3 * D + 4 * P].rearrange("p (t s) -> p t s", t=TT)
        place = work[:, 3 * D + 4 * P:3 * D + 6 * P]
        route = work[:, 4 * D:5 * D]
        logitT = work[0:EXPERTS, 5 * D:5 * D + SEQ]
        hid_hi = [m_hi[:, 2 * i:2 * i + 2] for i in range(2)]
        hid_lo = [m_lo[:, 2 * i:2 * i + 2] for i in range(2)]
        hidT_hi = m_hi[:, 0:2].rearrange("p a (b s) -> p (a b) s", b=2)
        hidT_lo = m_lo[:, 0:2].rearrange("p a (b s) -> p (a b) s", b=2)
        jobs = sb("jobs", [P, JOBS + 1, 2, TT])
        job = sb("job", [P, 1, 2, TT])
        job_int = sb("job_int", [1, 4], I32)
        table_probe = sb("table_probe", [1, 5])
        ident = cst[:, C_IDENT:C_IDENT + P]
        iota = cst[:, C_IOTA:C_IOTA + P]
        bank = [ctx.enter_context(nc.psum_tensor(f"bank{i}", [P, HALF], F32)) for i in range(8)]

        tile_loaded = [sem(f"tile_loaded{i}") for i in range(RAW)]
        hi_made, lo_made, tile_used = sem("hi_made"), sem("lo_made"), sem("tile_used")
        x_loaded, cst_loaded = [sem("x_loaded0"), sem("x_loaded1")], sem("cst_loaded")
        diag_in_loaded, aux_loaded = sem("diag_in_loaded"), sem("aux_loaded")
        first_gain_loaded = sem("first_gain_loaded")
        gain_loaded = [sem("gain_loaded0"), sem("gain_loaded1")]
        diag_ready, diag_copied = sem("diag_ready"), sem("diag_copied")
        diag_stored = [sem("diag_stored0"), sem("diag_stored1")]
        bias_loaded = [sem("bias_loaded0"), sem("bias_loaded1")]
        taps_ready, taps_made = sem("taps_ready"), sem("taps_made")
        pT_ready, p_hi_made, p_lo_made = sem("pT_ready"), sem("p_hi_made"), sem("p_lo_made")
        r_hi_made, r_lo_made = sem("r_hi_made"), sem("r_lo_made")
        memsets_done = sem("memsets_done")
        h_ready, squares_made, xn_ready = sem("h_ready"), sem("squares_made"), sem("xn_ready")
        xT_ready, x_hi_made, x_lo_made = sem("xT_ready"), sem("x_hi_made"), sem("x_lo_made")
        vec_step = sem("vec_step")
        q0_made, kv0_made, c_made, b_made = sem("q0_made"), sem("kv0_made"), sem("c_made"), sem("b_made")
        conv_hi_made, conv_lo_made, conv_made = sem("conv_hi_made"), sem("conv_lo_made"), sem("conv_made")
        qkv1_made = sem("qkv1_made")
        scores_ready, negmax_ready, exp_made = sem("scores_ready"), sem("negmax_ready"), sem("exp_made")
        probs_ready, probT_ready, probT_made = sem("probs_ready"), sem("probT_ready"), sem("probT_made")
        oT_ready, oT_hi_made, oT_lo_made = sem("oT_ready"), sem("oT_hi_made"), sem("oT_lo_made")
        silu_made, hid_made = sem("silu_made"), sem("hid_made")
        hid_hi_made, hid_lo_made = sem("hid_hi_made"), sem("hid_lo_made")
        gated_made = sem("gated_made")
        sig_made, proj_made = sem("sig_made"), sem("proj_made")
        logitT_ready, logitT_made = sem("logitT_ready"), sem("logitT_made")
        logits_ready, route_exp_ready, route_exp_made = sem("logits_ready"), sem("route_exp_ready"), sem("route_exp_made")
        chosen_ready, ranks_ready, jobs_ready = sem("chosen_ready"), sem("ranks_ready"), sem("jobs_ready")
        pick_made, gather_ready, xg_hi_made, xg_lo_made = sem("pick_made"), sem("gather_ready"), sem("xg_hi_made"), sem("xg_lo_made")
        job_read = sem("job_read")
        pickT_ready, place_made = sem("pickT_ready"), sem("place_made")
        e_silu_made, e_hid_made = sem("e_silu_made"), sem("e_hid_made")
        hidT_ready, hidT_hi_made, hidT_lo_made = sem("hidT_ready"), sem("hidT_hi_made"), sem("hidT_lo_made")
        y_ready = sem("y_ready")
        y_made, scatter_ready, scatter_added = sem("y_made"), sem("scatter_ready"), sem("scatter_added")
        out_stored = sem("out_stored")
        sum_ready = sem("sum_ready")

        block = ctx.enter_context(nc.Block())

        def last_job(eng):
            eng.wait_ge(jobs_ready, 1)
            return eng.value_load(job_int[0:1, 3:4], min_val=EXPERTS - 1, max_val=JOBS - 1)

        def each_job(eng, body):
            with eng.Fori(0, EXPERTS - 1) as j:
                body(j)
            last = last_job(eng)
            with eng.If(last > EXPERTS - 1):
                with eng.Fori(EXPERTS - 1, last) as j:
                    body(j)
            body(last, last=True)
            return last + 1

        def by_group(tile, regrouped):
            if regrouped:
                v = tile.rearrange("p (k j g d) -> p g k j d", k=4, j=4, g=SWA_KV)
            else:
                v = tile.rearrange("p (k g j d) -> p g k j d", k=4, g=SWA_KV, j=4)
            return [v[:, g] for g in range(SWA_KV)]

        def head_out(layer, hd, dst):
            if layer == 0:
                lanes = slice(SWA_D * (hd % 2), SWA_D * (hd % 2) + SWA_D)
                return dst[lanes, 4 + hd // 2, :], bank[7][lanes, 0:SEQ]
            return dst[:, hd, :], bank[7][:, 0:SEQ]

        def qkv_beside(hd):
            i = 3 * (hd // 2) + 3
            return [] if hd >= HEADS - 2 else [i + 2] if hd % 2 else [i, i + 1]

        QUARTERS = [(half, t) for half in range(2) for t in range(TT)]

        def norm_groups(i):
            first = 0 if i == 3 else 4
            return [(g, half, t, bank[first + g]) for g, (half, t) in enumerate(QUARTERS)]

        def wait_sum(eng, done, b, n):
            eng.wait_ge(*((tile_used, n + 1) if b == 3 else (sum_ready, 3 * done + b + 1)))

        @block.sync
        def _(sp):
            def load(n, src, slot=None):
                if slot is not None or n >= RAW:
                    sp.wait_ge(lo_made, n - RAW + 1)
                slot = n % RAW if slot is None else slot
                sp.dma_start(raw[:, slot].rearrange("p (c n) -> p c n", c=src.shape[1]), src)\
                  .then_inc(tile_loaded[slot], 16)

            def cols_of(w, c0, n, k0=0, k=KC):
                return w[k0 * P:(k0 + k) * P, c0:c0 + n].rearrange("(c p) n -> p c n", p=P)

            def rows_of(w, pair):
                return w[pair * 2 * P:(pair + 1) * 2 * P, :].rearrange("(c p) n -> p c n", p=P)

            for t in range(TT):
                sp.dma_start(h[:, t], x[0, t * P:(t + 1) * P, :]).then_inc(x_loaded[t], 16)
            w_in = e_w_in[0]
            for i in range(2):
                load(Q0_T + i, cols_of(w_in, 3 * SC, HALF, 4 * i, 4))
            load(KV_T, cols_of(w_in, 4 * SC, 2 * P))
            sp.wait_ge(diag_stored[0], 16)
            for i in range(2):
                for part, first in enumerate((SC, 2 * SC, 0)):
                    load(CONV_T + 3 * i + part, cols_of(w_in, first + i * 2 * P, 2 * P))
            for i in range(4):
                load(OUT0_T + i, rows_of(e_w_out[0], i))
            load(FFN_T, cols_of(e_ffn_gate[0], 0, 2 * P))
            load(FFN_T + 1, cols_of(e_ffn_up[0], 0, 2 * P))
            gate_v = e_ffn_gate[0].rearrange("(c p) (i n) -> i p c n", p=P, n=2 * P)
            up_v = e_ffn_up[0].rearrange("(c p) (i n) -> i p c n", p=P, n=2 * P)
            down_v = e_ffn_down[0].rearrange("(i c p) n -> i p c n", p=P, c=2)
            with sp.Fori(0, (PAIRS - 1) // 2) as r:
                for u in range(2):
                    i = 1 + u + 2 * r
                    for part, src in enumerate((gate_v[i], up_v[i], down_v[i - 1])):
                        n = FFN_T + 2 + 3 * u + part
                        load(n + 6 * r, src, slot=n % RAW)
            load(PLE0_T - 1, down_v[PAIRS - 1])
            load(PLE0_T, rows_of(e_ple_proj[0], 0))
            for i in range(4):
                load(PLE0_T + 1 + i, rows_of(e_ple_gate[0], i))
            for i in range(3 * HEADS // 2):
                load(QKV_T + i, cols_of(o_w_qkv[0], i % 3 * D + i // 3 * 2 * P, 2 * P))
            for i in range(4):
                load(OUT1_T + i, rows_of(o_w_o[0], i))
            load(PROJ1_T, rows_of(o_ple_proj[0], 0))
            eg = o_exp_gate[0].rearrange("e (c p) (b n) -> e b p c n", p=P, n=HALF)
            eu = o_exp_up[0].rearrange("e (c p) (b n) -> e b p c n", p=P, n=HALF)
            ed = o_exp_down[0].rearrange("e (i c p) n -> e i p c n", p=P, c=2)

            def expert(j, e):
                base = MOE_T + JOB_TILES * j

                halves = tuple(enumerate(((eg, 0), (eg, 4), (eu, 0), (eu, 4))))
                for i, (w, k) in halves:
                    load(base + i, w[e, 0, :, k:k + 4], slot=(MOE_T + i) % RAW)
                with sp.Fori(1, BLOCKS) as b:
                    for i, (w, k) in halves:
                        load(base + 6 * b + (i - 2), w[e, b, :, k:k + 4], slot=(MOE_T + 4 + i) % RAW)
                    for i in range(2):
                        load(base + 6 * b + (i + 2), ed[e, 2 * b + (i - 2)], slot=(MOE_T + 8 + i) % RAW)
                for i in range(2):
                    load(base + (JOB_TILES - 2 + i), ed[e, 2 * BLOCKS - 2 + i], slot=(MOE_T + 4 + i) % RAW)

            with sp.Fori(0, EXPERTS) as j:
                expert(j, j)
            nj = last_job(sp) + 1
            with sp.If(nj > EXPERTS):
                with sp.Fori(EXPERTS, nj) as j:
                    expert(j, sp.value_load(job_int[0:1, bass.ds(j - EXPERTS, 1)], min_val=0, max_val=EXPERTS - 1))
            for i in range(4):
                load(JOB_TILES * nj + (GATE1_T + i), rows_of(o_ple_gate[0], i), slot=(GATE1_T + i) % RAW)
            for q in range(4):
                t, cols = q // 2, slice(q % 2 * HALF, (q % 2 + 1) * HALF)
                sp.wait_ge(xn_ready, 4 * 6 + q + 1)
                sp.dma_start(out[0, t * P:(t + 1) * P, cols], xn[:, t, cols]).then_inc(out_stored, 16)
            sp.wait_ge(out_stored, 16 * 4)

        @block.gpsimd
        def _(pool):
            def load_gain(i):
                pool.dma_start(gain[:, i % 2], bass.AP(tensor=gains[i].tensor, offset=gains[i].offset, ap=[[0, P], [1, D]]))\
                    .then_inc(gain_loaded[i % 2], 16)

            pool.dma_start(oh, onehots).then_inc(diag_in_loaded, 16)
            pool.dma_start(rel[0:BUCKETS, :], rel_bias).then_inc(diag_in_loaded, 16)
            pool.dma_start(rel[BUCKETS:BUCKETS + 1, :], consts[0:1, C_ONES:C_ONES + HEADS]).then_inc(diag_in_loaded, 16)
            pool.dma_start(sink[:, :], bass.AP(tensor=e_sinks.tensor, offset=0, ap=[[0, P], [1, HEADS]])).then_inc(aux_loaded, 16)
            pool.dma_start(p_raw[:, 0], p[0, 0].rearrange("(t q) n -> q t n", q=P)).then_inc(aux_loaded, 16)
            pool.dma_start(p_raw[:, 1], p[1, 0].rearrange("(t q) n -> q t n", q=P)).then_inc(aux_loaded, 16)
            pool.dma_start(taps, e_conv_w[0].rearrange("k (c q) -> (k c) q", q=P)).then_inc(aux_loaded, 16)
            pool.dma_start(r_raw[:, :, :], o_router[0].rearrange("(c q) e -> q c e", q=P)).then_inc(aux_loaded, 16)
            load_gain(1)
            def store_diagonals(layer):
                pool.dma_start(diag_dram[layer], diag[:, layer * DIAGS:(layer + 1) * DIAGS].unsqueeze(1)
                               .broadcast_to((HEADS, P, DIAGS))).then_inc(diag_stored[layer], 16)

            def load_bias(layer):
                pool.wait_ge(diag_stored[layer], 16)
                for first, col, n in ((P, 0, P), (0, P, 2 * P)):
                    pool.dma_start(bias[:, :, col:col + n],
                                   bass.AP(tensor=diag_dram.tensor, offset=layer * HEADS * P * DIAGS + P - 1 + first,
                                           ap=[[DIAGS - 1, P], [P * DIAGS, HEADS], [1, n]])).then_inc(bias_loaded[layer], 16)

            pool.wait_ge(diag_copied, 2)
            store_diagonals(0)
            load_bias(0)
            store_diagonals(1)
            pool.wait_ge(negmax_ready, HEADS)
            load_bias(1)
            for i in range(2, 7):
                pool.wait_ge(xn_ready, 4 * (i - 1))
                load_gain(i)

        @block.scalar
        def _(act):
            act.dma_start(gain[:, 0], bass.AP(tensor=gains[0].tensor, offset=gains[0].offset, ap=[[0, P], [1, D]]))\
               .then_inc(first_gain_loaded, 16)
            act.dma_start(cst[:, :], consts).then_inc(cst_loaded, 16)

            def split(n, slot=None, rounds=None):
                slot = n % RAW if slot is None else slot
                rounds = n // RAW if rounds is None else rounds
                act.wait_ge(tile_loaded[slot], 16 * rounds + 16)
                act.activation(w_hi[:, slot % SPLIT], raw[:, slot], ACT.Copy).then_inc(hi_made, 1)

            def load_table(use, function):
                act.activation(table_probe[:, use:use + 1], cst[0:1, 0:1], function)

            def step(n, slot=None, rounds=None):
                act.wait_ge(tile_used, n + 1)
                split(n + SPLIT if slot is None else None, None if slot is None else (slot + SPLIT) % RAW, rounds)

            def norm(i, between):
                for t in range(TT):
                    for half in range(2):
                        act.wait_ge(*((h_ready, 4 * (i - 1) + 2 * t + half + 1) if i else (x_loaded[t], 16)))
                        at = slice(half * HALF, (half + 1) * HALF)
                        act.activation(xn[:, t, at], h[:, t, at], ACT.Square, scale=D ** -0.5,
                                       accum_out=ssq[:, half, t:t + 1]).then_inc(squares_made, 1)
                if i == 6:
                    return
                between()
                for g, half, t, b in norm_groups(i):
                    act.wait_ge(xT_ready, 4 * i + g + 1)
                    act.activation(x_hi[:, 4 * half:4 * half + 4, t * P:(t + 1) * P],
                                   b[:, :].rearrange("p (c t) -> p c t", c=4), ACT.Copy).then_inc(x_hi_made, 1)

            def attention(layer, lead, extra):
                first = layer * HEADS

                def exponentials(hd):
                    a = first + hd
                    s, st = score[:, a % 2], stat[:, a % 2]
                    act.wait_ge(negmax_ready, a + 1)
                    act.activation(s[:, 0:P], s[:, 0:P], ACT.Exp, bias=st[:, 1, 0:1], accum_out=st[:, 2, 0:1])
                    if layer == 0:
                        act.activation(st[:, 3, :], st[:, 1, :], ACT.Exp, bias=sink[:, hd:hd + 1])
                    act.activation(s[:, P:DIAGS], s[:, P:DIAGS], ACT.Exp, bias=st[:, 1, 1:2],
                                   accum_out=st[:, 2, 1:2]).then_inc(exp_made, 1)

                def output(hd):
                    act.wait_ge(oT_ready, first + hd + 1)
                    dst, src = head_out(layer, hd, m_hi)
                    act.activation(dst, src, ACT.Copy).then_inc(oT_hi_made, 1)

                exponentials(0)
                exponentials(1)
                lead()
                for hd in range(HEADS):
                    extra(hd)
                    if hd:
                        output(hd - 1)
                    act.wait_ge(probT_ready, first + hd + 1)
                    if hd == 0:
                        act.wait_ge(diag_stored[1], 16)
                    act.activation(probT[:, hd % 2], bank[6][:, 0:DIAGS], ACT.Copy).then_inc(probT_made, 1)
                    if hd + 2 < HEADS:
                        exponentials(hd + 2)
                output(HEADS - 1)

            def split_q(n):
                act.wait_ge(tile_loaded[n], 16)
                for dst, src in zip(by_group(w_hi[:, n], True), by_group(raw[:, n], False)):
                    ins = act.activation(dst, src, ACT.Copy)
                ins.then_inc(hi_made, 1)

            norm(0, lambda: split_q(0))
            split_q(1)
            split(KV_T)
            for l in range(2):
                act.wait_ge(diag_ready, l + 1)
                act.activation(diag[:, l * DIAGS:(l + 1) * DIAGS], bank[2 + l][0:HEADS, 0:DIAGS], ACT.Copy).then_inc(diag_copied, 1)
            step(Q0_T)
            act.wait_ge(tile_used, Q0_T + 2)
            for j in range(4):
                act.activation(q0T[:, j], bank[j][:, 0:SEQ], ACT.Copy).then_inc(q0_made, 1)
            split(Q0_T + 1 + SPLIT)
            act.wait_ge(tile_used, KV_T + 1)
            act.activation(k0T, bank[4][:, 0:SEQ], ACT.Copy).then_inc(kv0_made, 1)
            act.activation(v0, bank[5][:, 0:SEQ].rearrange("p (t n) -> p t n", t=TT), ACT.Copy).then_inc(kv0_made, 1)
            split(KV_T + SPLIT)
            act.wait_ge(taps_ready, 1)
            act.activation(conv_w[:, :], bank[1][:, 0:12], ACT.Copy).then_inc(taps_made, 1)
            for l in range(2):
                act.wait_ge(pT_ready, l + 1)
                act.activation(p_hi[:, l], bank[6 + l][:, :].rearrange("p (c t) -> p c t", c=2), ACT.Copy).then_inc(p_hi_made, 1)
            act.activation(r_hi[:, :, :], r_raw[:, :, :], ACT.Copy).then_inc(r_hi_made, 1)

            def beside(hd):
                if hd < 4:
                    conv_tile(hd + 2)
                elif hd % 2:
                    step(OUT0_T + hd // 2 - 2)

            def conv_tile(n):
                act.wait_ge(tile_used, CONV_T + n + 1)
                i, part = n // 3, n % 3
                if part == 0:
                    if i:
                        act.wait_ge(conv_made, 1)
                    act.activation(c_sb, bank[(3 * i) % 4][:, :].rearrange("p (j t) -> p j t", j=2), ACT.Copy).then_inc(c_made, 1)
                if part == 2:
                    act.wait_ge(conv_made, i + 1)
                    act.activation(m_hi[:, 2 * i:2 * i + 2], conv_a, ACT.Copy).then_inc(conv_hi_made, 1)
                split(CONV_T + n + SPLIT)

            conv_tile(0)
            attention(0, lambda: conv_tile(1), beside)
            step(OUT0_T + 2)
            load_table(0, ACT.Silu)
            norm(1, lambda: step(OUT0_T + 3))

            def ffn_up(n, i, parity, slot, rounds):
                step(n, slot, rounds[0])
                if not isinstance(i, int):
                    act.wait_ge(hid_made, i)
                act.activation(silu, bank[0][:, :], ACT.Silu).then_inc(silu_made, 1)
                act.wait_ge(hid_made, i + 1)
                act.activation(hid_hi[parity], hid.rearrange("p (j t) -> p j t", j=2), ACT.Copy).then_inc(hid_hi_made, 1)
                step(n + 1, (slot + 1) % RAW, rounds[1])

            def rounds(n):
                return (n + SPLIT) // RAW

            ffn_up(FFN_T, 0, 0, FFN_T % RAW, (rounds(FFN_T), rounds(FFN_T + 1)))
            with act.Fori(0, (PAIRS - 1) // 2) as r:
                for u in range(2):
                    n = FFN_T + 2 + 3 * u
                    ffn_up(n + 6 * r, 1 + u + 2 * r, 1 - u, n % RAW, (rounds(n) + r, rounds(n + 1) + r))
                    step(n + 2 + 6 * r, (n + 2) % RAW, rounds(n + 2) + r)

            def sigmoids(done, n):
                for b in range(4):
                    wait_sum(act, done, b, n)
                    act.activation(sig[:, b], bank[4 + b][:, :], ACT.Sigmoid).then_inc(sig_made, 1)

            norm(2, lambda: step(PLE0_T - 1))
            for i in range(3):
                step(PLE0_T + i)
            load_table(1, ACT.Sigmoid)
            sigmoids(2, PLE0_T + 4)
            norm(3, lambda: step(PLE0_T + 3))
            load_table(2, ACT.Exp)
            split(PLE0_T + 4 + SPLIT)
            def qkv_tile(i):
                act.wait_ge(tile_used, QKV_T + i + 1)
                pair, part = i // 3, i % 3
                if part < 2:
                    dst, src = (q1T, k1T)[part][:, 2 * pair:2 * pair + 2], bank[i % 4][:, :].rearrange("p (j t) -> p j t", j=2)
                else:
                    dst, src = v1[:, :, pair * 2 * P:(pair + 1) * 2 * P], bank[i % 4][:, :].rearrange("p (t n) -> p t n", t=TT)
                act.activation(dst, src, ACT.Copy).then_inc(qkv1_made, 1)
                split(QKV_T + i + SPLIT)

            def beside1(hd):
                for i in qkv_beside(hd):
                    qkv_tile(i)
                if hd >= HEADS - 2:
                    step(OUT1_T + hd - HEADS + 2)

            qkv_tile(0)
            qkv_tile(1)
            attention(1, lambda: qkv_tile(2), beside1)
            step(OUT1_T + 2)
            norm(4, lambda: step(OUT1_T + 3))
            act.wait_ge(logitT_ready, 1)
            act.activation(logitT, bank[0][0:EXPERTS, 0:SEQ], ACT.Copy).then_inc(logitT_made, 1)
            act.wait_ge(route_exp_ready, 1)
            for t in range(TT):
                act.activation(route[:, 32 + 8 * t:40 + 8 * t], route[:, 8 * t:8 * t + 8], ACT.Exp,
                               bias=route[:, 24 + t:25 + t]).then_inc(route_exp_made, 1)
            load_table(3, ACT.Silu)
            act.wait_ge(tile_used, PROJ1_T + 1)
            for b in range(4):
                act.activation(proj1[:, b], bank[b][:, :], ACT.Copy).then_inc(proj_made, 1)

            def gathered(j):
                for half in range(2):
                    act.wait_ge(gather_ready, 2 * j + (half + 1))
                    act.activation(x_hi[:, 4 * half:4 * half + 4, 0:P],
                                   bank[4 + half][:, :].rearrange("p (c t) -> p c t", c=4), ACT.Copy).then_inc(xg_hi_made, 1)

            def expert(j, last=False):
                done = JOB_TILES * j

                def st(k, b=None):
                    n = MOE_T + k
                    r = (n + SPLIT) // RAW + (JOB_TILES // RAW) * j
                    if b is None:
                        step(n + done, n % RAW, r)
                    else:
                        step(n + done + 6 * b, n % RAW, r + b)

                def silu_of():
                    act.activation(silu, bank[0][:, :], ACT.Silu).then_inc(e_silu_made, 1)

                def hidT_of(b):
                    act.wait_ge(hidT_ready, BLOCKS * j + b + 1)
                    act.activation(hidT_hi, bank[2][:, :].rearrange("p (c t) -> p c t", c=4), ACT.Copy).then_inc(hidT_hi_made, 1)

                st(0)
                st(1)
                silu_of()
                st(2)
                act.wait_ge(pickT_ready, j + 1)
                act.activation(place, bank[3][:, 0:2 * P], ACT.Copy).then_inc(place_made, 1)
                with act.Fori(1, BLOCKS) as b:
                    for k in range(-3, 0):
                        st(k, b)
                    silu_of()
                    hidT_of(b - 1)
                    for k in range(3):
                        st(k, b)
                hidT_of(BLOCKS - 1)
                st(JOB_TILES - 3)
                if not last:
                    gathered(j + 1)
                st(JOB_TILES - 2)
                for half in range(2):
                    act.wait_ge(*((tile_used, done + (MOE_T + JOB_TILES)) if half else (y_ready, j + 1)))
                    act.activation(y_sb[:, half * HALF:(half + 1) * HALF], bank[6 + half][:, :], ACT.Copy).then_inc(y_made, 1)
                if not last:
                    st(JOB_TILES - 1)

            gathered(0)
            split(PROJ1_T + SPLIT)
            nj = each_job(act, expert)
            load_table(4, ACT.Sigmoid)
            n = GATE1_T + JOB_TILES * nj
            norm(5, lambda: step(n - 1, (GATE1_T - 1) % RAW, (GATE1_T - 1 + SPLIT) // RAW + (JOB_TILES // RAW) * nj))
            step(n, GATE1_T % RAW, (GATE1_T + SPLIT) // RAW + (JOB_TILES // RAW) * nj)
            sigmoids(4, n + 3)
            norm(6, None)

        PASSES = ((0, 1), (1, 0), (0, 0))

        @block.tensor
        def _(pe):
            def three(dst, stat_hl, mov_hl, start, stop, tick=None):
                for i, (a, b) in enumerate(PASSES):
                    mm = pe.matmul(dst, stat_hl[a], mov_hl[b], start=start and i == 0, stop=stop and i == 2)
                if tick is not None:
                    mm.then_inc(tick, 1)

            def w_tile(slot, n):
                return [w[:, slot % SPLIT].rearrange("p (c n) -> p c n", n=n) for w in (w_hi, w_lo)]

            def both(pair, *at):
                return [t[at] for t in pair]

            XHL, MHL = (x_hi, x_lo), (m_hi, m_lo)
            ALL = slice(None)

            def wait_tile(n):
                pe.wait_ge(lo_made, n + 1)

            def wait_chunks(norm, k):
                pe.wait_ge(x_lo_made, 4 * norm + 2 + 2 * (k // 4))

            def up_tile(n, b, slot=None, norm=None):
                wait_tile(n)
                w = w_tile(n if slot is None else slot, 2 * P)
                for f in range(2):
                    for k in range(KC):
                        if norm is not None and f == 0 and k in (0, 4):
                            wait_chunks(norm, k)
                        three(bank[b][:, f * SEQ:(f + 1) * SEQ], both(w, ALL, k, slice(f * P, (f + 1) * P)),
                              both(XHL, ALL, k), k == 0, k == KC - 1, tile_used if (f, k) == (1, KC - 1) else None)

            def token_tile(n, b, first, cols, tick):
                w = w_tile(n, 2 * P)
                for t in range(TT):
                    for k in range(KC):
                        three(bank[b][:, t * cols:(t + 1) * cols], both(XHL, ALL, k, slice(t * P, (t + 1) * P)),
                              both(w, ALL, k, slice(first, first + cols)), k == 0, k == KC - 1,
                              tick if (t, k) == (TT - 1, KC - 1) else None)

            def down_tile(n, a, c0, b0, start, stop, slot=None, last=False, norm=None, chunks=(0, 1)):
                wait_tile(n)
                w = w_tile(n if slot is None else slot, D)
                for b in range(4):
                    t, half = b // 2, b % 2
                    if norm is not None and b in (0, 2):
                        wait_chunks(norm, 2 * b)
                    for kk in chunks:
                        three(bank[b0 + b][:, :], both(a, ALL, c0 + kk, slice(t * P, (t + 1) * P)),
                              both(w, ALL, kk, slice(half * HALF, (half + 1) * HALF)),
                              start and kk == 0, stop and kk == 1,
                              None if kk == 0 else tile_used if b == 3 else sum_ready if last else None)

            def norm(i):
                for g, half, t, b in norm_groups(i):
                    pe.wait_ge(xn_ready, 4 * i + g + 1)
                    for c in range(4):
                        at = (4 * half + c) * P
                        mm = pe.transpose(b[:, c * P:(c + 1) * P], xn[:, t, at:at + P], ident)
                    mm.then_inc(xT_ready, 1)

            def attention(layer, qT_of, kT_of, v_of, lead, extra, out_tile):
                def scores(hd):
                    a = layer * HEADS + hd
                    b = bank[4 + a % 2]
                    if hd >= 2:
                        pe.wait_ge(negmax_ready, a - 1)
                    if layer == 1:
                        pe.wait_ge(qkv1_made, 3 * (hd // 2) + 2)
                    q, k = qT_of(hd), kT_of(hd)
                    pe.matmul(b[:, 0:P], q[:, 0:P], k[:, 0:P], start=True, stop=True)
                    pe.matmul(b[:, P:DIAGS], q[:, P:SEQ], k, start=True, stop=True).then_inc(scores_ready, 1)

                def output(hd):
                    a = layer * HEADS + hd
                    if layer == 1:
                        pe.wait_ge(qkv1_made, 3 * (hd // 2) + 3)
                    pe.wait_ge(probT_made, a + 1)
                    if hd:
                        pe.wait_ge(oT_lo_made, a)
                    o = head_out(layer, hd, m_hi)[1]
                    v, pT = v_of(hd), probT[:, hd % 2]
                    pe.matmul(o[:, 0:P], v[0], pT[:, 0:P], start=True, stop=True)
                    pe.matmul(o[:, P:SEQ], v[0], pT[:, P:2 * P], start=True, stop=False)
                    pe.matmul(o[:, P:SEQ], v[1], pT[:, 2 * P:DIAGS], start=False, stop=True).then_inc(oT_ready, 1)

                scores(0)
                scores(1)
                lead()
                for hd in range(HEADS):
                    a = layer * HEADS + hd
                    extra(hd)
                    if hd:
                        output(hd - 1)
                    pe.wait_ge(probs_ready, a + 1)
                    for c in range(3):
                        mm = pe.transpose(bank[6][:, c * P:(c + 1) * P], score[:, a % 2, c * P:(c + 1) * P], ident)
                    mm.then_inc(probT_ready, 1)
                    if hd + 2 < HEADS:
                        scores(hd + 2)
                out_tile(2)
                output(HEADS - 1)
                out_tile(3, (0,))
                out_tile(3, (1,))

            pe.wait_ge(cst_loaded, 16)
            norm(0)
            pe.wait_ge(diag_in_loaded, 48)
            for l in range(2):
                pe.matmul(bank[2 + l][0:HEADS, 0:DIAGS], rel[:, :], oh[:, l * DIAGS:(l + 1) * DIAGS],
                          start=True, stop=True).then_inc(diag_ready, 1)
            for i in range(2):
                wait_chunks(0, 4 * i)
                wait_tile(Q0_T + i)
                w = w_tile(Q0_T + i, HALF)
                for j in range(4):
                    if j == 2:
                        pe.wait_ge(diag_copied, 2)
                    for k in range(4):
                        three(bank[j][:, 0:SEQ], both(w, ALL, k, slice(j * P, (j + 1) * P)), both(XHL, ALL, 4 * i + k), (i, k) == (0, 0), (i, k) == (1, 3),
                              tile_used if (j, k) == (3, 3) else None)
            wait_tile(KV_T)
            w = w_tile(KV_T, 2 * P)
            for k in range(KC):
                three(bank[4][:, 0:SEQ], both(w, ALL, k, slice(0, P)), both(XHL, ALL, k), k == 0, k == KC - 1)
            token_tile(KV_T, 5, P, P, tile_used)

            def group(hd):
                return slice(SWA_D * (hd // 4), SWA_D * (hd // 4) + SWA_D)

            def out_tile(i, chunks=(0, 1)):
                if i == 0:
                    pe.wait_ge(conv_lo_made, 2)
                if i >= 2:
                    pe.wait_ge(oT_lo_made, 4 * i - 6 + 2 * chunks[-1])
                down_tile(OUT0_T + i, MHL, 2 * i, 0, i == 0, i == 3, last=i == 3, chunks=chunks)

            def beside(hd):
                if hd < 4:
                    conv_tile(hd + 2)
                else:
                    out_tile(hd // 2 - 2, (hd % 2,))

            def conv_tile(n):
                if n == 1:
                    pe.wait_ge(taps_made, 1)
                if n == 4:
                    pe.wait_ge(c_made, 1)
                if n == 5:
                    pe.wait_ge(conv_made, 1)
                up_tile(CONV_T + n, n % 4)

            pe.wait_ge(q0_made, 4)
            pe.wait_ge(aux_loaded, 80)
            pe.transpose(bank[1][:, 0:12], taps, cst[0:12, C_IDENT:C_IDENT + 12]).then_inc(taps_ready, 1)
            for l in range(2):
                for c in range(2):
                    for t in range(TT):
                        mm = pe.transpose(bank[6 + l][:, c * SEQ + t * P:c * SEQ + (t + 1) * P],
                                          p_raw[:, l, t, c * P:(c + 1) * P], ident)
                mm.then_inc(pT_ready, 1)
            conv_tile(0)
            pe.wait_ge(kv0_made, 2)
            pe.wait_ge(p_lo_made, 2)
            attention(0, lambda hd: q0T[group(hd), hd % 4], lambda hd: k0T[group(hd)],
                      lambda hd: [v0[:, t, group(hd)] for t in range(TT)], lambda: conv_tile(1), beside, out_tile)
            norm(1)
            HHL = [(hid_hi[parity], hid_lo[parity]) for parity in range(2)]
            up_tile(FFN_T, 0, norm=1)
            up_tile(FFN_T + 1, 1)
            pe.wait_ge(memsets_done, 2)
            for b in range(4, 8):
                for q in range(4):
                    pe.matmul(bank[b][:, q * P:(q + 1) * P], zeros_r[:, :], zeros_r[:, :], start=q == 0, stop=False,
                              skip_group_check=True)

            def acc_down(n, a, slot, last):
                wait_tile(n)
                w = w_tile(slot, D)
                for b in range(4):
                    t, half = b // 2, b % 2
                    for kk in range(2):
                        for i, (s, m) in enumerate(PASSES):
                            mm = pe.matmul(bank[4 + b][:, :], a[s][:, kk, t * P:(t + 1) * P],
                                           w[m][:, kk, half * HALF:(half + 1) * HALF], start=False,
                                           stop=last and (kk, i) == (1, 2), skip_group_check=True)
                    if b == 3:
                        mm.then_inc(tile_used, 1)
                    elif last:
                        mm.then_inc(sum_ready, 1)

            with pe.Fori(0, (PAIRS - 1) // 2) as r:
                for u in range(2):
                    n = FFN_T + 2 + 3 * u
                    pe.wait_ge(silu_made, 2 * r + (1 + u))
                    up_tile(n + 6 * r, 0, n)
                    pe.wait_ge(hid_made, 2 * r + (1 + u))
                    up_tile(n + 1 + 6 * r, 1, n + 1)
                    pe.wait_ge(hid_lo_made, 2 * r + (1 + u))
                    acc_down(n + 2 + 6 * r, HHL[u], n + 2, False)
            pe.wait_ge(hid_lo_made, PAIRS)
            acc_down(PLE0_T - 1, HHL[(PAIRS - 1) % 2], PLE0_T - 1, True)

            def gate(i, n, at):
                norm(i)
                for g in range(4):
                    down_tile(n + g, XHL, 2 * g, 4, g == 0, g == 3, at + g, last=g == 3, norm=None if g else i)

            down_tile(PLE0_T, (p_hi[:, 0], p_lo[:, 0]), 0, 0, True, True)
            gate(2, PLE0_T + 1, PLE0_T + 1)
            norm(3)
            def qkv_tile(i):
                if i >= 4:
                    pe.wait_ge(qkv1_made, i - 3)
                if i % 3 < 2:
                    up_tile(QKV_T + i, i % 4, norm=None if i else 3)
                else:
                    wait_tile(QKV_T + i)
                    token_tile(QKV_T + i, i % 4, 0, 2 * P, tile_used)

            def out_tile(i, chunks=(0, 1)):
                if i == 0:
                    pe.wait_ge(qkv1_made, 12)
                pe.wait_ge(oT_lo_made, HEADS + 2 * i + 1 + chunks[-1])
                down_tile(OUT1_T + i, MHL, 2 * i, 0, i == 0, i == 3, last=i == 3, chunks=chunks)

            def beside1(hd):
                for i in qkv_beside(hd):
                    qkv_tile(i)
                if hd >= HEADS - 2:
                    out_tile(hd - HEADS + 2)

            qkv_tile(0)
            qkv_tile(1)
            attention(1, lambda hd: q1T[:, hd], lambda hd: k1T[:, hd],
                      lambda hd: [v1[:, t, hd * P:(hd + 1) * P] for t in range(TT)],
                      lambda: qkv_tile(2), beside1, out_tile)
            norm(4)
            pe.wait_ge(r_lo_made, 1)
            for k in range(KC):
                if k in (0, 4):
                    wait_chunks(4, k)
                three(bank[0][0:EXPERTS, 0:SEQ], (r_hi[:, k], r_lo[:, k]), both(XHL, ALL, k), k == 0, k == KC - 1,
                      logitT_ready if k == KC - 1 else None)
            pe.wait_ge(logitT_made, 1)
            for t in range(TT):
                mm = pe.transpose(bank[4][:, t * EXPERTS:(t + 1) * EXPERTS], logitT[:, t * P:(t + 1) * P],
                                  cst[0:EXPERTS, C_IDENT:C_IDENT + EXPERTS])
            mm.then_inc(logits_ready, 1)
            PHL = (p_hi[:, 1], p_lo[:, 1])
            down_tile(PROJ1_T, PHL, 0, 0, True, True, chunks=(0,))
            pe.wait_ge(chosen_ready, 1)
            tri, ones = cst[:, C_TRI:C_TRI + P], cst[:, C_ONES:C_ONES + P]
            chosen = [route[:, 64 + 8 * t:72 + 8 * t] for t in range(TT)]
            pe.matmul(bank[5][:, 0:8], tri, chosen[0], start=True, stop=True)
            pe.matmul(bank[5][:, 8:16], tri, chosen[1], start=True, stop=False)
            pe.matmul(bank[5][:, 8:16], ones, chosen[0], start=False, stop=True)
            pe.matmul(bank[5][:, 16:24], ones, chosen[0], start=True, stop=False)
            pe.matmul(bank[5][:, 16:24], ones, chosen[1], start=False, stop=True).then_inc(ranks_ready, 1)

            def gather(j):
                pe.wait_ge(pick_made, j + 1)
                for c in range(KC):
                    for t in range(TT):
                        mm = pe.matmul(bank[4 + c // 4][:, (c % 4) * P:(c % 4 + 1) * P], xn[:, t, c * P:(c + 1) * P],
                                       pick[:, t], start=t == 0, stop=t == TT - 1)
                    if c % 4 == 3:
                        mm.then_inc(gather_ready, 1)

            def scatter(j):
                pe.wait_ge(y_made, 2 * j + 2)
                pe.wait_ge(place_made, j + 1)
                for q in range(4):
                    pe.matmul(bank[2 + q][:, :], place[:, (q // 2) * P:(q // 2 + 1) * P],
                              y_sb[:, (q % 2) * HALF:(q % 2 + 1) * HALF], start=True, stop=True).then_inc(scatter_ready, 1)

            def expert(j, last=False):
                def up(k, b=None):
                    for i in range(4):
                        if b is not None and i == 2:
                            turn(b - 1)
                        n = MOE_T + k + i
                        wait_tile(n + JOB_TILES * j if b is None else n + JOB_TILES * j + 6 * b)
                        if b is None and i < 2:
                            pe.wait_ge(xg_lo_made, 2 * j + (i + 1))
                        w = w_tile(n, HALF)
                        for kk in range(4):
                            three(bank[i // 2][:, :], both(XHL, ALL, 4 * (i % 2) + kk, slice(0, P)), both(w, ALL, kk),
                                  (i % 2, kk) == (0, 0), (i % 2, kk) == (1, 3), tile_used if kk == 3 else None)

                def down(k, b, prev, stop):
                    pe.wait_ge(hidT_lo_made, BLOCKS * j + prev + 1)
                    for i in range(2):
                        n = MOE_T + k + i
                        wait_tile(n + JOB_TILES * j if b is None else n + JOB_TILES * j + 6 * b)
                        w = w_tile(n, D)
                        for half in range(2):
                            for kk in range(2):
                                for q, (s, m) in enumerate(PASSES):
                                    mm = pe.matmul(bank[6 + half][:, :], (hidT_hi, hidT_lo)[s][:, 2 * i + kk, :],
                                                   w[m][:, kk, half * HALF:(half + 1) * HALF], start=False,
                                                   stop=stop and (i, kk, q) == (1, 1, 2), skip_group_check=True)
                            if half:
                                mm.then_inc(tile_used, 1)
                            elif stop and i:
                                mm.then_inc(y_ready, 1)

                def turn(b):
                    pe.wait_ge(e_hid_made, BLOCKS * j + b + 1)
                    for c in range(4):
                        mm = pe.transpose(bank[2][:, c * P:(c + 1) * P], hid[:, c * P:(c + 1) * P], ident)
                    mm.then_inc(hidT_ready, 1)

                up(0)
                scatter(j)
                for half in range(2):
                    for q in range(4):
                        pe.matmul(bank[6 + half][:, q * P:(q + 1) * P], zeros_r[:, :], zeros_r[:, :], start=q == 0,
                                  stop=False, skip_group_check=True)
                pe.wait_ge(scatter_added, 4 * j + 2)
                for t in range(TT):
                    mm = pe.transpose(bank[3][:, t * P:(t + 1) * P], pick_g[:, t], ident)
                mm.then_inc(pickT_ready, 1)
                with pe.Fori(1, BLOCKS) as b:
                    up(-2, b)
                    down(2, b, b - 1, False)
                turn(BLOCKS - 1)
                if not last:
                    pe.wait_ge(scatter_added, 4 * j + 4)
                    gather(j + 1)
                down(JOB_TILES - 2, None, BLOCKS - 1, True)

            down_tile(PROJ1_T, PHL, 0, 0, True, True, chunks=(1,))
            gather(0)
            pe.wait_ge(proj_made, 4)
            nj = each_job(pe, expert)
            pe.wait_ge(scatter_added, 4 * nj)
            scatter(nj)
            gate(5, GATE1_T + JOB_TILES * nj, GATE1_T)

        @block.vector
        def _(ve):
            steps = [0]

            def link(ins):
                ins.then_inc(vec_step, 1)
                steps[0] += 1
                ve.wait_ge(vec_step, steps[0])

            def split(n, slot=None):
                slot = n % RAW if slot is None else slot % RAW
                ve.wait_ge(hi_made, n + 1)
                ve.tensor_tensor(w_lo[:, slot % SPLIT], raw[:, slot], w_hi[:, slot % SPLIT], ALU.subtract).then_inc(lo_made, 1)

            def norm(i, between=None):
                v, a, b, y = ssq[:, 0], ssq[:, 2], ssq[:, 3], rstd[:, :]
                ve.wait_ge(squares_made, 4 * (i + 1))
                link(ve.scalar_tensor_tensor(out=v, in0=v, scalar=EPS, in1=ssq[:, 1], op0=ALU.add, op1=ALU.add))
                link(ve.tensor_scalar(y.bitcast(I32), v.bitcast(I32), -0.5, float(0x5F3759DF), ALU.mult, ALU.add))
                for _ in range(3):
                    link(ve.tensor_tensor(a, y, y, ALU.mult))
                    link(ve.scalar_tensor_tensor(out=b, in0=a, scalar=-0.5, in1=v, op0=ALU.mult, op1=ALU.mult))
                    link(ve.scalar_tensor_tensor(out=y, in0=b, scalar=1.5, in1=y, op0=ALU.add, op1=ALU.mult))
                ve.wait_ge(*((gain_loaded[i % 2], 16 * ((i + 1) // 2)) if i else (first_gain_loaded, 16)))
                for half, t in QUARTERS if i < 6 else [(half, t) for t in range(TT) for half in range(2)]:
                    at = slice(half * HALF, (half + 1) * HALF)
                    ve.scalar_tensor_tensor(out=xn[:, t, at], in0=h[:, t, at], scalar=rstd[:, t:t + 1], in1=gain[:, i % 2, at],
                                            op0=ALU.mult, op1=ALU.mult).then_inc(xn_ready, 1)
                if i == 6:
                    return
                if between is not None:
                    between()
                for g, half, t, b in norm_groups(i):
                    ve.wait_ge(x_hi_made, 4 * i + g + 1)
                    at = (slice(None), slice(4 * half, 4 * half + 4), slice(t * P, (t + 1) * P))
                    ve.tensor_tensor(x_lo[at], b[:, :].rearrange("p (c t) -> p c t", c=4), x_hi[at],
                                     ALU.subtract).then_inc(x_lo_made, 1)

            def add_banks(first, done, n):
                for t in range(TT):
                    for half in range(2):
                        wait_sum(ve, done, 2 * t + half, n)
                        at = h[:, t, half * HALF:(half + 1) * HALF]
                        ve.tensor_tensor(at, at, bank[first + 2 * t + half][:, :], ALU.add).then_inc(h_ready, 1)

            def attention(layer, scale, lead, extra):
                first = layer * HEADS

                def maxima(hd):
                    a = first + hd
                    s, st = score[:, a % 2], stat[:, a % 2]
                    ve.wait_ge(scores_ready, a + 1)
                    if hd == 0:
                        ve.wait_ge(bias_loaded[layer], 32)
                    link(ve.scalar_tensor_tensor(out=s, in0=bank[4 + a % 2][:, 0:DIAGS], scalar=scale, in1=bias[:, hd],
                                                 op0=ALU.mult, op1=ALU.add))
                    ve.tensor_reduce(st[:, 0, 0:1], s[:, 0:P], AX, ALU.max)
                    link(ve.tensor_reduce(st[:, 0, 1:2], s[:, P:DIAGS], AX, ALU.max))
                    if layer == 0:
                        ve.tensor_scalar(st[:, 1, :], st[:, 0, :], sink[:, hd:hd + 1], -1.0, ALU.max, ALU.mult)\
                            .then_inc(negmax_ready, 1)
                    else:
                        ve.tensor_scalar(st[:, 1, :], st[:, 0, :], -1.0, None, ALU.mult).then_inc(negmax_ready, 1)

                def output(hd):
                    ve.wait_ge(oT_hi_made, first + hd + 1)
                    dst, src = head_out(layer, hd, m_lo)
                    ve.tensor_tensor(dst, src, head_out(layer, hd, m_hi)[0], ALU.subtract).then_inc(oT_lo_made, 1)

                maxima(0)
                maxima(1)
                lead()
                for hd in range(HEADS):
                    a = first + hd
                    s, st = score[:, a % 2], stat[:, a % 2]
                    ve.wait_ge(exp_made, a + 1)
                    if layer == 0:
                        link(ve.tensor_tensor(st[:, 2], st[:, 2], st[:, 3], ALU.add))
                    link(ve.reciprocal(st[:, 4], st[:, 2]))
                    ve.tensor_scalar(s[:, 0:P], s[:, 0:P], st[:, 4, 0:1], None, ALU.mult)
                    ve.tensor_scalar(s[:, P:DIAGS], s[:, P:DIAGS], st[:, 4, 1:2], None, ALU.mult).then_inc(probs_ready, 1)
                    extra(hd)
                    if hd:
                        output(hd - 1)
                    if hd + 2 < HEADS:
                        maxima(hd + 2)
                output(HEADS - 1)

            ve.memset(zeros_r[:, :].bitcast(F32), 0.0).then_inc(memsets_done, 1)
            ve.memset(cu[:, :, 0:2], 0.0).then_inc(memsets_done, 1)
            for t in range(TT):
                ve.wait_ge(x_loaded[t], 16)

            def split_q(n):
                ve.wait_ge(hi_made, n + 1)
                for dst, src, hi in zip(by_group(w_lo[:, n], True), by_group(raw[:, n], False), by_group(w_hi[:, n], True)):
                    ins = ve.tensor_tensor(dst, src, hi, ALU.subtract)
                ins.then_inc(lo_made, 1)

            norm(0, lambda: split_q(0))
            split_q(1)
            split(KV_T)
            for i in range(3):
                split(SPLIT + i)
            for l in range(2):
                ve.wait_ge(p_hi_made, l + 1)
                ve.tensor_tensor(p_lo[:, l], bank[6 + l][:, :].rearrange("p (c t) -> p c t", c=2), p_hi[:, l],
                                 ALU.subtract).then_inc(p_lo_made, 1)
            ve.wait_ge(r_hi_made, 1)
            ve.tensor_tensor(r_lo[:, :, :], r_raw[:, :, :], r_hi[:, :, :], ALU.subtract).then_inc(r_lo_made, 1)
            ve.wait_ge(aux_loaded, 80)
            ve.wait_ge(taps_made, 1)
            ve.wait_ge(memsets_done, 2)

            def beside(hd):
                if hd < 4:
                    conv_tile(hd + 2)
                elif hd % 2:
                    split(OUT0_T + hd // 2 - 2 + SPLIT)

            def conv_tile(n):
                i, part = n // 3, n % 3
                ve.wait_ge(tile_used, CONV_T + n + 1)
                ps = bank[n % 4][:, :].rearrange("p (j t) -> p j t", j=2)
                if part == 1:
                    ve.wait_ge(c_made, i + 1)
                    link(ve.tensor_tensor(cu[:, 2 * i:2 * i + 2, 2:SEQ + 2], c_sb, ps, ALU.mult))
                    for tap in range(3):
                        for j in range(2):
                            src, w = cu[:, 2 * i + j, tap:tap + SEQ], conv_w[:, 4 * tap + 2 * i + j:4 * tap + 2 * i + j + 1]
                            if tap == 0:
                                ins = ve.tensor_scalar(conv_y[:, j], src, w, None, ALU.mult)
                            else:
                                ins = ve.scalar_tensor_tensor(out=conv_y[:, j], in0=src, scalar=w, in1=conv_y[:, j],
                                                              op0=ALU.mult, op1=ALU.add)
                        link(ins)
                if part == 2:
                    ve.tensor_tensor(conv_a, conv_y, ps, ALU.mult).then_inc(conv_made, 1)
                    ve.wait_ge(conv_hi_made, i + 1)
                    ve.tensor_tensor(m_lo[:, 2 * i:2 * i + 2], conv_a, m_hi[:, 2 * i:2 * i + 2], ALU.subtract)\
                        .then_inc(conv_lo_made, 1)
                split(CONV_T + n + SPLIT)

            conv_tile(0)
            attention(0, SWA_D ** -0.5, lambda: conv_tile(1), beside)
            add_banks(0, 0, OUT0_T + 3)
            norm(1)
            split(OUT0_T + 2 + SPLIT)
            split(OUT0_T + 3 + SPLIT)

            def hidden(n, i):
                ve.wait_ge(tile_used, n + 1)
                ve.wait_ge(silu_made, i + 1)
                if not isinstance(i, int):
                    ve.wait_ge(hid_lo_made, i)
                ve.tensor_tensor(hid, silu, bank[1][:, :], ALU.mult).then_inc(hid_made, 1)

            def hidden_lo(i, parity):
                ve.wait_ge(hid_hi_made, i + 1)
                ve.tensor_tensor(hid_lo[parity], hid.rearrange("p (j t) -> p j t", j=2), hid_hi[parity],
                                 ALU.subtract).then_inc(hid_lo_made, 1)

            split(FFN_T + SPLIT)
            hidden(FFN_T + 1, 0)
            hidden_lo(0, 0)
            split(FFN_T + 1 + SPLIT)
            with ve.Fori(0, (PAIRS - 1) // 2) as r:
                for u in range(2):
                    n = FFN_T + 2 + 3 * u
                    i = 1 + u + 2 * r
                    split(n + SPLIT + 6 * r, n + SPLIT)
                    hidden(n + 1 + 6 * r, i)
                    hidden_lo(i, 1 - u)
                    split(n + 1 + SPLIT + 6 * r, n + 1 + SPLIT)
                    split(n + 2 + SPLIT + 6 * r, n + 2 + SPLIT)
            add_banks(4, 1, PLE0_T - 1)

            def embed(l, proj):
                for t in range(TT):
                    for half in range(2):
                        b = 2 * t + half
                        ve.wait_ge(sig_made, 4 * l + b + 1)
                        ve.tensor_tensor(sig[:, b], sig[:, b], proj(b), ALU.mult).then_inc(gated_made, 1)
                        ve.wait_ge(gated_made, 4 * l + b + 1)
                        at = h[:, t, half * HALF:(half + 1) * HALF]
                        ve.tensor_tensor(at, at, sig[:, b], ALU.add).then_inc(h_ready, 1)

            norm(2)
            for i in range(-1, 3):
                split(PLE0_T + i + SPLIT)
            embed(0, lambda b: bank[b][:, :])
            norm(3)
            split(PLE0_T + 3 + SPLIT)
            split(PLE0_T + 4 + SPLIT)
            def beside1(hd):
                for i in qkv_beside(hd):
                    split(QKV_T + i + SPLIT)
                if hd >= HEADS - 2:
                    split(OUT1_T + hd - HEADS + 2 + SPLIT)

            split(QKV_T + SPLIT)
            split(QKV_T + 1 + SPLIT)
            attention(1, MOBA_D ** -0.5, lambda: split(QKV_T + 2 + SPLIT), beside1)
            add_banks(0, 3, OUT1_T + 3)
            norm(4)
            split(OUT1_T + 2 + SPLIT)
            E = EXPERTS
            R = lambda a, n: route[:, a:a + n]
            logit = R(0, 16).rearrange("p (t e) -> p t e", t=TT)
            top, negtop = R(16, 2), R(24, 2)
            ex = R(32, 16).rearrange("p (t e) -> p t e", t=TT)
            rank = R(48, 16).rearrange("p (t e) -> p t e", t=TT)
            chosen = R(64, 16).rearrange("p (t e) -> p t e", t=TT)
            gate = R(80, 16).rearrange("p (t e) -> p t e", t=TT)
            pos1 = R(96, 16).rearrange("p (t e) -> p t e", t=TT)
            den, rden = R(112, 2), R(114, 2)
            over, orank, eid = R(116, 8), R(124, 8), R(144, 4)
            is_o = R(320, EXTRA * E).rearrange("p (o e) -> p o e", o=EXTRA)
            eid_terms = R(352, EXTRA * E).rearrange("p (o e) -> p o e", o=EXTRA)
            terms = R(384, 4 * EXTRA * E).rearrange("p (q t o e) -> p q t o e", q=2, t=TT, o=EXTRA)
            sums = R(512, 4 * EXTRA).rearrange("p (q t o) -> p q t o", q=2, t=TT)
            tmp = R(160, 64).rearrange("p (e f) -> p e f", e=E)
            tmp2 = R(224, 64).rearrange("p (e f) -> p e f", e=E)
            before = cst[:, C_BEFORE:C_EIDX].rearrange("p (e f) -> p e f", e=E)
            eidx = cst[:, C_EIDX:C_END]
            ve.wait_ge(logits_ready, 1)
            link(ve.tensor_copy(logit, bank[4][:, 0:2 * E].rearrange("p (t e) -> p t e", t=TT)))
            link(ve.tensor_reduce(top, logit, AX, ALU.max))
            ve.tensor_scalar(negtop, top, -1.0, None, ALU.mult).then_inc(route_exp_ready, 1)
            for t in range(TT):
                mine = logit[:, t].unsqueeze(2).broadcast_to((P, E, E))
                other = logit[:, t].unsqueeze(1).broadcast_to((P, E, E))
                ve.tensor_tensor(tmp, other, mine, ALU.is_gt)
                link(ve.tensor_tensor(tmp2, other, mine, ALU.is_equal))
                link(ve.tensor_tensor(tmp2, tmp2, before, ALU.mult))
                link(ve.tensor_tensor(tmp, tmp, tmp2, ALU.add))
                link(ve.tensor_reduce(rank[:, t], tmp, AX, ALU.add))
            ve.tensor_scalar(chosen, rank, TOP_K - 0.5, None, ALU.is_lt).then_inc(chosen_ready, 1)
            ve.wait_ge(chosen_ready, 1)
            ve.wait_ge(route_exp_made, 2)
            link(ve.tensor_tensor(ex, ex, chosen, ALU.mult))
            link(ve.tensor_reduce(den, ex, AX, ALU.add))
            link(ve.reciprocal(rden, den))
            for t in range(TT):
                link(ve.tensor_scalar(gate[:, t], ex[:, t], rden[:, t:t + 1], None, ALU.mult))
            ve.wait_ge(ranks_ready, 1)
            ve.tensor_scalar(over, bank[5][:, 2 * E:3 * E], P + 0.5, None, ALU.is_gt)
            link(ve.scalar_tensor_tensor(out=pos1, in0=bank[5][:, 0:2 * E].rearrange("p (t e) -> p t e", t=TT),
                                         scalar=1.0, in1=chosen, op0=ALU.add, op1=ALU.mult))
            for t in range(TT):
                ve.tensor_scalar(jobs[:, 0:E, 0, t], pos1[:, t], -1.0, None, ALU.add)
                link(ve.tensor_copy(jobs[:, 0:E, 1, t], gate[:, t]))

            def picks(j):
                ve.tensor_copy(job[:, :, :, :], jobs[:, bass.ds(j, 1), :, :]).then_inc(job_read, 1)
                ve.wait_ge(job_read, j + 1)
                for t in range(TT):
                    ve.tensor_scalar(pick_g[:, t], iota, job[:, 0, 0, t:t + 1], job[:, 0, 1, t:t + 1], ALU.is_equal, ALU.mult)
                for t in range(TT):
                    ins = ve.tensor_scalar(pick[:, t], iota, job[:, 0, 0, t:t + 1], None, ALU.is_equal)
                ins.then_inc(pick_made, 1)

            def gathered(j):
                for half in range(2):
                    ve.wait_ge(xg_hi_made, 2 * j + (half + 1))
                    at = x_lo[:, 4 * half:4 * half + 4, 0:P]
                    ve.tensor_tensor(at, bank[4 + half][:, :].rearrange("p (c t) -> p c t", c=4),
                                     x_hi[:, 4 * half:4 * half + 4, 0:P], ALU.subtract).then_inc(xg_lo_made, 1)

            def scattered(j, quarters, last=False):
                for q in quarters:
                    ve.wait_ge(scatter_ready, 4 * j + (q + 1))
                    at = h[:, q // 2, (q % 2) * HALF:(q % 2 + 1) * HALF]
                    ve.tensor_tensor(at, at, bank[2 + q][:, :], ALU.add).then_inc(h_ready if last else scatter_added, 1)

            def expert(j, last=False):
                def lo(k, b=None):
                    n = MOE_T + k + SPLIT
                    split(n + JOB_TILES * j if b is None else n + JOB_TILES * j + 6 * b, n)

                def hidden_of(k, b, looped):
                    n = MOE_T + k + 1 + JOB_TILES * j
                    ve.wait_ge(tile_used, n + 6 * b if looped else n)
                    ve.wait_ge(e_silu_made, BLOCKS * j + b + 1)
                    ve.tensor_tensor(hid, silu, bank[1][:, :], ALU.mult).then_inc(e_hid_made, 1)

                def hidT_of(b):
                    ve.wait_ge(hidT_hi_made, BLOCKS * j + b + 1)
                    ve.tensor_tensor(hidT_lo, bank[2][:, :].rearrange("p (c t) -> p c t", c=4), hidT_hi,
                                     ALU.subtract).then_inc(hidT_lo_made, 1)

                for k in range(3):
                    lo(k)
                hidden_of(3, 0, False)
                scattered(j, range(4))
                if not last:
                    ve.wait_ge(place_made, j + 2)
                    picks(j + 1)
                with ve.Fori(1, BLOCKS) as b:
                    for k in range(-3, 0):
                        lo(k, b)
                    hidT_of(b - 1)
                    lo(0, b)
                    hidden_of(1, b, True)
                    lo(1, b)
                    lo(2, b)
                hidT_of(BLOCKS - 1)
                lo(JOB_TILES - 3)
                if not last:
                    gathered(j + 1)
                lo(JOB_TILES - 2)
                if not last:
                    lo(JOB_TILES - 1)

            picks(0)
            split(OUT1_T + 3 + SPLIT)
            ve.memset(y_sb[:, 0:HALF], 0.0).then_inc(y_made, 1)
            ve.memset(y_sb[:, HALF:D], 0.0).then_inc(y_made, 1)
            ve.memset(place, 0.0).then_inc(place_made, 1)
            gathered(0)
            split(PROJ1_T + SPLIT)
            link(ve.tensor_tensor(tmp, before, over.unsqueeze(1).broadcast_to((P, E, E)), ALU.mult))
            ve.tensor_reduce(orank, tmp, AX, ALU.add)
            link(ve.tensor_reduce(eid[:, 3:4], over, AX, ALU.add))
            for o in range(EXTRA):
                ins = ve.scalar_tensor_tensor(out=is_o[:, o], in0=orank, scalar=float(o), in1=over, op0=ALU.is_equal, op1=ALU.mult)
            link(ins)
            link(ve.tensor_scalar(eid[:, 3:4], eid[:, 3:4], float(EXPERTS - 1), None, ALU.add))
            link(ve.tensor_tensor(eid_terms, is_o, eidx.unsqueeze(1).broadcast_to((P, EXTRA, E)), ALU.mult))
            for q, of in enumerate((pos1, gate)):
                for t in range(TT):
                    ins = ve.tensor_tensor(terms[:, q, t], is_o, of[:, t].unsqueeze(1).broadcast_to((P, EXTRA, E)), ALU.mult)
            link(ins)
            ve.tensor_reduce(eid[:, 0:EXTRA], eid_terms, AX, ALU.add)
            link(ve.tensor_reduce(sums, terms, AX, ALU.add))
            ve.tensor_scalar(jobs[:, E:JOBS, 0].rearrange("p o t -> p t o"), sums[:, 0], -1.0 - P, None, ALU.add)
            ve.tensor_copy(jobs[:, E:JOBS, 1].rearrange("p o t -> p t o"), sums[:, 1])
            link(ve.memset(jobs[:, JOBS], -1.0))
            ve.tensor_copy(job_int[:, :], eid[0:1, :]).then_inc(jobs_ready, 1)
            nj = each_job(ve, expert)
            scattered(nj, range(4), last=True)
            norm(5)
            split(GATE1_T + SPLIT - 1 + JOB_TILES * nj, GATE1_T + SPLIT - 1)
            split(GATE1_T + SPLIT + JOB_TILES * nj, GATE1_T + SPLIT)
            embed(1, lambda b: proj1[:, b])
            norm(6)


_INS = ["x", "p", "rel_bias", "final_norm", "e_norm_mix", "e_w_in", "e_conv_w", "e_sinks", "e_w_out",
        "e_norm_ffn", "e_ffn_gate", "e_ffn_up", "e_ffn_down", "e_norm_ple", "e_ple_gate", "e_ple_proj",
        "o_norm_mix", "o_w_qkv", "o_w_o", "o_norm_ffn", "o_router", "o_exp_gate", "o_exp_up", "o_exp_down",
        "o_norm_ple", "o_ple_gate", "o_ple_proj"]


def kernel(**inputs):
    import concourse.bacc as _bacc
    from concourse.bass_utils import run_bass_kernel_spmd as _run

    nc = _bacc.Bacc("TRN2", target_bir_lowering=False, num_devices=1)
    arrays = {f"in_{name}": np.ascontiguousarray(inputs[name]) for name in _INS}
    consts, onehots = shape_constants()
    arrays["in_consts"], arrays["in_onehots"] = consts, onehots
    args = [nc.dram_tensor(n, a.shape, mybir.dt.from_np(a.dtype), kind="ExternalInput").ap() for n, a in arrays.items()]
    out = nc.dram_tensor("out_0", (1, SEQ, D), F32, kind="ExternalOutput").ap()
    trunk(nc, *args, out)
    r = _run(nc, [arrays], core_ids=[0])
    return r.results[0]["out_0"]
```
